# Optimizing a Trainium2 kernel written in Bass

```python
import math
import jax, jax.numpy as jnp
from jax import lax
import numpy as np

D_MODEL = 1024
BATCH = 1
SEQ = 256
DEPTH = 2

ATTN_HEADS = 8
ATTN_KV_HEADS = 2
ATTN_HEAD_DIM = D_MODEL // ATTN_HEADS
ATTN_WIDTH = ATTN_HEADS * ATTN_HEAD_DIM
ATTN_KV_WIDTH = ATTN_KV_HEADS * ATTN_HEAD_DIM
ATTN_ROT_DIM = ATTN_HEAD_DIM // 4
IDX_HEADS = 8
IDX_DIM = 64
IDX_ROT_DIM = IDX_DIM // 4
INDEX_TOPK = 256
Q_BLOCK = 128
ROPE_THETA = 500000.0
GDN_HEADS = 8
GDN_DK = 128
GDN_DV = 128
GDN_QK_WIDTH = GDN_HEADS * GDN_DK
GDN_WIDTH = GDN_HEADS * GDN_DV
GDN_QKV_WIDTH = 2 * GDN_QK_WIDTH + GDN_WIDTH
CONV_K = 4
CHUNK = 64
N_BRANCH = 2
NORM_EPS = 1e-6

IN_SPLITS = [
    ATTN_WIDTH,
    ATTN_KV_WIDTH,
    ATTN_KV_WIDTH,
    ATTN_WIDTH,
    IDX_HEADS * IDX_DIM,
    IDX_DIM,
    IDX_HEADS,
    GDN_QKV_WIDTH,
    GDN_WIDTH,
    GDN_HEADS,
    GDN_HEADS,
    N_BRANCH * D_MODEL,
]
IN_COLS = sum(IN_SPLITS)
IN_SPLIT_IDX = [sum(IN_SPLITS[:i + 1]) for i in range(len(IN_SPLITS) - 1)]


def rms_norm(x, gain):
    xf = x.astype(jnp.float32)
    y = xf * lax.rsqrt(jnp.mean(xf * xf, axis=-1, keepdims=True) + NORM_EPS)
    return (y * gain.astype(jnp.float32)).astype(x.dtype)

def l2_normalize(x):
    xf = x.astype(jnp.float32)
    return xf * lax.rsqrt(jnp.sum(xf * xf, axis=-1, keepdims=True) + NORM_EPS)

def rope_tables(positions, rot_dim):
    inv_freq = ROPE_THETA ** (-jnp.arange(0, rot_dim, 2, dtype=jnp.float32) / rot_dim)
    ang = positions.astype(jnp.float32)[..., None] * inv_freq
    return jnp.cos(ang)[:, :, None, :], jnp.sin(ang)[:, :, None, :]

def apply_partial_rope(x, cos, sin):
    half = cos.shape[-1]
    rot = 2 * half
    x1, x2, xp = x[..., :half], x[..., half:rot], x[..., rot:]
    c, s = cos.astype(x.dtype), sin.astype(x.dtype)
    return jnp.concatenate([x1 * c - x2 * s, x2 * c + x1 * s, xp], axis=-1)

def dsa_attention(q, k, v, q_idx, k_idx, w_idx):
    B, S = q.shape[0], q.shape[1]
    topk = min(INDEX_TOPK, S // 4)
    nb = S // Q_BLOCK
    group = ATTN_HEADS // ATTN_KV_HEADS
    scale = ATTN_HEAD_DIM ** -0.5
    key_pos = jnp.arange(S, dtype=jnp.int32)

    def blocks(t):
        return t.reshape(B, nb, Q_BLOCK, *t.shape[2:]).swapaxes(0, 1)

    def one_block(args):
        qb, qib, wb, tb = args
        raw = jnp.einsum('bqhd,bsd->bqhs', qib, k_idx)
        iscore = jnp.einsum('bqhs,bqh->bqs', jax.nn.relu(raw), wb).astype(jnp.float32)
        causal = key_pos[None, :] <= tb[:, None]
        iscore = jnp.where(causal[None], iscore, -jnp.inf)
        _, sel = lax.top_k(iscore, topk)
        valid = sel <= tb[None, :, None]
        k_sel = jax.vmap(lambda kb, ib: kb[ib])(k, sel)
        v_sel = jax.vmap(lambda vb, ib: vb[ib])(v, sel)
        qg = qb.reshape(B, Q_BLOCK, ATTN_KV_HEADS, group, ATTN_HEAD_DIM)
        logits = jnp.einsum('bqhgd,bqkhd->bqhgk', qg, k_sel).astype(jnp.float32) * scale
        logits = jnp.where(valid[:, :, None, None, :], logits, -jnp.inf)
        p = jax.nn.softmax(logits, axis=-1).astype(v.dtype)
        o = jnp.einsum('bqhgk,bqkhd->bqhgd', p, v_sel)
        return o.reshape(B, Q_BLOCK, ATTN_WIDTH)

    out = lax.map(one_block, (blocks(q), blocks(q_idx), blocks(w_idx),
                              key_pos.reshape(nb, Q_BLOCK)))
    return out.swapaxes(0, 1).reshape(B, S, ATTN_WIDTH)

def causal_depthwise_conv(x, w):
    C = x.shape[-1]
    return lax.conv_general_dilated(
        x, w[:, None, :].astype(x.dtype), window_strides=(1,),
        padding=[(CONV_K - 1, 0)], dimension_numbers=('NWC', 'WIO', 'NWC'),
        feature_group_count=C)

def chunked_gated_delta_rule(q, k, v, beta, g):
    B, S, H, dk = q.shape
    dv = v.shape[-1]
    nc = S // CHUNK

    def c4(t):
        return t.reshape(B, nc, CHUNK, H, t.shape[-1]).transpose(0, 3, 1, 2, 4)

    def c3(t):
        return t.reshape(B, nc, CHUNK, H).transpose(0, 3, 1, 2)

    q, k, v = c4(q) * (dk ** -0.5), c4(k), c4(v)
    beta, gc = c3(beta), jnp.cumsum(c3(g), axis=-1)
    incl = jnp.tril(jnp.ones((CHUNK, CHUNK), dtype=bool))
    strict = jnp.tril(jnp.ones((CHUNK, CHUNK), dtype=bool), k=-1)
    decay = jnp.exp(jnp.where(incl, gc[..., :, None] - gc[..., None, :], -jnp.inf))
    kb = k * beta[..., None]
    lower = jnp.where(strict, jnp.einsum('bhnid,bhnjd->bhnij', kb, k) * decay, 0.0)
    tmat = jnp.eye(CHUNK, dtype=jnp.float32) + lower
    u = lax.linalg.triangular_solve(tmat, v * beta[..., None], left_side=True,
                                    lower=True, unit_diagonal=True)
    w = lax.linalg.triangular_solve(tmat, kb * jnp.exp(gc)[..., None], left_side=True,
                                    lower=True, unit_diagonal=True)
    qk = jnp.einsum('bhnid,bhnjd->bhnij', q, k) * decay
    q_dec = q * jnp.exp(gc)[..., None]
    k_dec = k * jnp.exp(gc[..., -1:] - gc)[..., None]
    g_tot = jnp.exp(gc[..., -1])
    xs = (jnp.moveaxis(qk, 2, 0), jnp.moveaxis(q_dec, 2, 0), jnp.moveaxis(k_dec, 2, 0),
          jnp.moveaxis(u, 2, 0), jnp.moveaxis(w, 2, 0), jnp.moveaxis(g_tot, 2, 0))

    def step(state, xc):
        qk_c, qd_c, kd_c, u_c, w_c, gt_c = xc
        v_new = u_c - jnp.einsum('bhcd,bhde->bhce', w_c, state)
        o_c = (jnp.einsum('bhcd,bhde->bhce', qd_c, state)
               + jnp.einsum('bhij,bhje->bhie', qk_c, v_new))
        state = state * gt_c[..., None, None] + jnp.einsum('bhcd,bhce->bhde', kd_c, v_new)
        return state, o_c

    state0 = jnp.zeros((B, H, dk, dv), dtype=jnp.float32)
    _, o = lax.scan(step, state0, xs)
    return o.transpose(1, 0, 3, 2, 4).reshape(B, S, H, dv)

def first_inputs(seed: int = 0) -> dict:
    key = jax.random.key(seed)
    ks = jax.random.split(key, 12)
    x = jax.random.normal(ks[0], (BATCH, SEQ, D_MODEL), jnp.float32)
    positions = jnp.broadcast_to(jnp.arange(SEQ, dtype=jnp.int32), (BATCH, SEQ))
    norm_gain = 1.0 + 0.02 * jax.random.normal(ks[1], (DEPTH, D_MODEL), jnp.float32)
    w_in = jax.random.normal(ks[2], (DEPTH, D_MODEL, IN_COLS), jnp.float32) * D_MODEL ** -0.5
    conv_w = jax.random.normal(ks[3], (DEPTH, CONV_K, GDN_QKV_WIDTH), jnp.float32) * CONV_K ** -0.5
    a_log = jnp.log(jax.random.uniform(ks[4], (DEPTH, GDN_HEADS), jnp.float32, 1.0, 16.0))
    dt = jnp.exp(jax.random.uniform(ks[5], (DEPTH, GDN_HEADS), jnp.float32,
                                    math.log(1e-3), math.log(1e-1)))
    dt_bias = dt + jnp.log(-jnp.expm1(-dt))
    gdn_norm_gain = 1.0 + 0.02 * jax.random.normal(ks[6], (DEPTH, GDN_DV), jnp.float32)
    idx_k_gain = 1.0 + 0.02 * jax.random.normal(ks[7], (DEPTH, IDX_DIM), jnp.float32)
    w_out = jax.random.normal(ks[8], (DEPTH, D_MODEL, D_MODEL), jnp.float32) * D_MODEL ** -0.5
    final_gain = 1.0 + 0.02 * jax.random.normal(ks[9], (D_MODEL,), jnp.float32)
    return {"x": x, "positions": positions, "norm_gain": norm_gain, "w_in": w_in,
            "conv_w": conv_w, "a_log": a_log, "dt_bias": dt_bias,
            "gdn_norm_gain": gdn_norm_gain, "idx_k_gain": idx_k_gain,
            "w_out": w_out, "final_gain": final_gain}

def first_block(x, positions, norm_gain, w_in, conv_w, a_log, dt_bias, gdn_norm_gain,
              idx_k_gain, w_out, final_gain):
    B, S = x.shape[0], x.shape[1]
    cos_a, sin_a = rope_tables(positions, ATTN_ROT_DIM)
    cos_i, sin_i = rope_tables(positions, IDX_ROT_DIM)
    idx_scale = IDX_HEADS ** -0.5 * IDX_DIM ** -0.5
    for layer in range(DEPTH):
        h = rms_norm(x, norm_gain[layer])
        proj = h @ w_in[layer]
        (q_a, k_a, v_a, z_a, q_i, k_i, w_i, qkv_b, z_b, beta_l, a_l, gate_l) = jnp.split(
            proj, IN_SPLIT_IDX, axis=-1)

        q_a = apply_partial_rope(q_a.reshape(B, S, ATTN_HEADS, ATTN_HEAD_DIM), cos_a, sin_a)
        k_a = apply_partial_rope(k_a.reshape(B, S, ATTN_KV_HEADS, ATTN_HEAD_DIM), cos_a, sin_a)
        v_a = v_a.reshape(B, S, ATTN_KV_HEADS, ATTN_HEAD_DIM)
        q_i = apply_partial_rope(q_i.reshape(B, S, IDX_HEADS, IDX_DIM), cos_i, sin_i)
        k_i = apply_partial_rope(rms_norm(k_i, idx_k_gain[layer])[:, :, None, :],
                                 cos_i, sin_i)[:, :, 0, :]
        w_i = w_i * idx_scale
        y_a = dsa_attention(q_a, k_a, v_a, q_i, k_i, w_i) * jax.nn.silu(z_a)

        qkv_b = jax.nn.silu(causal_depthwise_conv(qkv_b, conv_w[layer]))
        q_b, k_b, v_b = jnp.split(qkv_b, [GDN_QK_WIDTH, 2 * GDN_QK_WIDTH], axis=-1)
        q_b = l2_normalize(q_b.reshape(B, S, GDN_HEADS, GDN_DK))
        k_b = l2_normalize(k_b.reshape(B, S, GDN_HEADS, GDN_DK))
        v_b = v_b.reshape(B, S, GDN_HEADS, GDN_DV).astype(jnp.float32)
        beta = jax.nn.sigmoid(beta_l.astype(jnp.float32))
        g = -jnp.exp(a_log[layer].astype(jnp.float32)) * jax.nn.softplus(
            a_l.astype(jnp.float32) + dt_bias[layer].astype(jnp.float32))
        o_b = chunked_gated_delta_rule(q_b, k_b, v_b, beta, g).astype(x.dtype)
        y_b = (rms_norm(o_b, gdn_norm_gain[layer])
               * jax.nn.silu(z_b.reshape(B, S, GDN_HEADS, GDN_DV))).reshape(B, S, GDN_WIDTH)

        gates = jax.nn.sigmoid(gate_l).reshape(B, S, N_BRANCH, D_MODEL)
        mixed = gates[:, :, 0, :] * y_a + gates[:, :, 1, :] * y_b
        x = x + mixed @ w_out[layer]
    return rms_norm(x, final_gain)


N_MIXERS = 4
HEADS_PER_GROUP = 4
GROUP_WIDTH = D_MODEL // N_MIXERS
HD = GROUP_WIDTH // HEADS_PER_GROUP
MIX_WIDTH = N_MIXERS * GROUP_WIDTH

NSA_HEADS = HEADS_PER_GROUP
NSA_CMP_LEN = 32
NSA_CMP_STRIDE = 16
NSA_CMP_HIDDEN = 4 * HD
NSA_SEL_LEN = 64
NSA_TOPK = 16
NSA_WINDOW = 512

DIFF_HEADS = HEADS_PER_GROUP
DIFF_QK_DIM = HD // 2
DIFF_V_DIM = HD

GLA_HEADS = HEADS_PER_GROUP
GLA_DK = HD // 2
GLA_DV = HD
GLA_GATE_RANK = 16
GLA_TAU = 16.0

HG_HEADS = HEADS_PER_GROUP
HG_DK = HD
HG_DV = HD


D_FF = 7 * D_MODEL // 2
N_EXPERTS = 8
TOP_K = 2
D_FF_EXPERT = 7 * D_MODEL // 2
PLE_DIM = 256
EPS = 1e-6
NEG = -1e30
BIG = 1e30

IN_SPLITS_2 = (
    NSA_HEADS * HD, HD, HD, HD, HD, HD, HD, NSA_HEADS * 3,
    DIFF_HEADS * 2 * DIFF_QK_DIM, DIFF_HEADS * 2 * DIFF_QK_DIM, DIFF_HEADS * DIFF_V_DIM,
    GLA_HEADS * GLA_DK, GLA_HEADS * GLA_DK, GLA_HEADS * GLA_DV, GLA_GATE_RANK, GLA_HEADS * GLA_DV,
    HG_HEADS * HG_DK, HG_HEADS * HG_DK, HG_HEADS * HG_DV, HG_HEADS * HG_DV,
)
IN_COLS_2 = sum(IN_SPLITS_2)


def rms_norm_2(x, gain):
    xf = x.astype(jnp.float32)
    y = xf * lax.rsqrt(jnp.mean(xf * xf, axis=-1, keepdims=True) + EPS)
    return (y * gain.astype(jnp.float32)).astype(x.dtype)

def split_cols(u, sizes):
    offsets = np.cumsum(sizes)[:-1].tolist()
    return jnp.split(u, offsets, axis=-1)

def chunked_gated_linear_attention(q, k, v, log_g):
    B, S, H, DK = q.shape
    DV = v.shape[-1]
    n_chunks = S // CHUNK

    def to_chunks(t):
        return t.astype(jnp.float32).reshape(B, n_chunks, CHUNK, H, -1).transpose(1, 0, 3, 2, 4)

    qc, kc, vc = to_chunks(q), to_chunks(k), to_chunks(v)
    bc = jnp.cumsum(to_chunks(log_g), axis=3)
    causal = np.tril(np.ones((CHUNK, CHUNK), dtype=bool))[None, None, :, :, None]

    def step(state, inp):
        q_, k_, v_, b_ = inp
        o_inter = jnp.einsum('bhik,bhkv->bhiv', q_ * jnp.exp(b_), state)
        rel = jnp.where(causal, b_[:, :, :, None, :] - b_[:, :, None, :, :], NEG)
        attn = jnp.einsum('bhik,bhjk,bhijk->bhij', q_, k_, jnp.exp(rel))
        o_intra = jnp.einsum('bhij,bhjv->bhiv', attn, v_)
        b_last = b_[:, :, -1:, :]
        new_state = (jnp.exp(b_last[:, :, 0, :, None]) * state
                     + jnp.einsum('bhjk,bhjv->bhkv', k_ * jnp.exp(b_last - b_), v_))
        return new_state, o_inter + o_intra

    state0 = jnp.zeros((B, H, DK, DV), jnp.float32)
    _, o = lax.scan(step, state0, (qc, kc, vc, bc))
    return o.transpose(1, 0, 3, 2, 4).reshape(B, S, H, DV).astype(v.dtype)

def nsa_attention(q, k_cmp, v_cmp, k_slc, v_slc, k_win, v_win, gate_logits,
                  cmp_pos, cmp_w1, cmp_w2, qk_gain):
    B, S, H, _ = q.shape
    scale = HD ** -0.5
    q = rms_norm_2(q, qk_gain[0])
    t_pos = np.arange(S)

    n_cmp = (S - NSA_CMP_LEN) // NSA_CMP_STRIDE + 1
    cmp_idx = np.arange(n_cmp)[:, None] * NSA_CMP_STRIDE + np.arange(NSA_CMP_LEN)[None, :]

    def compress(t, j):
        blocks = t[:, cmp_idx] + cmp_pos[j]
        hidden = jax.nn.silu(blocks.reshape(B, n_cmp, NSA_CMP_LEN * HD) @ cmp_w1[j])
        return hidden @ cmp_w2[j]

    kc = rms_norm_2(compress(k_cmp, 0), qk_gain[1])
    vc = compress(v_cmp, 1)
    cmp_ok = cmp_idx[:, -1][None, :] <= t_pos[:, None]
    s_c = jnp.einsum('bthd,bnd->bhtn', q, kc).astype(jnp.float32) * scale
    p_c = jax.nn.softmax(jnp.where(cmp_ok, s_c, NEG), axis=-1) * cmp_ok
    o_c = jnp.einsum('bhtn,bnd->bthd', p_c.astype(vc.dtype), vc)

    n_sel = S // NSA_SEL_LEN
    k_sel = min(NSA_TOPK, n_sel)
    sel_start = np.arange(n_sel) * NSA_SEL_LEN
    cmp_start = cmp_idx[:, 0]
    overlap = ((cmp_start[:, None] <= sel_start[None, :] + NSA_SEL_LEN - 1)
               & (cmp_start[:, None] + NSA_CMP_LEN - 1 >= sel_start[None, :])).astype(np.float32)
    importance = jnp.einsum('bhtn,nm->btm', p_c, overlap)
    blk = np.arange(n_sel)[None, :]
    cur = (t_pos // NSA_SEL_LEN)[:, None]
    forced = (blk == 0) | (blk == cur) | (blk == cur - 1)
    importance = jnp.where(forced, BIG,
                           jnp.where(sel_start[None, :] <= t_pos[:, None], importance, NEG))
    _, sel = lax.top_k(lax.stop_gradient(importance), k_sel)

    kb = rms_norm_2(k_slc, qk_gain[2]).reshape(B, n_sel, NSA_SEL_LEN, HD)
    vb = v_slc.reshape(B, n_sel, NSA_SEL_LEN, HD)
    kw_pad = jnp.pad(rms_norm_2(k_win, qk_gain[3]), ((0, 0), (NSA_WINDOW, 0), (0, 0)))
    vw_pad = jnp.pad(v_win, ((0, 0), (NSA_WINDOW, 0), (0, 0)))
    band = NSA_WINDOW + Q_BLOCK
    gather_blocks = jax.vmap(lambda t, i: t[i])

    def block_body(args):
        qb, selb, t0 = args
        tq = t0 + jnp.arange(Q_BLOCK)
        kg = gather_blocks(kb, selb)
        vg = gather_blocks(vb, selb)
        s = jnp.einsum('bqhd,bqnld->bhqnl', qb, kg).astype(jnp.float32) * scale
        kpos = selb[..., None] * NSA_SEL_LEN + jnp.arange(NSA_SEL_LEN)
        s = jnp.where((kpos <= tq[None, :, None, None])[:, None], s, NEG)
        p = jax.nn.softmax(s.reshape(B, H, Q_BLOCK, k_sel * NSA_SEL_LEN), axis=-1).reshape(s.shape)
        o_s = jnp.einsum('bhqnl,bqnld->bqhd', p.astype(vg.dtype), vg)
        kwb = lax.dynamic_slice_in_dim(kw_pad, t0, band, axis=1)
        vwb = lax.dynamic_slice_in_dim(vw_pad, t0, band, axis=1)
        s = jnp.einsum('bqhd,bkd->bhqk', qb, kwb).astype(jnp.float32) * scale
        kp = t0 - NSA_WINDOW + jnp.arange(band)
        m = ((kp[None, :] <= tq[:, None]) & (kp[None, :] > tq[:, None] - NSA_WINDOW)
             & (kp[None, :] >= 0))
        p = jax.nn.softmax(jnp.where(m, s, NEG), axis=-1)
        o_w = jnp.einsum('bhqk,bkd->bqhd', p.astype(vwb.dtype), vwb)
        return o_s, o_w

    nq = S // Q_BLOCK
    qs = q.reshape(B, nq, Q_BLOCK, H, HD).transpose(1, 0, 2, 3, 4)
    sels = sel.reshape(B, nq, Q_BLOCK, k_sel).transpose(1, 0, 2, 3)
    t0s = jnp.arange(nq, dtype=jnp.int32) * Q_BLOCK
    o_s, o_w = lax.map(block_body, (qs, sels, t0s))
    o_s = o_s.transpose(1, 0, 2, 3, 4).reshape(B, S, H, HD)
    o_w = o_w.transpose(1, 0, 2, 3, 4).reshape(B, S, H, HD)

    g = jax.nn.sigmoid(gate_logits.astype(jnp.float32)).reshape(B, S, H, 3).astype(q.dtype)
    o = g[..., 0:1] * o_c + g[..., 1:2] * o_s + g[..., 2:3] * o_w
    return o.reshape(B, S, H * HD)

def diff_attention(q, k, v, qk_gain, lam, sub_gain, layer_idx):
    B, S, H = q.shape[:3]
    q = rms_norm_2(q, qk_gain[0])
    k = rms_norm_2(k, qk_gain[1])
    lam_init = 0.8 - 0.6 * math.exp(-0.3 * layer_idx)
    lam32 = lam.astype(jnp.float32)
    lam_full = (jnp.exp(jnp.sum(lam32[0] * lam32[1])) - jnp.exp(jnp.sum(lam32[2] * lam32[3]))
                + lam_init)
    scale = DIFF_QK_DIM ** -0.5
    outs = []
    for blk in range(S // Q_BLOCK):
        t0, t1 = blk * Q_BLOCK, (blk + 1) * Q_BLOCK
        s = jnp.einsum('bqhcd,bkhcd->bhcqk', q[:, t0:t1], k[:, :t1]).astype(jnp.float32) * scale
        mask = np.arange(t1)[None, :] <= np.arange(t0, t1)[:, None]
        p = jax.nn.softmax(jnp.where(mask, s, NEG), axis=-1)
        w = p[:, :, 0] - lam_full * p[:, :, 1]
        outs.append(jnp.einsum('bhqk,bkhd->bqhd', w.astype(v.dtype), v[:, :t1]))
    o = jnp.concatenate(outs, axis=1)
    o = rms_norm_2(o, sub_gain) * (1.0 - lam_init)
    return o.reshape(B, S, H * DIFF_V_DIM)

def gla_mixer(q, k, v, g_lr, og, w_gate2, b_gate, norm_gain):
    B, S = q.shape[:2]
    log_a = jax.nn.log_sigmoid((g_lr @ w_gate2 + b_gate).astype(jnp.float32)) / GLA_TAU
    shp = (B, S, GLA_HEADS, GLA_DK)
    o = chunked_gated_linear_attention(q.reshape(shp) * (GLA_DK ** -0.5), k.reshape(shp),
                                       v.reshape(B, S, GLA_HEADS, GLA_DV), log_a.reshape(shp))
    o = rms_norm_2(o, norm_gain) * jax.nn.silu(og.reshape(B, S, GLA_HEADS, GLA_DV))
    return o.reshape(B, S, GLA_HEADS * GLA_DV)

def hgrn2_mixer(q, f_pre, i_in, og, lb, norm_gain):
    B, S = q.shape[:2]
    z = f_pre.astype(jnp.float32)
    lb = lb.astype(jnp.float32)
    f = lb + (1.0 - lb) * jax.nn.sigmoid(z)
    log_f = jnp.log(f)
    one_minus_f = (1.0 - lb) * jax.nn.sigmoid(-z)
    shp = (B, S, HG_HEADS, HG_DK)
    o = chunked_gated_linear_attention(q.reshape(shp), one_minus_f.reshape(shp).astype(q.dtype),
                                       i_in.reshape(B, S, HG_HEADS, HG_DV), log_f.reshape(shp))
    o = rms_norm_2(o, norm_gain) * jax.nn.silu(og.reshape(B, S, HG_HEADS, HG_DV))
    return o.reshape(B, S, HG_HEADS * HG_DV)

def swiglu(x, w_gate, w_up, w_down):
    return (jax.nn.silu(x @ w_gate) * (x @ w_up)) @ w_down

def moe_swiglu(x, router, w_gate, w_up, w_down):
    logits = (x @ router).astype(jnp.float32)
    top_val, top_idx = lax.top_k(logits, TOP_K)
    top_w = jax.nn.softmax(top_val, axis=-1)
    combine = jnp.sum(jax.nn.one_hot(top_idx, N_EXPERTS, dtype=jnp.float32) * top_w[..., None], axis=-2)
    out = jnp.zeros_like(x)
    for e in range(N_EXPERTS):
        out = out + combine[..., e:e + 1].astype(x.dtype) * swiglu(x, w_gate[e], w_up[e], w_down[e])
    return out

def second_inputs(seed: int = 0) -> dict:
    key = jax.random.key(seed)
    keys = iter(jax.random.split(key, 32))

    def nrm(shape, scale):
        return scale * jax.random.normal(next(keys), shape, jnp.float32)

    def gain(shape):
        return 1.0 + 0.02 * jax.random.normal(next(keys), shape, jnp.float32)

    n_dense = (DEPTH + 1) // 2
    n_moe = DEPTH // 2
    return {
        'x': nrm((BATCH, SEQ, D_MODEL), 1.0),
        'p': nrm((DEPTH, BATCH, SEQ, PLE_DIM), 1.0),
        'norm_attn': gain((DEPTH, D_MODEL)),
        'w_in': nrm((DEPTH, D_MODEL, IN_COLS_2), D_MODEL ** -0.5),
        'w_out': nrm((DEPTH, MIX_WIDTH, D_MODEL), MIX_WIDTH ** -0.5),
        'nsa_cmp_pos': nrm((DEPTH, 2, NSA_CMP_LEN, HD), 0.1),
        'nsa_cmp_w1': nrm((DEPTH, 2, NSA_CMP_LEN * HD, NSA_CMP_HIDDEN), (NSA_CMP_LEN * HD) ** -0.5),
        'nsa_cmp_w2': nrm((DEPTH, 2, NSA_CMP_HIDDEN, HD), NSA_CMP_HIDDEN ** -0.5),
        'nsa_qk_gain': gain((DEPTH, 4, HD)),
        'diff_qk_gain': gain((DEPTH, 2, DIFF_QK_DIM)),
        'diff_lambda': nrm((DEPTH, 4, DIFF_QK_DIM), 0.1),
        'diff_norm': gain((DEPTH, DIFF_V_DIM)),
        'gla_w_gate2': nrm((DEPTH, GLA_GATE_RANK, GLA_HEADS * GLA_DK), GLA_GATE_RANK ** -0.5),
        'gla_b_gate': nrm((DEPTH, GLA_HEADS * GLA_DK), 0.1),
        'gla_norm': gain((DEPTH, GLA_DV)),
        'hgrn_lb_logits': nrm((DEPTH, HG_HEADS * HG_DK), 1.0),
        'hgrn_norm': gain((DEPTH, HG_DV)),
        'norm_ffn': gain((DEPTH, D_MODEL)),
        'ffn_w_gate': nrm((n_dense, D_MODEL, D_FF), D_MODEL ** -0.5),
        'ffn_w_up': nrm((n_dense, D_MODEL, D_FF), D_MODEL ** -0.5),
        'ffn_w_down': nrm((n_dense, D_FF, D_MODEL), D_FF ** -0.5),
        'moe_router': nrm((n_moe, D_MODEL, N_EXPERTS), D_MODEL ** -0.5),
        'moe_w_gate': nrm((n_moe, N_EXPERTS, D_MODEL, D_FF_EXPERT), D_MODEL ** -0.5),
        'moe_w_up': nrm((n_moe, N_EXPERTS, D_MODEL, D_FF_EXPERT), D_MODEL ** -0.5),
        'moe_w_down': nrm((n_moe, N_EXPERTS, D_FF_EXPERT, D_MODEL), D_FF_EXPERT ** -0.5),
        'ple_norm': gain((DEPTH, D_MODEL)),
        'ple_w_gate': nrm((DEPTH, D_MODEL, D_MODEL), D_MODEL ** -0.5),
        'ple_w_proj': nrm((DEPTH, PLE_DIM, D_MODEL), PLE_DIM ** -0.5),
    }

def second_block(x, p, norm_attn, w_in, w_out, nsa_cmp_pos, nsa_cmp_w1, nsa_cmp_w2, nsa_qk_gain,
              diff_qk_gain, diff_lambda, diff_norm, gla_w_gate2, gla_b_gate, gla_norm,
              hgrn_lb_logits, hgrn_norm, norm_ffn, ffn_w_gate, ffn_w_up, ffn_w_down,
              moe_router, moe_w_gate, moe_w_up, moe_w_down, ple_norm, ple_w_gate, ple_w_proj):
    B, S, _ = x.shape
    lb_p = jax.nn.softmax(hgrn_lb_logits.astype(jnp.float32), axis=0)
    lower_bounds = jnp.cumsum(lb_p, axis=0) - lb_p[0]
    h = x
    for i in range(DEPTH):
        a = rms_norm_2(h, norm_attn[i])
        u = a @ w_in[i]
        (nsa_q, k_cmp, v_cmp, k_slc, v_slc, k_win, v_win, nsa_g,
         d_q, d_k, d_v,
         g_q, g_k, g_v, g_lr, g_og,
         r_q, r_f, r_i, r_og) = split_cols(u, IN_SPLITS_2)
        o_a = nsa_attention(nsa_q.reshape(B, S, NSA_HEADS, HD), k_cmp, v_cmp, k_slc, v_slc,
                            k_win, v_win, nsa_g, nsa_cmp_pos[i], nsa_cmp_w1[i], nsa_cmp_w2[i],
                            nsa_qk_gain[i])
        o_b = diff_attention(d_q.reshape(B, S, DIFF_HEADS, 2, DIFF_QK_DIM),
                             d_k.reshape(B, S, DIFF_HEADS, 2, DIFF_QK_DIM),
                             d_v.reshape(B, S, DIFF_HEADS, DIFF_V_DIM),
                             diff_qk_gain[i], diff_lambda[i], diff_norm[i], i)
        o_c = gla_mixer(g_q, g_k, g_v, g_lr, g_og, gla_w_gate2[i], gla_b_gate[i], gla_norm[i])
        o_d = hgrn2_mixer(r_q, r_f, r_i, r_og, lower_bounds[i], hgrn_norm[i])
        mix = jnp.concatenate([o_a, o_b, o_c, o_d], axis=-1)
        h = h + mix @ w_out[i]
        c = rms_norm_2(h, norm_ffn[i])
        if i % 2 == 0:
            h = h + swiglu(c, ffn_w_gate[i // 2], ffn_w_up[i // 2], ffn_w_down[i // 2])
        else:
            h = h + moe_swiglu(c, moe_router[i // 2], moe_w_gate[i // 2], moe_w_up[i // 2],
                               moe_w_down[i // 2])
        gate = jax.nn.sigmoid(rms_norm_2(h, ple_norm[i]) @ ple_w_gate[i])
        h = h + (p[i] @ ple_w_proj[i]) * gate
    return h


def setup_inputs(seed=0):
    out = dict(first_inputs(seed))
    for name, value in second_inputs(seed + 1).items():
        if name != "x":
            out[name + "_2"] = value
    return out


def reference(
    x, positions, norm_gain, w_in, conv_w, a_log, dt_bias, gdn_norm_gain, idx_k_gain, w_out,
    final_gain, p_2, norm_attn_2, w_in_2, w_out_2, nsa_cmp_pos_2, nsa_cmp_w1_2, nsa_cmp_w2_2,
    nsa_qk_gain_2, diff_qk_gain_2, diff_lambda_2, diff_norm_2, gla_w_gate2_2, gla_b_gate_2,
    gla_norm_2, hgrn_lb_logits_2, hgrn_norm_2, norm_ffn_2, ffn_w_gate_2, ffn_w_up_2,
    ffn_w_down_2, moe_router_2, moe_w_gate_2, moe_w_up_2, moe_w_down_2, ple_norm_2,
    ple_w_gate_2, ple_w_proj_2,
):
    x = first_block(
        x, positions, norm_gain, w_in, conv_w, a_log, dt_bias, gdn_norm_gain, idx_k_gain, w_out,
        final_gain,
    )
    return second_block(
        x, p_2, norm_attn_2, w_in_2, w_out_2, nsa_cmp_pos_2, nsa_cmp_w1_2, nsa_cmp_w2_2,
        nsa_qk_gain_2, diff_qk_gain_2, diff_lambda_2, diff_norm_2, gla_w_gate2_2, gla_b_gate_2,
        gla_norm_2, hgrn_lb_logits_2, hgrn_norm_2, norm_ffn_2, ffn_w_gate_2, ffn_w_up_2,
        ffn_w_down_2, moe_router_2, moe_w_gate_2, moe_w_up_2, moe_w_down_2, ple_norm_2,
        ple_w_gate_2, ple_w_proj_2,
    )


_drawn_inputs = setup_inputs


def setup_inputs(seed=0):
    import zlib

    import numpy as np

    out = dict(_drawn_inputs(seed))
    spreads = {}
    factors = {'gdn_norm_gain': 2.714,
     'nsa_qk_gain_2': 4.113,
     'diff_qk_gain_2': 3.167,
     'gla_norm_2': 3.37,
     'hgrn_norm_2': 3.337,
     'ple_norm_2': 38.636,
     'diff_lambda_2': 4.219,
     'diff_norm_2': 5.619,
     'norm_ffn_2': 3.002}
    for name, (base, spread) in spreads.items():
        noise = np.random.default_rng([zlib.crc32(name.encode()), seed]).standard_normal(out[name].shape)
        drawn = base * np.exp(spread * noise) if base else spread * noise
        out[name] = __import__('jax').numpy.asarray(drawn.astype(out[name].dtype))
    for name, factor in factors.items():
        out[name] = (out[name] * factor).astype(out[name].dtype)
    return out
```

```python
import math
from contextlib import ExitStack

import numpy as np

import concourse.bass as bass
from concourse import mybir

P = 128
S = 256
T = S // P
D = 1024
KD = D // P
DEPTH = 2
F32 = mybir.dt.float32
I32 = mybir.dt.int32
ALU = mybir.AluOpType
ACT = mybir.ActivationFunctionType
AX = mybir.AxisListType
EPS = 1e-6
NEG = -1e30
NONCAUSAL = -3.0e38
TAKEN = -3.3e38

HQ, HKV, DH = 8, 2, 128
ROT, IDX_H, IDX_D, IDX_ROT, TOPK = 32, 8, 64, 16, 64
GH, DK, CONV = 8, 128, 4
Q0, K0, V0, Z0, QI0, KI0, WI0, QKV0, ZB0, BETA0, GATE0, COLS1 = (
    0, 1024, 1280, 1536, 2560, 3072, 3136, 3144, 6216, 7240, 7256, 9304)
CT = 3 * GH
W_P1B = GATE0 - ZB0
HD = 64
(NQ0, KC0, KS0, VS0, KW0, VW0, NG0, DQ0, DK0, DV0, GQ0, GK0, GV0, GLR0, GOG0, RQ0, RF0, RI0, ROG0, COLS2) = (
    0, 256, 384, 448, 512, 576, 640, 652, 908, 1164, 1420, 1548, 1676, 1932, 1948, 2204, 2460, 2716, 2972, 3228)
NCMP, CMP_L, CMP_S = 15, 32, 16
FF = 3584
NE = 8
PLE = 256
LEVELS = 7

RING = 7
HALF = 2048
PER_EXPERT = 2 * 7 * 2 + 14


def blocks_kernel(nc, A, out):
    ctx = ExitStack()
    with ctx:
        sems = {}

        def sem(name):
            if name not in sems:
                sems[name] = ctx.enter_context(nc.semaphore(name))
            return sems[name]

        CHAINS = {
            "cmp_by_tensor": ("cmp_kv", "cmp_kT", "cmp_scores", "cmp_pT", "cmp_out"),
            "cmp_by_scalar": ("cmp_silu", "cmp_ksq", "cmp_kroot", "cmp_kT_out", "cmp_scaled", "cmp_exp", "cmp_pT_out"),
            "cmp_by_vector": ("cmp_x", "cmp_hid", "cmp_kms", "cmp_k", "cmp_shifted", "cmp_probs", "cmp_done"),
            "gdn_by_scalar": ("gdn_ln", "gdn_eg", "gdn_osq", "gdn_oroot"),
            "gdn_by_vector": ("gdn_xx", "gdn_normed", "gdn_g", "gdn_gc_out", "gdn_oms"),
            "m_by_scalar": ("m_squares", "m_roots", "gla_ln", "hg_sig", "hg_ln", "m_osq", "m_oroot"),
            "m_by_vector": ("m_means", "m_normed", "gla_zb", "hg_f", "m_oms"),
            "dsa_by_scalar": ("dsa_ksq", "dsa_kroot"),
            "dsa_by_vector": ("dsa_kms", "dsa_roped"),
        }
        CHAINED = {name: (chain, i, len(names)) for chain, names in CHAINS.items() for i, name in enumerate(names)}

        def signal(name):
            return sem(CHAINED[name][0] if name in CHAINED else name)

        def reached(name, times):
            if name in CHAINED:
                _, i, n = CHAINED[name]
                return n * (times - 1) + i + 1
            return times

        def sb(name, cols, dt=F32):
            return ctx.enter_context(nc.sbuf_tensor(name, [P, cols], dt))

        x_t = sb("x", T * D)
        X = x_t[:, :].rearrange("p (t d) -> p t d", t=T)
        ht_t = sb("hT", KD * S)
        HT = ht_t[:, :].rearrange("p (k s) -> p k s", k=KD)
        xn_t = sb("xn", T * D)
        XN = xn_t[:, :].rearrange("p (t d) -> p t d", t=T)
        mix_t = sb("mix", T * D)
        MIX = mix_t[:, :].rearrange("p (t d) -> p t d", t=T)
        ring = sb("ring", RING * HALF)

        ident_t = sb("ident", P)
        IDENT = ident_t[:, :]
        ones_t = sb("ones", P)
        ONES = ones_t[:, :]
        upper_t = sb("upper", P)
        UPPER = upper_t[:, :]
        supper_t = sb("supper", P)
        SUPPER = supper_t[:, :]
        slow_t = sb("slower", P)
        SLOWER = slow_t[:, :]
        iota_t = sb("iota", P)
        ms_t = sb("lvl_lower", LEVELS * P)
        MS = ms_t[:, :].rearrange("p (l c) -> p l c", l=LEVELS)
        mt_t = sb("lvl_upper", (LEVELS + 1) * P)
        MT = mt_t[:, :].rearrange("p (l c) -> p l c", l=LEVELS + 1)
        cb_t = sb("causal_bias", T * S)
        CB = cb_t[:, :].rearrange("p (t s) -> p t s", t=T)
        cok_t = sb("cmp_ok", T * 32)
        COK = cok_t[:, :].rearrange("p (t n) -> p t n", t=T)
        cbias_t = sb("cmp_bias", T * 32)
        CBIAS = cbias_t[:, :].rearrange("p (t n) -> p t n", t=T)
        cols_t = sb("param_cols", 64 + 192)
        GAINC = cols_t[:, 0:64]
        TAPS = cols_t[:, 64:256].rearrange("p (l k c) -> p l k c", l=DEPTH, k=CONV)
        rows_t = sb("param_rows", 2440)
        at = [0]

        def rows(n):
            at[0] += n
            return rows_t[:, at[0] - n:at[0]]

        R_GDN = rows(DEPTH * DK)
        R_KI = rows(DEPTH * IDX_D)
        R_DT = rows(DEPTH * GH)
        R_EA = rows(DEPTH * GH)
        R_NSA = rows(DEPTH * 4 * HD)
        R_DQK = rows(DEPTH * 2 * 32)
        R_LAM = rows(DEPTH * 4 * 32)
        R_DN = rows(DEPTH * HD)
        R_GLAN = rows(DEPTH * HD)
        R_HGN = rows(DEPTH * HD)
        CMPPOS = rows(DEPTH * CMP_L)
        GLAB = rows(DEPTH)
        WG2 = rows(DEPTH * P)
        LBC = rows(2 * 4)
        FREQ = rows(24)
        EPS1, EPSK = rows(1), rows(1)
        sm_t = sb("small", 1100)
        sat = [0]

        def small(n):
            sat[0] += n
            return sm_t[:, sat[0] - n:sat[0]]

        SS, MSQ, RT, RSTD = small(2), small(2), small(2), small(2)
        SIN, COS = small(T * 24), small(T * 24)
        T_ANG, T_K = small(T * 24), small(T * 24)
        POSF = small(T)
        pos_t = sb("pos", T, I32)
        w2_t = sb("cmp_w2", DEPTH * 2 * 2 * HD)
        W2 = w2_t[:, :].rearrange("p (l j k n) -> p l j k n", l=DEPTH, j=2, k=2)
        router_t = sb("router", KD * NE)
        ROUTER = router_t[:, :].rearrange("p (k e) -> p k e", k=KD)

        AREA = 22720
        area = sb("area", AREA)

        def view(a, n):
            assert a + n <= AREA
            return area[:, a:a + n]

        psum = ctx.enter_context(nc.psum_tensor("psum", [P, 8, 512], F32))
        PS = psum[:, :, :]

        def banks(a, n):
            return PS[:, a:a + n, :].rearrange("p b c -> p (b c)")

        told = {}

        class Steps:

            def __init__(self, eng, name):
                self.eng, self.own, self.n, self.fences = eng, sem(name + "_steps"), 0, 0

            def do(self, ins):
                self.n += 1
                ins.then_inc(self.own, 1)
                self.eng.wait_ge(self.own, self.n)

            def after(self, ins, name):
                told[name] = told.get(name, 0) + 1
                self.eng.wait_ge(signal(name), reached(name, told[name]))

            def fence(self):
                self.fences += 1
                self.eng.drain().then_inc(sem("fence"), 1)
                self.eng.wait_ge(sem("fence"), 4 * self.fences)

        TILES, LOADS = [], []

        def half_view(n, shape):
            k, w = shape
            r = n % RING
            return ring[:, r * HALF:r * HALF + k * w].rearrange("p (k w) -> p k w", k=k)

        def kview(w):
            return w.rearrange("(k p) n -> p k n", p=P)

        def tile(group, w, c0, n, evac, nk=KD):
            per = nk if nk * n <= HALF else nk // 2
            first = len(LOADS)
            for k in range(0, nk, per):
                LOADS.append(((per, n), [(None, kview(w)[:, k:k + per, c0:c0 + n])]))
            TILES.append(dict(group=group, n=n, c0=c0, evac=evac, first=first, halves=nk // per, per=per, nk=nk,
                              end=len(LOADS)))

        def span(group, w, c0, c1, evac, nk=KD):
            for c in range(c0, c1, 512):
                tile(group, w, c, min(512, c1 - c), evac, nk)

        CMPW = {}
        DOWN = {}
        for L in range(DEPTH):
            w = A["w_in"][L]
            span(("qkv", L), w, QKV0, ZB0, "act")
            span(("p1b", L), w, ZB0, GATE0, "act")
            span(("p1", L), w, 0, QKV0, "act")
            span(("gate", L), w, GATE0, COLS1, "act")
            span(("out", L), A["w_out"][L], 0, D, "dve")
        for L in range(DEPTH):
            span(("u", L), A["w_in_2"][L], 0, COLS2, "act")
            CMPW[L] = len(LOADS)
            for q in range(4):
                src = A["nsa_cmp_w1_2"][L].rearrange("j (l d) n -> j d l n", d=HD)
                LOADS.append(((8, 256), [(j, src[j, :, 8 * q:8 * q + 8, :]) for j in range(2)]))
            span(("out2", L), A["w_out_2"][L], 0, D, "dve")
            if L % 2 == 0:
                for c in range(0, FF, 512):
                    tile(("ffn", L), A["ffn_w_gate_2"][0], c, 512, "act")
                    tile(("ffn", L), A["ffn_w_up_2"][0], c, 512, "dve")
                DOWN[L] = len(LOADS)
                for k in range(0, FF // P, 2):
                    LOADS.append(((2, D), [(None, kview(A["ffn_w_down_2"][0])[:, k:k + 2, :])]))
            else:
                MOE0 = len(LOADS)
                for _ in range(NE * PER_EXPERT):
                    LOADS.append(None)
            span(("pg", L), A["ple_w_gate_2"][L], 0, D, "act")
            span(("pp", L), A["ple_w_proj_2"][L], 0, D, "dve", PLE // P)
        LANDED, counts = [], [0] * RING
        for n, load in enumerate(LOADS):
            counts[n % RING] += 16 * (len(load[1]) if load else 1)
            LANDED.append(counts[n % RING])
        assert PER_EXPERT % RING == 0

        def group(name, L):
            return [g for g, d in enumerate(TILES) if d["group"] == (name, L)]

        def evacuated(g):
            kind = TILES[g]["evac"]
            return "gemm_out_" + kind, sum(1 for d in TILES[:g + 1] if d["evac"] == kind)

        def acc(g):
            return PS[:, 2 * (g % 2):2 * (g % 2) + 2, :]

        def landed(eng, n):
            eng.wait_ge(sem(f"landed{n % RING}"), LANDED[n])

        def used(n):
            return n + 1

        def gemm_begin(pe, g):
            if g >= 2:
                name, value = evacuated(g - 2)
                pe.wait_ge(sem(name), value)

        def gemm(pe, g, lhs):
            d = TILES[g]
            gemm_begin(pe, g)
            for h in range(d["halves"]):
                n = d["first"] + h
                landed(pe, n)
                w = half_view(n, (d["per"], d["n"]))
                for k in range(d["per"]):
                    kk = h * d["per"] + k
                    for t in range(T):
                        last = nc.tensor.matmul(acc(g)[:, t, 0:d["n"]], lhs(kk, t), w[:, k, :],
                                                start=kk == 0, stop=kk == d["nk"] - 1)
                last.then_inc(sem("weights_used"), 1)

        def ht_lhs(k, t):
            return HT[:, k, t * P:(t + 1) * P]

        def transposes(blocks, bank0):
            for b, block in enumerate(blocks):
                for t in range(T):
                    src = block(t)
                    m = src.shape[1]
                    last = nc.tensor.transpose(PS[0:m, bank0 + b // 2, (b % 2) * S + t * P:(b % 2) * S + (t + 1) * P],
                                               src, IDENT)
            return last

        def bc(ap, shape):
            return ap.to_broadcast(shape)

        def norm_act(s, n):
            if n == 0:
                s.eng.wait_ge(sem("x_loaded"), 16)
            else:
                s.eng.wait_ge(sem("x_updated"), n)
            s.do(nc.scalar.activation(XN[:, 0, :], X[:, 0, :], ACT.Square, accum_out=SS[:, 0:1]))
            s.after(nc.scalar.activation(XN[:, 1, :], X[:, 1, :], ACT.Square, accum_out=SS[:, 1:2]).then_inc(sem("norm_sums"), 1), "norm_sums")
            s.eng.wait_ge(sem("norm_means"), n + 1)
            s.after(nc.scalar.activation(RT, MSQ, ACT.Sqrt).then_inc(sem("norm_roots"), 1), "norm_roots")

        def norm_dve(s, n, gain):
            s.eng.wait_ge(sem("norm_sums"), n + 1)
            s.after(nc.vector.tensor_scalar(MSQ, SS, 1.0 / D, EPS, ALU.mult, ALU.add).then_inc(sem("norm_means"), 1), "norm_means")
            s.eng.wait_ge(sem("norm_roots"), n + 1)
            s.do(nc.vector.reciprocal(RSTD, RT))
            for t in range(T):
                ins = nc.vector.tensor_scalar(XN[:, t, :], X[:, t, :], RSTD[:, t:t + 1], None, ALU.mult)
                if t == 0:
                    s.do(ins)
                else:
                    s.after(ins.then_inc(sem("xn_ready"), 1), "xn_ready")
            if gain is not None:
                s.eng.wait_ge(sem("norm_transposed"), told.get("ht_ready", 0) + 1)
                s.after(nc.vector.tensor_tensor(HT, banks(4, 4).rearrange("p (k s) -> p k s", k=KD),
                                               bc(gain.unsqueeze(2), [P, KD, S]), ALU.mult).then_inc(sem("ht_ready"), 1), "ht_ready")

        def norm_pe(pe, n):
            pe.wait_ge(sem("xn_ready"), n + 1)
            last = transposes([(lambda t, k=k: XN[:, t, k * P:(k + 1) * P]) for k in range(KD)], 4)
            last.then_inc(sem("norm_transposed"), 1)

        U = view(0, T * (QKV0)).rearrange("p (t c) -> p t c", t=T)
        P1B = view(6288, T * W_P1B).rearrange("p (t c) -> p t c", t=T)
        Y = view(8368, CT * S).rearrange("p (c s) -> p c s", c=CT)
        XC = view(14512, CT * (S + 3)).rearrange("p (c s) -> p c s", c=CT)

        def proj1_pe(pe, L):
            pe.wait_ge(sem("ht_ready"), L + 1)
            for g in group("qkv", L):
                d = TILES[g]
                gemm_begin(pe, g)
                for h in range(2):
                    landed(pe, d["first"] + h)
                for j in range(4):
                    for k in range(KD):
                        n = d["first"] + k // 4
                        last = nc.tensor.matmul(
                            acc(g)[:, j // 2, (j % 2) * S:(j % 2) * S + S],
                            half_view(n, (4, 512))[:, k % 4, j * P:(j + 1) * P], HT[:, k, :],
                            start=k == 0, stop=k == KD - 1)
                        if j == 3 and k % 4 == 3:
                            last.then_inc(sem("weights_used"), 1)
            for g in group("p1b", L) + group("p1", L):
                gemm(pe, g, ht_lhs)

        def proj1_act(s, L):
            for j, g in enumerate(group("qkv", L)):
                s.eng.wait_ge(sem("weights_used"), used(TILES[g]["end"] - 1))
                src = acc(g).rearrange("p b (j s) -> p (b j) s", j=2)
                s.after(nc.scalar.activation(XC[:, 4 * j:4 * j + 4, 3:3 + S], src, ACT.Copy).then_inc(sem("gemm_out_act"), 1), "gemm_out_act")
            for name, dst, base in (("p1b", P1B, ZB0), ("p1", U, 0)):
                for g in group(name, L):
                    d = TILES[g]
                    s.eng.wait_ge(sem("weights_used"), used(d["end"] - 1))
                    a, b = d["c0"], d["c0"] + d["n"]
                    z0, z1 = (ZB0, BETA0) if name == "p1b" else (Z0, QI0)
                    parts = [(max(a, lo), min(b, hi), f) for lo, hi, f in
                             ((0, z0, ACT.Copy), (z0, z1, ACT.Silu), (z1, COLS1, ACT.Copy)) if max(a, lo) < min(b, hi)]
                    for i, (lo, hi, f) in enumerate(parts):
                        ins = nc.scalar.activation(dst[:, :, lo - base:hi - base], acc(g)[:, :, lo - a:hi - a], f)
                        if i < len(parts) - 1:
                            s.do(ins)
                        else:
                            s.after(ins.then_inc(sem("gemm_out_act"), 1), "gemm_out_act")
            for j in range(6):
                s.eng.wait_ge(sem("conv_done"), 6 * L + j + 1)
                s.do(nc.scalar.activation(Y[:, 4 * j:4 * j + 4, :], Y[:, 4 * j:4 * j + 4, :], ACT.Silu))

        def conv_dve(s, L):
            if L == 0:
                s.eng.wait_ge(sem("params_ready"), 1)
            s.do(nc.vector.memset(XC[:, :, 0:3], 0.0))
            for j, g in enumerate(group("qkv", L)):
                s.eng.wait_ge(sem("gemm_out_act"), evacuated(g)[1])
                for tap in range(CONV):
                    for c in range(4 * j, 4 * j + 4):
                        w = TAPS[:, L, tap, c:c + 1]
                        if tap == 0:
                            ins = nc.vector.tensor_scalar(Y[:, c, :], XC[:, c, 0:S], w, None, ALU.mult)
                        else:
                            ins = nc.vector.scalar_tensor_tensor(Y[:, c, :], XC[:, c, tap:tap + S], w, Y[:, c, :],
                                                                 ALU.mult, ALU.add)
                        if tap == CONV - 1 and c == 4 * j + 3:
                            s.after(ins.then_inc(sem("conv_done"), 1), "conv_done")
                        elif c == 4 * j + 3:
                            s.do(ins)

        HG = 4 * P
        G0 = 14512
        SQ = view(G0, 2048)
        RN = view(G0 + 2048, 2048)

        def unit(k):
            return [view(G0 + k * 1024 + u * 512, 512).rearrange("p (h c) -> p h c", h=4) for u in range(2)]

        LF, LM, XI, XT, VV, AT, BV = [unit(k) for k in range(7)]
        VN = LM
        STATE = view(G0 + 7168, GH * P).rearrange("p (h c) -> p h c", h=GH)
        GG = small(T * GH)
        G3 = GG.rearrange("p (t h) -> p t h", t=T)
        BETA = small(T * GH)
        B3 = BETA.rearrange("p (t h) -> p t h", t=T)
        GC = small(3 * GH)
        EG = small(2 * GH)
        EGL = small(GH)
        GTMP, GTMP2 = small(T * GH), small(T * GH)
        ONM, ONR = small(T * GH), small(T * GH)

        def sm3(ap):
            return ap.rearrange("p (t h) -> p t h", t=T)

        def gdn_pe(pe, L):
            for hq in range(2):
                pe.wait_ge(sem("gdn_squares"), 2 * L + hq + 1)
                for b in range(4):
                    last = nc.tensor.matmul(PS[:, 4 * hq + b, :], ONES, SQ[:, 512 * b:512 * b + 512] if hq == 0
                                            else RN[:, 512 * b:512 * b + 512], start=True, stop=True)
                last.then_inc(sem("gdn_sums"), 1)
            pe.wait_ge(signal("gdn_g"), reached("gdn_g", L + 1))
            pe.wait_ge(signal("gdn_normed"), reached("gdn_normed", L + 1))
            for c in range(2):
                nc.tensor.matmul(PS[:, 0, c * GH:c * GH + GH], UPPER, G3[:, c, :], start=True, stop=True)
            nc.tensor.matmul(PS[:, 0, 2 * GH:3 * GH], ONES, G3[:, 0, :], start=True, stop=True)\
                .then_inc(sem("gdn_gc"), 1)
            pe.wait_ge(signal("gdn_gc_out"), reached("gdn_gc_out", L + 1))
            for c in range(2):
                tok = slice(c * P, (c + 1) * P)
                for u in range(2):
                    for h in range(4):
                        hh, cs = 4 * u + h, slice(h * P, (h + 1) * P)
                        q, k = Y[:, hh, tok], Y[:, GH + hh, tok]
                        nc.tensor.matmul(PS[:, u, cs], k, k, start=True, stop=True)
                        nc.tensor.matmul(PS[:, 2 + u, cs], k, q, start=True, stop=True)
                        last = nc.tensor.matmul(PS[:, 4 + u, cs], bc(G3[:, c, hh:hh + 1], [P, P]), UPPER,
                                                start=True, stop=True)
                    last.then_inc(sem("gdn_scores"), 1)
                for lv in range(LEVELS):
                    base = ((2 * L + c) * LEVELS + lv) * 2
                    for u in range(2):
                        if lv == 0:
                            pe.wait_ge(sem("gdn_init"), 4 * L + 2 * c + u + 1)
                        else:
                            pe.wait_ge(sem("gdn_X"), base - 2 + u + 1)
                        pe.wait_ge(sem("gdn_Lm"), base + u + 1)
                        for h in range(4):
                            last = nc.tensor.matmul(PS[:, u, h * P:(h + 1) * P], LM[u][:, h, :], XT[u][:, h, :],
                                                    start=True, stop=True)
                        last.then_inc(sem("gdn_V"), 1)
                    for u in range(2):
                        pe.wait_ge(sem("gdn_V_out"), base + u + 1)
                        for h in range(4):
                            nc.tensor.matmul(PS[:, 2 + u, h * P:(h + 1) * P], VV[u][:, h, :], XI[u][:, h, :],
                                             start=True, stop=True)
                        for h in range(4):
                            last = nc.tensor.matmul(PS[:, 4 + u, h * P:(h + 1) * P], XI[u][:, h, :], VV[u][:, h, :],
                                                    start=True, stop=True)
                        last.then_inc(sem("gdn_Z"), 1)
                for u in range(2):
                    n = 4 * L + 2 * c + u
                    for h in range(4):
                        hh, cs = 4 * u + h, slice(h * P, (h + 1) * P)
                        last = nc.tensor.transpose(PS[:, 6 + u, cs], Y[:, 2 * GH + hh, tok], IDENT)
                    pe.wait_ge(sem("gdn_X"), ((2 * L + c) * LEVELS + LEVELS - 1) * 2 + u + 1)
                    if c == 1:
                        for h in range(4):
                            hh, cs = 4 * u + h, slice(h * P, (h + 1) * P)
                            nc.tensor.matmul(PS[:, u, cs], Y[:, GH + hh, tok], STATE[:, hh, :], start=True, stop=True)
                            last = nc.tensor.matmul(PS[:, 2 + u, cs], Y[:, hh, tok], STATE[:, hh, :],
                                                    start=True, stop=True)
                    else:
                        for h in range(4):
                            last = nc.tensor.transpose(PS[:, u, h * P:(h + 1) * P], Y[:, GH + 4 * u + h, tok], IDENT)
                    last.then_inc(sem("gdn_vT"), 1)
                    pe.wait_ge(sem("gdn_B"), n + 1)
                    for h in range(4):
                        last = nc.tensor.matmul(PS[:, 4 + u, h * P:(h + 1) * P], XT[u][:, h, :], BV[u][:, h, :],
                                                start=True, stop=True)
                    last.then_inc(sem("gdn_vn"), 1)
                    pe.wait_ge(sem("gdn_vn_out"), n + 1)
                    for h in range(4):
                        last = nc.tensor.matmul(PS[:, 6 + u, h * P:(h + 1) * P], AT[u][:, h, :], VN[u][:, h, :],
                                                start=True, stop=True)
                    last.then_inc(sem("gdn_o"), 1)
                    if c == 0:
                        pe.wait_ge(sem("gdn_vd"), 2 * L + u + 1)
                        pe.wait_ge(sem("gdn_k_out"), 2 * L + u + 1)
                        for h in range(4):
                            last = nc.tensor.matmul(PS[:, 2 + u, h * P:(h + 1) * P], LF[u][:, h, :], BV[u][:, h, :],
                                                    start=True, stop=True)
                        last.then_inc(sem("gdn_state"), 1)
                if c == 0:
                    pe.wait_ge(sem("gdn_state_out"), 2 * L + 2)
                    pe.wait_ge(sem("gdn_o_out"), 4 * L + 2)

        def gdn_act(s, L):
            s.do(nc.scalar.activation(SQ, Y[:, 0:GH, :].rearrange("p c s -> p (c s)"), ACT.Square))
            s.after(nc.scalar.nop() if False else nc.scalar.activation(SQ[:, 0:1], SQ[:, 0:1], ACT.Copy).then_inc(sem("gdn_squares"), 1), "gdn_squares")
            s.after(nc.scalar.activation(RN, Y[:, GH:2 * GH, :].rearrange("p c s -> p (c s)"), ACT.Square).then_inc(sem("gdn_squares"), 1), "gdn_squares")
            for hq in range(2):
                s.eng.wait_ge(sem("gdn_sums"), 2 * L + hq + 1)
                dst = SQ if hq == 0 else RN
                scale, eps = (float(DK), EPSK) if hq == 0 else (1.0, EPS1)
                s.after(nc.scalar.activation(dst, banks(4 * hq, 4), ACT.Sqrt, bias=eps, scale=scale).then_inc(sem("gdn_roots"), 1), "gdn_roots")
            s.do(nc.scalar.activation(B3, P1B[:, :, D:D + GH], ACT.Sigmoid))
            s.eng.wait_ge(signal("gdn_xx"), reached("gdn_xx", L + 1))
            s.do(nc.scalar.activation(GTMP2, GTMP, ACT.Abs))
            s.do(nc.scalar.activation(GTMP2, GTMP2, ACT.Exp, scale=-1.0))
            s.after(nc.scalar.activation(GTMP2, GTMP2, ACT.Ln, bias=1.0).then_inc(signal("gdn_ln"), 1), "gdn_ln")
            s.eng.wait_ge(signal("gdn_gc_out"), reached("gdn_gc_out", L + 1))
            s.do(nc.scalar.activation(EG, GC[:, 0:2 * GH], ACT.Exp))
            s.after(nc.scalar.activation(EGL, GC[:, 2 * GH:3 * GH], ACT.Exp).then_inc(signal("gdn_eg"), 1), "gdn_eg")
            for c in range(2):
                for u in range(2):
                    s.eng.wait_ge(sem("gdn_gaps"), 4 * L + 2 * c + u + 1)
                    s.do(nc.scalar.activation(XT[u], XT[u], ACT.Exp, scale=-1.0))
                    s.after(nc.scalar.activation(XI[u], XI[u], ACT.Exp).then_inc(sem("gdn_decays"), 1), "gdn_decays")
                for lv in range(LEVELS):
                    for u in range(2):
                        s.eng.wait_ge(sem("gdn_V"), ((2 * L + c) * LEVELS + lv) * 2 + u + 1)
                        s.after(nc.scalar.activation(VV[u], PS[:, u, :].rearrange("p (h c) -> p h c", h=4), ACT.Copy).then_inc(sem("gdn_V_out"), 1), "gdn_V_out")
                for u in range(2):
                    n = 4 * L + 2 * c + u
                    s.eng.wait_ge(sem("gdn_vT"), n + 1)
                    if c == 0:
                        s.after(nc.scalar.activation(LF[u], PS[:, u, :].rearrange("p (h c) -> p h c", h=4), ACT.Copy).then_inc(sem("gdn_k_out"), 1), "gdn_k_out")
                    s.eng.wait_ge(sem("gdn_vn"), n + 1)
                    s.after(nc.scalar.activation(VN[u], PS[:, 4 + u, :].rearrange("p (h c) -> p h c", h=4), ACT.Copy).then_inc(sem("gdn_vn_out"), 1), "gdn_vn_out")
                    if c == 0:
                        s.eng.wait_ge(sem("gdn_state"), 2 * L + u + 1)
                        s.after(nc.scalar.activation(STATE[:, 4 * u:4 * u + 4, :],
                                                    PS[:, 2 + u, :].rearrange("p (h c) -> p h c", h=4), ACT.Copy).then_inc(sem("gdn_state_out"), 1), "gdn_state_out")
            s.eng.wait_ge(sem("gdn_o_out"), 4 * L + 4)
            s.after(nc.scalar.activation(SQ, mix_t[:, :], ACT.Square).then_inc(signal("gdn_osq"), 1), "gdn_osq")
            s.eng.wait_ge(signal("gdn_oms"), reached("gdn_oms", L + 1))
            s.after(nc.scalar.activation(ONR, ONM, ACT.Sqrt).then_inc(signal("gdn_oroot"), 1), "gdn_oroot")

        def gdn_pool(s, L):
            for c in range(2):
                for lv in range(LEVELS):
                    for u in range(2):
                        base = ((2 * L + c) * LEVELS + lv) * 2
                        if lv == 0:
                            s.eng.wait_ge(sem("gdn_init"), 4 * L + 2 * c + u + 1)
                            if c == 1:
                                s.eng.wait_ge(sem("gdn_o_out"), 4 * L + u + 1)
                        else:
                            s.eng.wait_ge(sem("gdn_V"), base - 2 + u + 1)
                        s.after(nc.gpsimd.tensor_tensor(LM[u], LF[u], bc(MS[:, lv, :].unsqueeze(1), [P, 4, P]),
                                                       ALU.mult).then_inc(sem("gdn_Lm"), 1), "gdn_Lm")

        def gdn_dve(s, L):
            if L == 0:
                s.eng.wait_ge(sem("params_ready"), 1)
            s.do(nc.vector.tensor_tensor(sm3(GTMP), P1B[:, :, D + GH:D + 2 * GH],
                                         bc(R_DT[:, L * GH:(L + 1) * GH].unsqueeze(1), [P, T, GH]), ALU.add))
            s.after(nc.vector.tensor_scalar(GTMP, GTMP, 1.0, None, ALU.mult).then_inc(signal("gdn_xx"), 1), "gdn_xx")
            for hq in range(2):
                s.eng.wait_ge(sem("gdn_roots"), 2 * L + hq + 1)
                r = SQ if hq == 0 else RN
                s.do(nc.vector.reciprocal(r, r))
                q = Y[:, GH * hq:GH * hq + GH, :].rearrange("p c s -> p (c s)")
                ins = nc.vector.tensor_tensor(q, q, r, ALU.mult)
                if hq == 0:
                    s.do(ins)
                else:
                    s.after(ins.then_inc(signal("gdn_normed"), 1), "gdn_normed")
            s.eng.wait_ge(signal("gdn_ln"), reached("gdn_ln", L + 1))
            s.do(nc.vector.scalar_tensor_tensor(GTMP, GTMP, 0.0, GTMP2, ALU.max, ALU.add))
            s.after(nc.vector.scalar_tensor_tensor(G3, sm3(GTMP), -1.0,
                                                  bc(R_EA[:, L * GH:(L + 1) * GH].unsqueeze(1), [P, T, GH]),
                                                  ALU.mult, ALU.mult).then_inc(signal("gdn_g"), 1), "gdn_g")
            s.eng.wait_ge(sem("gdn_gc"), L + 1)
            s.do(nc.vector.tensor_copy(GC, PS[:, 0, 0:3 * GH]))
            s.after(nc.vector.tensor_tensor(GC[:, 2 * GH:], GC[:, 2 * GH:], GC[:, 0:GH], ALU.subtract).then_inc(signal("gdn_gc_out"), 1), "gdn_gc_out")
            s.eng.wait_ge(signal("gdn_eg"), reached("gdn_eg", L + 1))
            for c in range(2):
                for u in range(2):
                    n = 4 * L + 2 * c + u
                    hs = slice(c * GH + 4 * u, c * GH + 4 * u + 4)
                    p3 = [PS[:, b + u, :].rearrange("p (h c) -> p h c", h=4) for b in (0, 2, 4)]
                    s.eng.wait_ge(sem("gdn_scores"), n + 1)
                    s.do(nc.vector.tensor_tensor(XI[u], p3[2], bc(GC[:, hs].unsqueeze(2), [P, 4, P]), ALU.subtract))
                    s.do(nc.vector.tensor_scalar(XT[u], XI[u], 0.0, None, ALU.max))
                    s.after(nc.vector.tensor_scalar(XI[u], XI[u], 0.0, None, ALU.min).then_inc(sem("gdn_gaps"), 1), "gdn_gaps")
                for u in range(2):
                    n = 4 * L + 2 * c + u
                    hs = slice(c * GH + 4 * u, c * GH + 4 * u + 4)
                    p3 = [PS[:, b + u, :].rearrange("p (h c) -> p h c", h=4) for b in (0, 2, 4)]
                    s.eng.wait_ge(sem("gdn_decays"), n + 1)
                    s.do(nc.vector.tensor_tensor(XT[u], XT[u], bc(SLOWER.unsqueeze(1), [P, 4, P]), ALU.mult))
                    s.do(nc.vector.tensor_tensor(XT[u], XT[u], bc(BETA[:, hs].unsqueeze(2), [P, 4, P]), ALU.mult))
                    s.do(nc.vector.tensor_tensor(LF[u], p3[0], XT[u], ALU.mult))
                    s.do(nc.vector.tensor_tensor(XI[u], XI[u], bc(UPPER.unsqueeze(1), [P, 4, P]), ALU.mult))
                    s.do(nc.vector.tensor_tensor(AT[u], p3[1], XI[u], ALU.mult))
                    s.do(nc.vector.tensor_copy(XI[u], bc(IDENT.unsqueeze(1), [P, 4, P])))
                    s.after(nc.vector.tensor_copy(XT[u], bc(IDENT.unsqueeze(1), [P, 4, P])).then_inc(sem("gdn_init"), 1), "gdn_init")
                for lv in range(LEVELS):
                    for u in range(2):
                        s.eng.wait_ge(sem("gdn_Z"), ((2 * L + c) * LEVELS + lv) * 2 + u + 1)
                        z = [PS[:, b + u, :].rearrange("p (h c) -> p h c", h=4) for b in (2, 4)]
                        s.do(nc.vector.tensor_tensor(XI[u], XI[u], z[0], ALU.subtract))
                        s.after(nc.vector.tensor_tensor(XT[u], XT[u], z[1], ALU.subtract).then_inc(sem("gdn_X"), 1), "gdn_X")
                for u in range(2):
                    n = 4 * L + 2 * c + u
                    hs = slice(c * GH + 4 * u, c * GH + 4 * u + 4)
                    beta, eg = bc(BETA[:, hs].unsqueeze(2), [P, 4, P]), bc(EG[:, hs].unsqueeze(2), [P, 4, P])
                    pk, pq, pn, pv = [PS[:, b + u, :].rearrange("p (h c) -> p h c", h=4) for b in (0, 2, 4, 6)]
                    o = MIX[:, c, 512 * u:512 * u + 512].rearrange("p (h c) -> p h c", h=4)
                    s.eng.wait_ge(sem("gdn_vT"), n + 1)
                    if c == 0:
                        s.after(nc.vector.tensor_tensor(BV[u], pv, beta, ALU.mult).then_inc(sem("gdn_B"), 1), "gdn_B")
                    else:
                        s.do(nc.vector.tensor_tensor(o, pq, eg, ALU.mult))
                        s.do(nc.vector.tensor_tensor(BV[u], pk, eg, ALU.mult))
                        s.do(nc.vector.tensor_tensor(BV[u], pv, BV[u], ALU.subtract))
                        s.after(nc.vector.tensor_tensor(BV[u], BV[u], beta, ALU.mult).then_inc(sem("gdn_B"), 1), "gdn_B")
                    if c == 0:
                        s.eng.wait_ge(sem("gdn_vn_out"), n + 1)
                        s.after(nc.vector.tensor_tensor(
                            BV[u], VN[u], bc(EGL[:, 4 * u:4 * u + 4].unsqueeze(2), [P, 4, P]), ALU.mult).then_inc(sem("gdn_vd"), 1), "gdn_vd")
                    s.eng.wait_ge(sem("gdn_o"), n + 1)
                    if c == 0:
                        s.after(nc.vector.tensor_copy(o, pv).then_inc(sem("gdn_o_out"), 1), "gdn_o_out")
                    else:
                        s.after(nc.vector.tensor_tensor(o, o, pv, ALU.add).then_inc(sem("gdn_o_out"), 1), "gdn_o_out")
            s.eng.wait_ge(signal("gdn_osq"), reached("gdn_osq", L + 1))
            s.do(nc.vector.tensor_reduce(ONM, SQ.rearrange("p (g c) -> p g c", c=P), AX.X, ALU.add))
            s.after(nc.vector.tensor_scalar(ONM, ONM, 1.0 / DK, EPS, ALU.mult, ALU.add).then_inc(signal("gdn_oms"), 1), "gdn_oms")
            s.eng.wait_ge(signal("gdn_oroot"), reached("gdn_oroot", L + 1))
            s.do(nc.vector.reciprocal(ONR, ONR))
            o = mix_t[:, :].rearrange("p (g c) -> p g c", c=P)
            s.do(nc.vector.tensor_tensor(o, o, bc(ONR.unsqueeze(2), [P, T * GH, P]), ALU.mult))
            s.do(nc.vector.tensor_tensor(o, o, bc(R_GDN[:, L * DK:(L + 1) * DK].unsqueeze(1), [P, T * GH, P]), ALU.mult))
            s.do(nc.vector.tensor_tensor(MIX, MIX, P1B[:, :, 0:D], ALU.mult))

        TT = view(8368, 16 * S).rearrange("p (b s) -> p b s", b=16)
        SCORES = view(12464, 8 * S).rearrange("p (h s) -> p h s", h=8)
        PT = view(14512, 8 * T * P).rearrange("p (h j q) -> p h j q", h=8, j=T)
        MAXS, DEN, RDEN = small(8), small(8), small(8)

        def attn_pe(pe, n, t, maps, values, outs):
            for h, (q, k) in enumerate(maps):
                last = nc.tensor.matmul(PS[:, h // 2, (h % 2) * S:(h % 2) * S + (t + 1) * P],
                                        q[:, t * P:(t + 1) * P], k[:, 0:(t + 1) * P], start=True, stop=True)
            last.then_inc(sem("at_scores"), 1)
            pe.wait_ge(sem("at_probs"), n + 1)
            for h in range(outs):
                for j in range(t + 1):
                    last = nc.tensor.transpose(PS[:, 4 + h // 2, ((h % 2) * T + j) * P:((h % 2) * T + j + 1) * P],
                                               SCORES[:, h, j * P:(j + 1) * P], IDENT)
            last.then_inc(sem("at_transposed"), 1)
            pe.wait_ge(sem("at_PT"), n + 1)
            w = values(0, 0).shape[1]
            per = 512 // w
            for h in range(outs):
                for j in range(t + 1):
                    last = nc.tensor.matmul(PS[:, h // per, (h % per) * w:(h % per + 1) * w], PT[:, h, j, :],
                                            values(h, j), start=j == 0, stop=j == t)
            last.then_inc(sem("at_out"), 1)

        def attn_act(s, n, t, maps, outs):
            keys = (t + 1) * P
            s.eng.wait_ge(sem("at_shifted"), n + 1)
            s.after(nc.scalar.activation(SCORES[:, 0:maps, 0:keys], SCORES[:, 0:maps, 0:keys], ACT.Exp).then_inc(sem("at_exp"), 1), "at_exp")
            s.eng.wait_ge(sem("at_transposed"), n + 1)
            s.after(nc.scalar.activation(
                PT[:, 0:outs, 0:t + 1, :],
                banks(4, 4).rearrange("p (h j q) -> p h j q", h=8, j=T)[:, 0:outs, 0:t + 1, :], ACT.Copy).then_inc(sem("at_PT"), 1), "at_PT")

        def attn_softmax_dve(s, n, t, maps, scale, bias, lam=None):
            keys = (t + 1) * P
            sc = SCORES[:, 0:maps, 0:keys]
            s.eng.wait_ge(sem("at_scores"), n + 1)
            s.do(nc.vector.scalar_tensor_tensor(
                sc, banks(0, 4).rearrange("p (h s) -> p h s", h=8)[:, 0:maps, 0:keys], scale,
                bc(bias.unsqueeze(1), [P, maps, keys]), ALU.mult, ALU.add))
            s.do(nc.vector.tensor_reduce(MAXS[:, 0:maps], sc, AX.X, ALU.max))
            s.after(nc.vector.tensor_tensor(sc, sc, bc(MAXS[:, 0:maps].unsqueeze(2), [P, maps, keys]), ALU.subtract).then_inc(sem("at_shifted"), 1), "at_shifted")
            s.eng.wait_ge(sem("at_exp"), n + 1)
            if lam is None:
                s.after(nc.vector.tensor_reduce(DEN[:, 0:maps], sc, AX.X, ALU.add).then_inc(sem("at_probs"), 1), "at_probs")
                s.do(nc.vector.reciprocal(RDEN[:, 0:maps], DEN[:, 0:maps]))
            else:
                s.do(nc.vector.tensor_reduce(DEN, sc, AX.X, ALU.add))
                s.do(nc.vector.reciprocal(RDEN, DEN))
                s.do(nc.vector.tensor_scalar(RDEN[:, 4:8], RDEN[:, 4:8], lam, None, ALU.mult))
                s.do(nc.vector.tensor_tensor(sc, sc, bc(RDEN.unsqueeze(2), [P, 8, keys]), ALU.mult))
                s.after(nc.vector.tensor_tensor(sc[:, 0:4, :], sc[:, 0:4, :], sc[:, 4:8, :], ALU.subtract).then_inc(sem("at_probs"), 1), "at_probs")

        RELU = view(16560, IDX_H * S).rearrange("p (h s) -> p h s", h=IDX_H)
        OA = view(18608, T * D).rearrange("p (t d) -> p t d", t=T)
        KI2 = view(20656, T * P).rearrange("p (t c) -> p t c", t=T)
        ISC, WORK = view(20912, S), view(21168, S)
        SELB = view(21424, T * S).rearrange("p (t s) -> p t s", t=T)
        TOP8, KSS = small(8), small(T)
        SG = [view(a, T * 512).rearrange("p (t c) -> p t c", t=T) for a in (12464, 13488)]

        def trig_tables(s_dve, s_act):
            a3 = [x.rearrange("p (t f) -> p t f", t=T) for x in (T_ANG, T_K)]
            c1, c2 = 6.28125, 2 * math.pi - 6.28125
            c2 = float(np.float32(int(c2 * 2 ** 21) / 2 ** 21))
            c3 = 2 * math.pi - c1 - c2
            magic = 1.5 * 2 ** 23
            if s_dve:
                s = s_dve
                s.do(nc.vector.tensor_copy(POSF, pos_t[:, :]))
                s.do(nc.vector.tensor_tensor(a3[0], bc(POSF.unsqueeze(2), [P, T, 24]),
                                             bc(FREQ.unsqueeze(1), [P, T, 24]), ALU.mult))
                for quarter, dst in ((0.0, SIN), (0.25, COS)):
                    s.do(nc.vector.tensor_scalar(T_K, T_ANG, 1 / (2 * math.pi), quarter, ALU.mult, ALU.add))
                    s.do(nc.vector.tensor_scalar(T_K, T_K, magic, None, ALU.add))
                    s.do(nc.vector.tensor_scalar(T_K, T_K, magic, None, ALU.subtract))
                    s.do(nc.vector.scalar_tensor_tensor(dst, T_K, -c1, T_ANG, ALU.mult, ALU.add))
                    s.do(nc.vector.scalar_tensor_tensor(dst, T_K, -c2, dst, ALU.mult, ALU.add))
                    s.do(nc.vector.scalar_tensor_tensor(dst, T_K, -c3, dst, ALU.mult, ALU.add))
                    if quarter:
                        s.do(nc.vector.tensor_scalar(dst, dst, math.pi / 2, None, ALU.add))
                    s.do(nc.vector.tensor_scalar(dst, dst, 3.1415925, -3.1415925, ALU.min, ALU.max))
                s.after(nc.vector.tensor_copy(POSF, POSF).then_inc(sem("angles"), 1), "angles")
            else:
                s = s_act
                s.eng.wait_ge(sem("angles"), 1)
                s.do(nc.scalar.activation(SIN, SIN, ACT.Sin))
                s.after(nc.scalar.activation(COS, COS, ACT.Sin).then_inc(sem("tables"), 1), "tables")

        def rope(s, v, half, f0, tmp):
            heads = v.shape[2]
            cos, sin = [bc(x.rearrange("p (t f) -> p t f", t=T)[:, :, f0:f0 + half].unsqueeze(2), [P, T, heads, half])
                        for x in (COS, SIN)]
            a, b = v[:, :, :, 0:half], v[:, :, :, half:2 * half]
            t1, t2 = [x[:, 0:T * heads * half].rearrange("p (t h f) -> p t h f", t=T, h=heads) for x in tmp]
            for t in range(T):
                at, bt, ct, st, u, w = a[:, t], b[:, t], cos[:, t], sin[:, t], t1[:, t], t2[:, t]
                s.do(nc.vector.tensor_tensor(u, at, ct, ALU.mult))
                s.do(nc.vector.tensor_tensor(w, at, st, ALU.mult))
                s.do(nc.vector.tensor_tensor(at, bt, st, ALU.mult))
                s.do(nc.vector.tensor_tensor(bt, bt, ct, ALU.mult))
                s.do(nc.vector.tensor_tensor(at, u, at, ALU.subtract))
                s.do(nc.vector.tensor_tensor(bt, bt, w, ALU.add))

        def dsa_blocks():
            b = [(lambda t, h=h: U[:, t, h * DH:(h + 1) * DH]) for h in range(HQ + HKV)]
            b += [(lambda t, i=i: U[:, t, QI0 + i * P:QI0 + (i + 1) * P]) for i in range(4)]
            return b + [lambda t: KI2[:, t, :]]

        def dsa_pe(pe, L, n0):
            pe.wait_ge(signal("dsa_roped"), reached("dsa_roped", L + 1))
            blocks = dsa_blocks()
            transposes(blocks[0:8], 0)
            transposes(blocks[8:15], 4).then_inc(sem("dsa_transposed"), 1)
            for t in range(T):
                pe.wait_ge(sem("dsa_TT"), 3 * L + 3 if t == 0 else 3 * L + 3)
                if t == 1:
                    pe.wait_ge(sem("dsa_relu"), 2 * L + 1)
                for h in range(IDX_H):
                    r = slice(64 * (h % 2), 64 * (h % 2) + 64)
                    c = (h // 2 % 2) * S
                    last = nc.tensor.matmul(PS[:, 4 + 2 * (h % 2) + h // 4, c:c + (t + 1) * P],
                                            TT[r, 10 + h // 2, t * P:(t + 1) * P], TT[r, 14, 0:(t + 1) * P],
                                            start=True, stop=True)
                last.then_inc(sem("dsa_raw"), 1)
            pe.wait_ge(sem("dsa_relu"), 2 * L + 2)
            for t in range(T):
                if t:
                    pe.wait_ge(sem("dsa_out"), 2 * L + t)
                attn_pe(pe, n0 + t, t, [(TT[:, h, :], TT[:, 8 + h // 4, :]) for h in range(HQ)],
                        lambda h, j: U[:, j, V0 + (h // 4) * DH:V0 + (h // 4 + 1) * DH], HQ)

        def dsa_act(s, L, n0):
            s.do(nc.scalar.activation(KI2[:, :, 0:IDX_D], U[:, :, KI0:KI0 + IDX_D], ACT.Square))
            s.after(nc.scalar.activation(KI2[:, :, IDX_D:P], U[:, :, KI0:KI0 + IDX_D], ACT.Copy).then_inc(signal("dsa_ksq"), 1), "dsa_ksq")
            s.eng.wait_ge(signal("dsa_kms"), reached("dsa_kms", L + 1))
            s.after(nc.scalar.activation(KSS, KSS, ACT.Sqrt).then_inc(signal("dsa_kroot"), 1), "dsa_kroot")
            s.eng.wait_ge(sem("dsa_transposed"), L + 1)
            s.after(nc.scalar.activation(TT[:, 0:8, :], banks(0, 4).rearrange("p (b s) -> p b s", b=8), ACT.Copy).then_inc(sem("dsa_TT"), 1), "dsa_TT")
            s.after(nc.scalar.activation(TT[:, 8:12, :], banks(4, 2).rearrange("p (b s) -> p b s", b=4), ACT.Copy).then_inc(sem("dsa_TT"), 1), "dsa_TT")
            s.after(nc.scalar.activation(TT[:, 12:15, :], banks(6, 2).rearrange("p (b s) -> p b s", b=4)[:, 0:3, :],
                                        ACT.Copy).then_inc(sem("dsa_TT"), 1), "dsa_TT")
            for t in range(T):
                s.eng.wait_ge(sem("dsa_raw"), 2 * L + t + 1)
                if t == 1:
                    s.eng.wait_ge(sem("dsa_index"), 2 * L + 1)
                s.after(nc.scalar.activation(
                    RELU[:, :, 0:(t + 1) * P], banks(4, 4).rearrange("p (h s) -> p h s", h=8)[:, :, 0:(t + 1) * P],
                    ACT.Relu).then_inc(sem("dsa_relu"), 1), "dsa_relu")
            for t in range(T):
                attn_act(s, n0 + t, t, HQ, HQ)

        def dsa_pool(s, L):
            for t in range(T):
                s.eng.wait_ge(sem("dsa_index"), 2 * L + t + 1)
                v = ISC[:, 0:(t + 1) * P]
                s.after(nc.gpsimd.affine_select(out=v, in_=v, compare_op=ALU.is_ge, fill=NONCAUSAL, base=t * P,
                                               pattern=[[-1, (t + 1) * P]], channel_multiplier=1).then_inc(sem("dsa_edge"), 1), "dsa_edge")

        def dsa_dve(s, L, n0):
            if L == 0:
                s.eng.wait_ge(sem("tables"), 1)
            s.eng.wait_ge(signal("dsa_ksq"), reached("dsa_ksq", L + 1))
            s.do(nc.vector.tensor_reduce(KSS, KI2[:, :, 0:IDX_D], AX.X, ALU.add))
            s.after(nc.vector.tensor_scalar(KSS, KSS, 1.0 / IDX_D, EPS, ALU.mult, ALU.add).then_inc(signal("dsa_kms"), 1), "dsa_kms")
            s.eng.wait_ge(signal("dsa_kroot"), reached("dsa_kroot", L + 1))
            s.do(nc.vector.reciprocal(KSS, KSS))
            ki = U[:, :, KI0:KI0 + IDX_D]
            s.do(nc.vector.tensor_tensor(ki, ki, bc(KSS.unsqueeze(2), [P, T, IDX_D]), ALU.mult))
            s.do(nc.vector.tensor_tensor(ki, ki, bc(R_KI[:, L * IDX_D:(L + 1) * IDX_D].unsqueeze(1), [P, T, IDX_D]),
                                         ALU.mult))
            tmp = [view(14512, 512), view(15024, 512)]
            rope(s, U[:, :, 0:V0].rearrange("p t (h d) -> p t h d", d=DH), ROT // 2, 0, tmp)
            rope(s, U[:, :, QI0:WI0].rearrange("p t (h d) -> p t h d", d=IDX_D), IDX_ROT // 2, ROT // 2, tmp)
            s.do(nc.vector.tensor_copy(KI2[:, :, 0:IDX_D], ki))
            s.do(nc.vector.tensor_copy(KI2[:, :, IDX_D:P], ki))
            wi = U[:, :, WI0:WI0 + IDX_H]
            s.after(nc.vector.tensor_scalar(wi, wi, IDX_H ** -0.5 * IDX_D ** -0.5, None, ALU.mult).then_inc(signal("dsa_roped"), 1), "dsa_roped")
            for t in range(T):
                keys = (t + 1) * P
                s.eng.wait_ge(sem("dsa_relu"), 2 * L + t + 1)
                r = RELU[:, :, 0:keys]
                for hp in range(2):
                    rr = RELU[:, 4 * hp:4 * hp + 4, 0:keys]
                    s.do(nc.vector.tensor_tensor(rr, rr, bc(wi[:, t, hp::2].unsqueeze(2), [P, 4, keys]), ALU.mult))
                s.after(nc.vector.tensor_reduce(ISC[:, 0:keys], r.rearrange("p h k -> p k h"), AX.X, ALU.add).then_inc(sem("dsa_index"), 1), "dsa_index")
                s.eng.wait_ge(sem("dsa_edge"), 2 * L + t + 1)
                cur = ISC[:, 0:keys]
                for _ in range(TOPK // 8):
                    s.do(nc.vector.max(TOP8, cur))
                    s.do(nc.vector.match_replace(out=WORK[:, 0:keys], in_to_replace=TOP8, in_values=cur,
                                                 imm_value=TAKEN))
                    cur = WORK[:, 0:keys]
                s.do(nc.vector.tensor_scalar(cur, cur, TAKEN, NEG, ALU.not_equal, ALU.mult))
                s.do(nc.vector.tensor_tensor(SELB[:, t, 0:keys], cur, CB[:, t, 0:keys], ALU.add))
            for t in range(T):
                n = n0 + t
                attn_softmax_dve(s, n, t, HQ, DH ** -0.5, SELB[:, t, 0:(t + 1) * P])
                s.eng.wait_ge(sem("at_out"), n + 1)
                s.after(nc.vector.tensor_tensor(OA[:, t, :].rearrange("p (h d) -> p h d", h=HQ),
                                               banks(0, 2).rearrange("p (h d) -> p h d", h=HQ),
                                               bc(RDEN.unsqueeze(2), [P, HQ, DH]), ALU.mult).then_inc(sem("dsa_out"), 1), "dsa_out")
                s.do(nc.vector.tensor_tensor(OA[:, t, :], OA[:, t, :], U[:, t, Z0:Z0 + D], ALU.mult))

        def mix_pe(pe, name, L, k):
            pe.wait_ge(sem("mix_ready"), k + 1)
            transposes([(lambda t, j=j: MIX[:, t, j * P:(j + 1) * P]) for j in range(KD)], 4)\
                .then_inc(sem("mix_transposed"), 1)
            pe.wait_ge(sem("mixT_ready"), k + 1)
            for g in group(name, L):
                gemm(pe, g, ht_lhs)

        def mix_act(s, k):
            s.eng.wait_ge(sem("mix_transposed"), k + 1)
            s.after(nc.scalar.activation(HT, banks(4, 4).rearrange("p (k s) -> p k s", k=KD), ACT.Copy).then_inc(sem("mixT_ready"), 1), "mixT_ready")

        def residual_dve(s, name, L):
            gs = group(name, L)
            for i, g in enumerate(gs):
                d = TILES[g]
                s.eng.wait_ge(sem("weights_used"), used(d["end"] - 1))
                xs = X[:, :, d["c0"]:d["c0"] + d["n"]]
                s.after(nc.vector.tensor_tensor(xs, xs, acc(g)[:, :, 0:d["n"]], ALU.add).then_inc(sem("gemm_out_dve"), 1), "gemm_out_dve")
            s.after(nc.vector.tensor_copy(SS[:, 0:1], SS[:, 0:1]).then_inc(sem("x_updated"), 1), "x_updated")

        def gate_pe(pe, L):
            for g in group("gate", L):
                gemm(pe, g, ht_lhs)

        def gate_act(s, L):
            for i, g in enumerate(group("gate", L)):
                s.eng.wait_ge(sem("weights_used"), used(TILES[g]["end"] - 1))
                if i >= 2:
                    s.eng.wait_ge(sem("gated"), 4 * L + i - 1)
                s.after(nc.scalar.activation(SG[i % 2], acc(g), ACT.Sigmoid).then_inc(sem("gemm_out_act"), 1), "gemm_out_act")

        def gate_dve(s, L):
            for i, g in enumerate(group("gate", L)):
                s.eng.wait_ge(sem("gemm_out_act"), evacuated(g)[1])
                c = slice(512 * (i % 2), 512 * (i % 2) + 512)
                y = OA[:, :, c] if i < 2 else MIX[:, :, c]
                s.after(nc.vector.tensor_tensor(y, y, SG[i % 2], ALU.mult).then_inc(sem("gated"), 1), "gated")
            s.after(nc.vector.tensor_tensor(MIX, MIX, OA, ALU.add).then_inc(sem("mix_ready"), 1), "mix_ready")

        U2 = view(0, T * COLS2).rearrange("p (t c) -> p t c", t=T)
        SQ2 = view(16560, T * 1152).rearrange("p (t c) -> p t c", t=T)
        KDUP = view(18864, T * 256).rearrange("p (t w r d) -> p t w r d", t=T, w=2, r=2)
        CX = view(19376, CMP_L * 16).rearrange("p (l n) -> p l n", l=CMP_L)
        HID4 = view(19888, 512).rearrange("p (g r n) -> p g r n", g=4, r=4)
        KCD = view(20400, P).rearrange("p (r d) -> p r d", r=2)
        KCT, VBD = view(20528, P), view(20656, 256)
        CS = view(20912, 256).rearrange("p (t h n) -> p t h n", t=T, h=4)
        PCT = view(21168, 256).rearrange("p (t q) -> p t q", t=T)
        O8 = view(21424, 512).rearrange("p (m d) -> p m d", m=8)
        STATS = small(52)
        ST64 = STATS[:, 0:20].rearrange("p (t g) -> p t g", t=T)
        ST32 = STATS[:, 20:52].rearrange("p (t g) -> p t g", t=T)
        GATES = small(T * 12)
        HIDT = small(4 * 15).rearrange("p (g n) -> p g n", g=4)
        KCS, RG8 = small(1), small(8)
        LAMP, LAMS, LAMC = small(64), small(2), small(DEPTH)
        CMAX, CSUM = small(8), small(8)
        OST = small(T * 12)
        G12 = rows(DEPTH * 192).rearrange("p (l m d) -> p l m d", l=DEPTH, m=3)

        def lam_init(L):
            return 0.8 - 0.6 * math.exp(-0.3 * L)

        def u_pe(pe, L):
            for g in group("u", L):
                gemm(pe, g, ht_lhs)

        def u_act(s, L):
            for g in group("u", L):
                d = TILES[g]
                s.eng.wait_ge(sem("weights_used"), used(d["end"] - 1))
                s.after(nc.scalar.activation(U2[:, :, d["c0"]:d["c0"] + d["n"]], acc(g)[:, :, 0:d["n"]], ACT.Copy).then_inc(sem("gemm_out_act"), 1), "gemm_out_act")

        def mixer_blocks():
            b = [(lambda t, i=i: U2[:, t, NQ0 + i * P:NQ0 + (i + 1) * P]) for i in range(2)]
            b += [(lambda t, i=i: KDUP[:, t, i].rearrange("p r d -> p (r d)")) for i in range(2)]
            b += [lambda t: U2[:, t, KC0:KC0 + P]]
            b += [(lambda t, c=c: U2[:, t, c:c + P]) for c in
                  (DQ0, DQ0 + P, DK0, DK0 + P, GQ0, GK0, RQ0, RQ0 + P, RF0, RF0 + P)]
            return b + [lambda t: U2[:, t, GLR0:GLR0 + 16]]

        ORDER = (0, 2, 1, 3)

        def heads2(ap, w):
            return ap.rearrange("p (hh hp d) -> p hp hh d", hh=2, hp=2)

        def nsa_map(h, block, key):
            r = slice(64 * (h % 2), 64 * (h % 2) + 64)
            return TT[r, h // 2, :], TT[r, key, :]

        NSA_MAPS = [(h, kind) for hp in range(2) for kind in range(2) for h in (hp, hp + 2)]

        def diff_map(h, c):
            f = 64 * h + 32 * c
            r = slice(f % P, f % P + 32)
            return TT[r, 5 + f // P, :], TT[r, 7 + f // P, :]

        def mixers_pe(pe, L, n0):
            pe.wait_ge(signal("m_normed"), reached("m_normed", L + 1))
            blocks = mixer_blocks()
            transposes(blocks[0:8], 0)
            transposes(blocks[8:16], 4).then_inc(sem("m_transposed"), 1)
            pe.wait_ge(signal("cmp_x"), reached("cmp_x", L + 1))
            for q in range(4):
                n = CMPW[L] + q
                landed(pe, n)
                w = half_view(n, (8, 256))
                for j in range(2):
                    r = slice(64 * j, 64 * j + 64)
                    for half in range(2):
                        for l in range(8):
                            last = nc.tensor.matmul(PS[:, 4 + 2 * j + half, 0:NCMP], w[r, l, half * P:(half + 1) * P],
                                                    CX[r, 8 * q + l, 0:NCMP], start=q + l == 0, stop=q == 3 and l == 7)
                last.then_inc(sem("weights_used"), 1)
            pe.wait_ge(signal("cmp_hid"), reached("cmp_hid", L + 1))
            for j in range(2):
                for half in range(2):
                    last = nc.tensor.matmul(PS[:, j, 0:HD], HID4[:, 2 * j + half].rearrange("p r n -> p (r n)"),
                                            W2[:, L, j, half, :], start=half == 0, stop=half == 1)
            last.then_inc(signal("cmp_kv"), 1)
            pe.wait_ge(signal("cmp_k"), reached("cmp_k", L + 1))
            nc.tensor.transpose(PS[:, 2, 0:P], KCD.rearrange("p r d -> p (r d)"), IDENT).then_inc(signal("cmp_kT"), 1)
            pe.wait_ge(signal("cmp_kT_out"), reached("cmp_kT_out", L + 1))
            for h in range(4):
                r = slice(64 * (h % 2), 64 * (h % 2) + 64)
                for t in range(T):
                    c = (2 * t + h // 2) * 32
                    last = nc.tensor.matmul(PS[:, 4 + h % 2, c:c + 32], TT[r, h // 2, t * P:(t + 1) * P],
                                            KCT[r, 0:32], start=True, stop=True)
            last.then_inc(signal("cmp_scores"), 1)
            pe.wait_ge(signal("cmp_probs"), reached("cmp_probs", L + 1))
            for t in range(T):
                last = nc.tensor.transpose(PS[:, 6, t * P:(t + 1) * P], CS[:, t].rearrange("p h n -> p (h n)"), IDENT)
            last.then_inc(signal("cmp_pT"), 1)
            pe.wait_ge(signal("cmp_pT_out"), reached("cmp_pT_out", L + 1))
            for t in range(T):
                last = nc.tensor.matmul(PS[:, 7, t * 256:(t + 1) * 256], PCT[:, t, :], VBD, start=True, stop=True)
            last.then_inc(signal("cmp_out"), 1)
            pe.wait_ge(signal("cmp_done"), reached("cmp_done", L + 1))
            for t in range(T):
                n = n0 + t
                if t:
                    pe.wait_ge(sem("nsa_out"), 2 * L + t)
                attn_pe(pe, n, t, [nsa_map(h, 0, 2 + kind) for h, kind in NSA_MAPS],
                        lambda m, j: U2[:, j, (VS0, VW0)[NSA_MAPS[m][1]]:(VS0, VW0)[NSA_MAPS[m][1]] + HD], 8)
            pe.wait_ge(sem("nsa_out"), 2 * L + 2)
            for t in range(T):
                n = n0 + 2 + t
                if t:
                    pe.wait_ge(sem("diff_out"), 2 * L + t)
                attn_pe(pe, n, t, [diff_map(h, c) for c in range(2) for h in ORDER],
                        lambda m, j: U2[:, j, DV0 + HD * ORDER[m]:DV0 + HD * (ORDER[m] + 1)], 4)
            pe.wait_ge(sem("diff_out"), 2 * L + 2)

        def mixers_act(s, L, n0):
            s.do(nc.scalar.activation(SQ2[:, :, 0:640], U2[:, :, 0:640], ACT.Square))
            s.after(nc.scalar.activation(SQ2[:, :, 640:1152], U2[:, :, DQ0:DV0], ACT.Square).then_inc(signal("m_squares"), 1), "m_squares")
            s.do(nc.scalar.activation(GATES.rearrange("p (t g) -> p t g", t=T), U2[:, :, NG0:NG0 + 12], ACT.Sigmoid))
            for c in (GOG0, ROG0):
                s.do(nc.scalar.activation(U2[:, :, c:c + 256], U2[:, :, c:c + 256], ACT.Silu))
            s.eng.wait_ge(signal("m_means"), reached("m_means", L + 1))
            s.after(nc.scalar.activation(STATS, STATS, ACT.Sqrt).then_inc(signal("m_roots"), 1), "m_roots")
            s.eng.wait_ge(sem("m_transposed"), L + 1)
            s.after(nc.scalar.activation(TT[:, 8:15, :], banks(4, 4).rearrange("p (b s) -> p b s", b=8)[:, 0:7, :],
                                        ACT.Copy).then_inc(sem("m_TT"), 1), "m_TT")
            s.after(nc.scalar.activation(TT[0:16, 15, :], PS[0:16, 7, S:2 * S], ACT.Copy).then_inc(sem("m_TT"), 1), "m_TT")
            s.after(nc.scalar.activation(TT[:, 0:8, :], banks(0, 4).rearrange("p (b s) -> p b s", b=8), ACT.Copy).then_inc(sem("m_TT"), 1), "m_TT")
            s.eng.wait_ge(sem("weights_used"), used(CMPW[L] + 3))
            s.after(nc.scalar.activation(HIDT, PS[:, 4:8, 0:NCMP], ACT.Silu).then_inc(signal("cmp_silu"), 1), "cmp_silu")
            s.eng.wait_ge(signal("cmp_kv"), reached("cmp_kv", L + 1))
            s.after(nc.scalar.activation(KCD[:, 0, :], PS[:, 0, 0:HD], ACT.Square, accum_out=KCS).then_inc(signal("cmp_ksq"), 1), "cmp_ksq")
            s.eng.wait_ge(signal("cmp_kms"), reached("cmp_kms", L + 1))
            s.after(nc.scalar.activation(KCS, KCS, ACT.Sqrt).then_inc(signal("cmp_kroot"), 1), "cmp_kroot")
            s.eng.wait_ge(signal("cmp_kT"), reached("cmp_kT", L + 1))
            s.after(nc.scalar.activation(KCT, PS[:, 2, 0:P], ACT.Copy).then_inc(signal("cmp_kT_out"), 1), "cmp_kT_out")
            s.eng.wait_ge(signal("cmp_scores"), reached("cmp_scores", L + 1))
            for hp in range(2):
                ins = nc.scalar.activation(CS.rearrange("p t (hh hp) n -> p t hh hp n", hp=2)[:, :, :, hp, :],
                                           PS[:, 4 + hp, 0:P].rearrange("p (t h n) -> p t h n", t=T, h=2),
                                           ACT.Copy, scale=HD ** -0.5)
                if hp == 0:
                    s.do(ins)
                else:
                    s.after(ins.then_inc(signal("cmp_scaled"), 1), "cmp_scaled")
            s.eng.wait_ge(signal("cmp_shifted"), reached("cmp_shifted", L + 1))
            s.after(nc.scalar.activation(CS, CS, ACT.Exp).then_inc(signal("cmp_exp"), 1), "cmp_exp")
            s.eng.wait_ge(signal("cmp_pT"), reached("cmp_pT", L + 1))
            s.after(nc.scalar.activation(PCT, PS[:, 6, 0:2 * P].rearrange("p (t q) -> p t q", t=T), ACT.Copy).then_inc(signal("cmp_pT_out"), 1), "cmp_pT_out")
            for t in range(T):
                attn_act(s, n0 + t, t, 8, 8)
            for t in range(T):
                attn_act(s, n0 + 2 + t, t, 8, 4)
                s.eng.wait_ge(sem("at_out"), n0 + 3 + t)
                s.after(nc.scalar.activation(
                    heads2(MIX[:, t, 256:512], HD), PS[:, 0, 0:256].rearrange("p (hp hh d) -> p hp hh d", hp=2, hh=2),
                    ACT.Copy).then_inc(sem("diff_out"), 1), "diff_out")

        def mixers_dve(s, L, n0):
            s.eng.wait_ge(signal("m_squares"), reached("m_squares", L + 1))
            s.do(nc.vector.tensor_reduce(ST64, SQ2[:, :, 0:640].rearrange("p t (g d) -> p t g d", d=64), AX.X, ALU.add))
            s.do(nc.vector.tensor_reduce(ST32, SQ2[:, :, 640:1152].rearrange("p t (g d) -> p t g d", d=32), AX.X,
                                         ALU.add))
            s.do(nc.vector.tensor_scalar(ST64, ST64, 1.0 / 64, EPS, ALU.mult, ALU.add))
            s.after(nc.vector.tensor_scalar(ST32, ST32, 1.0 / 32, EPS, ALU.mult, ALU.add).then_inc(signal("m_means"), 1), "m_means")
            s.eng.wait_ge(signal("m_roots"), reached("m_roots", L + 1))
            s.do(nc.vector.reciprocal(STATS, STATS))

            def gain(row, groups):
                w = row.shape[1]
                return bc(row.unsqueeze(1).unsqueeze(1), [P, T, groups, w])

            def nsa_gain(i):
                return R_NSA[:, (4 * L + i) * HD:(4 * L + i + 1) * HD]

            q = U2[:, :, NQ0:KC0].rearrange("p t (g d) -> p t g d", d=HD)
            s.do(nc.vector.tensor_tensor(q, q, bc(ST64[:, :, 0:4].unsqueeze(3), [P, T, 4, HD]), ALU.mult))
            s.do(nc.vector.tensor_tensor(q, q, gain(nsa_gain(0), 4), ALU.mult))
            for i, (c, g) in enumerate(((KS0, 6), (KW0, 8))):
                src = bc(U2[:, :, c:c + HD].unsqueeze(2), [P, T, 2, HD])
                s.do(nc.vector.tensor_tensor(KDUP[:, :, i], src, bc(ST64[:, :, g:g + 1].unsqueeze(3), [P, T, 2, HD]),
                                             ALU.mult))
                s.do(nc.vector.tensor_tensor(KDUP[:, :, i], KDUP[:, :, i], gain(nsa_gain(2 + i), 2), ALU.mult))
            for i, c in enumerate((DQ0, DK0)):
                v = U2[:, :, c:c + 256].rearrange("p t (g d) -> p t g d", d=32)
                s.do(nc.vector.tensor_tensor(v, v, bc(ST32[:, :, 8 * i:8 * i + 8].unsqueeze(3), [P, T, 8, 32]), ALU.mult))
                ins = nc.vector.tensor_tensor(v, v, gain(R_DQK[:, (2 * L + i) * 32:(2 * L + i + 1) * 32], 8), ALU.mult)
                if i == 0:
                    s.do(ins)
                else:
                    s.after(ins.then_inc(signal("m_normed"), 1), "m_normed")
            s.eng.wait_ge(sem("m_TT"), 3 * L + 3)
            blocks = TT[:, 4, :].rearrange("p (n b) -> p b n", b=CMP_S)
            for a in range(2):
                ins = nc.vector.tensor_tensor(
                    CX[:, a * CMP_S:(a + 1) * CMP_S, 0:NCMP], blocks[:, :, a:a + NCMP],
                    bc(CMPPOS[:, L * CMP_L + a * CMP_S:L * CMP_L + (a + 1) * CMP_S].unsqueeze(2), [P, CMP_S, NCMP]),
                    ALU.add)
                if a == 0:
                    s.do(ins)
                else:
                    s.after(ins.then_inc(signal("cmp_x"), 1), "cmp_x")
            s.do(nc.vector.memset(HID4, 0.0))
            s.do(nc.vector.memset(VBD, 0.0))
            s.eng.wait_ge(signal("cmp_silu"), reached("cmp_silu", L + 1))
            s.after(nc.vector.tensor_copy(HID4[:, :, :, 0:NCMP], bc(HIDT.unsqueeze(2), [P, 4, 4, NCMP])).then_inc(signal("cmp_hid"), 1), "cmp_hid")
            s.eng.wait_ge(signal("cmp_ksq"), reached("cmp_ksq", L + 1))
            s.after(nc.vector.tensor_scalar(KCS, KCS, 1.0 / HD, EPS, ALU.mult, ALU.add).then_inc(signal("cmp_kms"), 1), "cmp_kms")
            s.eng.wait_ge(signal("cmp_kroot"), reached("cmp_kroot", L + 1))
            s.do(nc.vector.reciprocal(KCS, KCS))
            s.do(nc.vector.scalar_tensor_tensor(KCD[:, 0, :], PS[:, 0, 0:HD], KCS, nsa_gain(1), ALU.mult, ALU.mult))
            s.after(nc.vector.tensor_copy(KCD[:, 1, :], KCD[:, 0, :]).then_inc(signal("cmp_k"), 1), "cmp_k")
            for h in range(4):
                r = slice(32 * h, 32 * h + 32)
                s.do(nc.vector.tensor_copy(VBD[r, HD * h:HD * (h + 1)], PS[r, 1, 0:HD]))
            s.eng.wait_ge(signal("cmp_scaled"), reached("cmp_scaled", L + 1))
            s.do(nc.vector.tensor_tensor(CS, CS, bc(CBIAS.unsqueeze(2), [P, T, 4, 32]), ALU.add))
            c8 = CS.rearrange("p t h n -> p (t h) n")
            s.do(nc.vector.tensor_reduce(CMAX, c8, AX.X, ALU.max))
            s.after(nc.vector.tensor_tensor(c8, c8, bc(CMAX.unsqueeze(2), [P, 8, 32]), ALU.subtract).then_inc(signal("cmp_shifted"), 1), "cmp_shifted")
            s.eng.wait_ge(signal("cmp_exp"), reached("cmp_exp", L + 1))
            s.do(nc.vector.tensor_reduce(CSUM, c8, AX.X, ALU.add))
            s.do(nc.vector.reciprocal(CSUM, CSUM))
            s.do(nc.vector.tensor_tensor(c8, c8, bc(CSUM.unsqueeze(2), [P, 8, 32]), ALU.mult))
            s.after(nc.vector.tensor_tensor(CS, CS, bc(COK.unsqueeze(2), [P, T, 4, 32]), ALU.mult).then_inc(signal("cmp_probs"), 1), "cmp_probs")
            g3 = GATES.rearrange("p (t h k) -> p t h k", t=T, k=3)
            s.eng.wait_ge(signal("cmp_out"), reached("cmp_out", L + 1))
            s.after(nc.vector.tensor_tensor(MIX[:, :, 0:256].rearrange("p t (h d) -> p t h d", h=4),
                                           PS[:, 7, :].rearrange("p (t h d) -> p t h d", t=T, h=4),
                                           bc(g3[:, :, :, 0:1], [P, T, 4, HD]), ALU.mult).then_inc(signal("cmp_done"), 1), "cmp_done")
            for t in range(T):
                n = n0 + t
                attn_softmax_dve(s, n, t, 8, HD ** -0.5, CB[:, t, 0:(t + 1) * P])
                s.do(nc.vector.tensor_tensor(
                    RG8.rearrange("p (a k b) -> p a k b", a=2, k=2), RDEN.rearrange("p (a k b) -> p a k b", a=2, k=2),
                    GATES[:, 12 * t:12 * t + 12].rearrange("p (hh hp k) -> p hp k hh", hh=2, hp=2)[:, :, 1:3, :],
                    ALU.mult))
                s.eng.wait_ge(sem("at_out"), n + 1)
                s.after(nc.vector.tensor_tensor(O8, PS[:, 0, :].rearrange("p (m d) -> p m d", m=8),
                                               bc(RG8.unsqueeze(2), [P, 8, HD]), ALU.mult).then_inc(sem("nsa_out"), 1), "nsa_out")
                mv = heads2(MIX[:, t, 0:256], HD)
                for kind in range(2):
                    s.do(nc.vector.tensor_tensor(mv, mv, O8.rearrange("p (hp k hh) d -> p hp k hh d", hp=2, k=2)
                                                 [:, :, kind], ALU.add))
            for t in range(T):
                attn_softmax_dve(s, n0 + 2 + t, t, 8, 32 ** -0.5, CB[:, t, 0:(t + 1) * P], LAMC[:, L:L + 1])

        GE = [view(a, 8 * S).rearrange("p (l s) -> p l s", l=8) for a in (12464, 14512)]
        MASKED = view(16560, 8 * P)
        AA = [view(17584 + 128 * i, P) for i in range(2)]
        ACR = [view(17840 + 128 * i, P) for i in range(2)]
        LOGF = view(18096, 3 * S).rearrange("p (f s) -> p f s", f=3)
        BSUM = view(18864, S)
        GLT, GLT2 = view(19120, S), view(19376, S)
        FAM = ((9, 10, GV0, (0, 1, 2, 3), 32, 512), (11, 13, RI0, (0, 1), 64, 768), (12, 14, RI0, (2, 3), 64, 768))
        UNITS = [(f, h, t) for f in range(3) for h in FAM[f][3] for t in range(T)]

        def gla_pe(pe, L):
            pe.wait_ge(sem("m_TT"), 3 * L + 3)
            nc.tensor.matmul(PS[:, 5, 0:S], WG2[0:16, L * P:(L + 1) * P], TT[0:16, 15, :], start=True, stop=True)\
                .then_inc(sem("gla_z"), 1)

            def out(u):
                f, h, t = UNITS[u]
                v0 = FAM[f][2] + HD * h
                pe.wait_ge(sem("gla_A"), 16 * L + u + 1)
                dst = PS[:, 6 if f == 0 else 7, (4 * t + h) * HD:(4 * t + h + 1) * HD]
                last = nc.tensor.matmul(dst, AA[u % 2], U2[:, t, v0:v0 + HD], start=True, stop=t == 0)
                if t == 1:
                    pe.wait_ge(sem("gla_cross_out"), 8 * L + u // 2 + 1)
                    last = nc.tensor.matmul(dst, ACR[u // 2 % 2], U2[:, 0, v0:v0 + HD], start=False, stop=True)
                last.then_inc(sem("gla_out"), 1)

            for u, (f, h, t) in enumerate(UNITS):
                w = FAM[f][4]
                r0 = (w * h) % P
                r, tok, b = slice(r0, r0 + w), slice(t * P, (t + 1) * P), 2 * (u % 2)
                pe.wait_ge(sem("gla_GE"), 3 * L + f + 1)
                for l in range(LEVELS):
                    nc.tensor.matmul(PS[:, b + l // 4, (l % 4) * P:(l % 4 + 1) * P], GE[f % 2][r, l, tok],
                                     GE[f % 2][r, l, tok], start=True, stop=True)
                last = nc.tensor.matmul(PS[:, b + 1, 3 * P:4 * P], TT[r, FAM[f][1], tok], TT[r, FAM[f][0], tok],
                                        start=True, stop=True)
                if t == 1:
                    last = nc.tensor.matmul(PS[:, 4, (u // 2 % 2) * P:(u // 2 % 2 + 1) * P], GE[f % 2][r, 7, 0:P],
                                            GE[f % 2][r, 7, P:S], start=True, stop=True)
                last.then_inc(sem("gla_prod"), 1)
                if u:
                    out(u - 1)
            out(15)

        def gla_act(s, L):
            s.eng.wait_ge(signal("gla_zb"), reached("gla_zb", L + 1))
            s.do(nc.scalar.activation(GLT2, GLT, ACT.Abs))
            s.do(nc.scalar.activation(GLT2, GLT2, ACT.Exp, scale=-1.0))
            s.after(nc.scalar.activation(GLT2, GLT2, ACT.Ln, bias=1.0).then_inc(signal("gla_ln"), 1), "gla_ln")
            rf = TT[:, 13:15, :]
            s.do(nc.scalar.activation(LOGF[:, 1:3, :], rf, ACT.Sigmoid))
            s.after(nc.scalar.activation(rf, rf, ACT.Sigmoid, scale=-1.0).then_inc(signal("hg_sig"), 1), "hg_sig")
            s.eng.wait_ge(signal("hg_f"), reached("hg_f", L + 1))
            s.after(nc.scalar.activation(LOGF[:, 1:3, :], LOGF[:, 1:3, :], ACT.Ln).then_inc(signal("hg_ln"), 1), "hg_ln")
            cross = 0
            for f in range(3):
                s.eng.wait_ge(sem("gla_gaps"), 3 * L + f + 1)
                s.after(nc.scalar.activation(GE[f % 2], GE[f % 2], ACT.Exp).then_inc(sem("gla_exp"), 1), "gla_exp")
                for u, (ff, h, t) in enumerate(UNITS):
                    if ff == f and t == 1:
                        s.eng.wait_ge(sem("gla_prod"), 16 * L + u + 1)
                        s.after(nc.scalar.activation(ACR[cross % 2], PS[:, 4, (cross % 2) * P:(cross % 2 + 1) * P],
                                                    ACT.Copy).then_inc(sem("gla_cross_out"), 1), "gla_cross_out")
                        cross += 1
            s.eng.wait_ge(sem("gla_out"), 16 * L + 16)
            for b, c in ((6, 512), (7, 768)):
                s.do(nc.scalar.activation(MIX[:, :, c:c + 256], PS[:, b, :].rearrange("p (t c) -> p t c", t=T), ACT.Copy))
            for t in range(T):
                ins = nc.scalar.activation(view(12464, T * 768).rearrange("p (t c) -> p t c", t=T)[:, t, :],
                                           MIX[:, t, 256:D], ACT.Square)
                if t == 0:
                    s.do(ins)
                else:
                    s.after(ins.then_inc(signal("m_osq"), 1), "m_osq")
            s.eng.wait_ge(signal("m_oms"), reached("m_oms", L + 1))
            s.after(nc.scalar.activation(OST, OST, ACT.Sqrt).then_inc(signal("m_oroot"), 1), "m_oroot")

        def gla_dve(s, L):
            s.eng.wait_ge(sem("gla_z"), L + 1)
            s.after(nc.vector.tensor_scalar(GLT, PS[:, 5, 0:S], GLAB[:, L:L + 1], None, ALU.add).then_inc(signal("gla_zb"), 1), "gla_zb")
            s.do(nc.vector.tensor_scalar(TT[:, 9, :], TT[:, 9, :], 32 ** -0.5, None, ALU.mult))
            s.eng.wait_ge(signal("gla_ln"), reached("gla_ln", L + 1))
            s.do(nc.vector.scalar_tensor_tensor(LOGF[:, 0, :], GLT, 0.0, GLT2, ALU.min, ALU.subtract))
            s.do(nc.vector.tensor_scalar(LOGF[:, 0, :], LOGF[:, 0, :], 1.0 / 16, None, ALU.mult))
            s.eng.wait_ge(signal("hg_sig"), reached("hg_sig", L + 1))
            for i in range(2):
                lb, one = LBC[:, 4 * i + L:4 * i + L + 1], LBC[:, 4 * i + 2 + L:4 * i + 3 + L]
                s.do(nc.vector.tensor_scalar(LOGF[:, 1 + i, :], LOGF[:, 1 + i, :], one, lb, ALU.mult, ALU.add))
                s.do(nc.vector.tensor_scalar(TT[:, 13 + i, :], TT[:, 13 + i, :], one, None, ALU.mult))
            s.after(nc.vector.tensor_scalar(LOGF[:, 1:3, :], LOGF[:, 1:3, :], 2.0 ** -63, None, ALU.max).then_inc(signal("hg_f"), 1), "hg_f")
            s.eng.wait_ge(signal("hg_ln"), reached("hg_ln", L + 1))

            def factors(f):
                if f == 2:
                    s.eng.wait_ge(sem("gla_prod"), 16 * L + 8)
                for t in range(T):
                    s.do(nc.vector.tensor_tensor_scan(BSUM[:, t * P:(t + 1) * P], ONES, LOGF[:, f, t * P:(t + 1) * P],
                                                      0.0, ALU.mult, ALU.add))
                for l in range(8):
                    n = 1 << l
                    b = BSUM.rearrange("p (b two n) -> p b two n", two=2, n=n)
                    e = GE[f % 2][:, l, :].rearrange("p (b two n) -> p b two n", two=2, n=n)
                    nb = S // (2 * n)
                    border = bc(b[:, :, 0, n - 1:n], [P, nb, n])
                    s.do(nc.vector.tensor_tensor(e[:, :, 0, :], border, b[:, :, 0, :], ALU.subtract))
                    if l < 7:
                        s.do(nc.vector.tensor_tensor(e[:, :, 1, :], b[:, :, 1, :], border, ALU.subtract))
                    else:
                        s.after(nc.vector.tensor_copy(e[:, :, 1, :], b[:, :, 1, :]).then_inc(sem("gla_gaps"), 1), "gla_gaps")
                s.eng.wait_ge(sem("gla_exp"), 3 * L + f + 1)
                for l in range(8):
                    n = 1 << l
                    e = GE[f % 2][:, l, :].rearrange("p (b two n) -> p b two n", two=2, n=n)
                    q, k = [TT[:, FAM[f][i], :].rearrange("p (b two n) -> p b two n", two=2, n=n) for i in range(2)]
                    s.do(nc.vector.tensor_tensor(e[:, :, 0, :], e[:, :, 0, :], k[:, :, 0, :], ALU.mult))
                    ins = nc.vector.tensor_tensor(e[:, :, 1, :], e[:, :, 1, :], q[:, :, 1, :], ALU.mult)
                    if l < 7:
                        s.do(ins)
                    else:
                        s.after(ins.then_inc(sem("gla_GE"), 1), "gla_GE")

            for f in range(3):
                factors(f)
                for u, (ff, h, t) in enumerate(UNITS):
                    if ff != f:
                        continue
                    s.eng.wait_ge(sem("gla_prod"), 16 * L + u + 1)
                    if u >= 2:
                        s.eng.wait_ge(sem("gla_out"), 16 * L + u - 1)
                    s.do(nc.vector.tensor_tensor(MASKED, banks(2 * (u % 2), 2), mt_t[:, :], ALU.mult))
                    s.after(nc.vector.tensor_reduce(AA[u % 2], MASKED.rearrange("p (l c) -> p c l", l=8), AX.X, ALU.add).then_inc(sem("gla_A"), 1), "gla_A")
            s.eng.wait_ge(signal("m_osq"), reached("m_osq", L + 1))
            s.do(nc.vector.tensor_reduce(OST, view(12464, T * 768).rearrange("p (g d) -> p g d", d=HD), AX.X, ALU.add))
            s.after(nc.vector.tensor_scalar(OST, OST, 1.0 / HD, EPS, ALU.mult, ALU.add).then_inc(signal("m_oms"), 1), "m_oms")
            s.eng.wait_ge(signal("m_oroot"), reached("m_oroot", L + 1))
            s.do(nc.vector.reciprocal(OST, OST))
            for t in range(T):
                o = MIX[:, t, 256:D].rearrange("p (g d) -> p g d", d=HD)
                s.do(nc.vector.tensor_tensor(o, o, bc(OST[:, 12 * t:12 * t + 12].unsqueeze(2), [P, 12, HD]), ALU.mult))
                o = MIX[:, t, 256:D].rearrange("p (m h d) -> p m h d", m=3, h=4)
                s.do(nc.vector.tensor_tensor(o, o, bc(G12[:, L].unsqueeze(2), [P, 3, 4, HD]), ALU.mult))
            s.do(nc.vector.tensor_tensor(MIX[:, :, 512:768], MIX[:, :, 512:768], U2[:, :, GOG0:GOG0 + 256], ALU.mult))
            s.after(nc.vector.tensor_tensor(MIX[:, :, 768:D], MIX[:, :, 768:D], U2[:, :, ROG0:ROG0 + 256], ALU.mult).then_inc(sem("mix_ready"), 1), "mix_ready")

        HFT = view(0, (FF // P) * S).rearrange("p (k s) -> p k s", s=S)
        SGF = [view(7168 + 1024 * i, 1024).rearrange("p (t c) -> p t c", t=T) for i in range(2)]
        HTOK = [view(9216 + 1024 * i, 1024).rearrange("p (t c) -> p t c", t=T) for i in range(2)]

        def ffn_pe(pe, L):
            gs = group("ffn", L)

            def turn(f):
                pe.wait_ge(sem("gemm_out_dve"), evacuated(gs[2 * f + 1])[1])
                if f >= 2:
                    pe.wait_ge(sem("ffn_HT"), f - 1)
                transposes([(lambda t, j=j: HTOK[f % 2][:, t, j * P:(j + 1) * P]) for j in range(4)], 4 + 2 * (f % 2))\
                    .then_inc(sem("ffn_T"), 1)

            for f in range(7):
                gemm(pe, gs[2 * f], ht_lhs)
                gemm(pe, gs[2 * f + 1], ht_lhs)
                if f:
                    turn(f - 1)
            turn(6)
            pe.wait_ge(sem("ffn_HT"), 7)
            for i in range(14):
                n = DOWN[L] + i
                landed(pe, n)
                w = half_view(n, (2, D))
                for k in range(2):
                    for t in range(T):
                        for dh in range(2):
                            last = nc.tensor.matmul(PS[:, 2 * t + dh, :], HFT[:, 2 * i + k, t * P:(t + 1) * P],
                                                    w[:, k, 512 * dh:512 * dh + 512], start=i + k == 0,
                                                    stop=i == 13 and k == 1)
                last.then_inc(sem("weights_used"), 1)

        def ffn_act(s, L):
            gs = group("ffn", L)

            def back(f):
                s.eng.wait_ge(sem("ffn_T"), f + 1)
                b = 4 + 2 * (f % 2)
                s.after(nc.scalar.activation(HFT[:, 4 * f:4 * f + 4, :], banks(b, 2).rearrange("p (k s) -> p k s", k=4),
                                            ACT.Copy).then_inc(sem("ffn_HT"), 1), "ffn_HT")

            for f in range(7):
                s.eng.wait_ge(sem("weights_used"), used(TILES[gs[2 * f]]["end"] - 1))
                if f >= 2:
                    s.eng.wait_ge(sem("gemm_out_dve"), evacuated(gs[2 * f - 3])[1])
                s.after(nc.scalar.activation(SGF[f % 2], acc(gs[2 * f]), ACT.Silu).then_inc(sem("gemm_out_act"), 1), "gemm_out_act")
                if f >= 2:
                    back(f - 2)
            back(5)
            back(6)

        def ffn_dve(s, L):
            gs = group("ffn", L)
            for f in range(7):
                g = gs[2 * f + 1]
                s.eng.wait_ge(sem("weights_used"), used(TILES[g]["end"] - 1))
                s.eng.wait_ge(sem("gemm_out_act"), evacuated(gs[2 * f])[1])
                if f >= 2:
                    s.eng.wait_ge(sem("ffn_T"), f - 1)
                s.after(nc.vector.tensor_tensor(HTOK[f % 2], SGF[f % 2], acc(g), ALU.mult).then_inc(sem("gemm_out_dve"), 1), "gemm_out_dve")
            s.eng.wait_ge(sem("weights_used"), used(DOWN[L] + 13))
            s.after(nc.vector.tensor_tensor(x_t[:, :], x_t[:, :], banks(0, 4), ALU.add).then_inc(sem("x_updated"), 1), "x_updated")

        PP = view(9216 + 2048, T * PLE).rearrange("p (t c) -> p t c", t=T)
        PPT = view(9216 + 2048 + 512, 2 * S).rearrange("p (k s) -> p k s", k=2)
        SGP = view(12464, T * D).rearrange("p (t c) -> p t c", t=T)
        TMP = view(14512, T * 512).rearrange("p (t c) -> p t c", t=T)

        def ple_pe(pe, L):
            pe.wait_ge(sem("ple_loaded"), 16 * (L + 1))
            transposes([(lambda t, j=j: PP[:, t, j * P:(j + 1) * P]) for j in range(2)], 4).then_inc(sem("ple_T"), 1)
            for g in group("pg", L):
                gemm(pe, g, ht_lhs)
            pe.wait_ge(sem("ple_pT"), L + 1)
            for g in group("pp", L):
                gemm(pe, g, lambda k, t: PPT[:, k, t * P:(t + 1) * P])

        def ple_act(s, L):
            s.eng.wait_ge(sem("ple_T"), L + 1)
            s.after(nc.scalar.activation(PPT, PS[:, 4, :].rearrange("p (k s) -> p k s", k=2), ACT.Copy).then_inc(sem("ple_pT"), 1), "ple_pT")
            for g in group("pg", L):
                d = TILES[g]
                s.eng.wait_ge(sem("weights_used"), used(d["end"] - 1))
                s.after(nc.scalar.activation(SGP[:, :, d["c0"]:d["c0"] + 512], acc(g), ACT.Sigmoid).then_inc(sem("gemm_out_act"), 1), "gemm_out_act")

        def ple_dve(s, L):
            s.eng.wait_ge(sem("gemm_out_act"), evacuated(group("pg", L)[-1])[1])
            for g in group("pp", L):
                d = TILES[g]
                c = slice(d["c0"], d["c0"] + 512)
                s.eng.wait_ge(sem("weights_used"), used(d["end"] - 1))
                s.after(nc.vector.tensor_tensor(TMP, SGP[:, :, c], acc(g), ALU.mult).then_inc(sem("gemm_out_dve"), 1), "gemm_out_dve")
                s.do(nc.vector.tensor_tensor(X[:, :, c], X[:, :, c], TMP, ALU.add))
            s.after(nc.vector.tensor_copy(SS[:, 0:1], SS[:, 0:1]).then_inc(sem("x_updated"), 1), "x_updated")

        SLOTS = 128
        PALL = view(0, T * NE * SLOTS).rearrange("p (t e s) -> p t e s", t=T, e=NE)
        WSEL = view(2048, T * NE * SLOTS).rearrange("p (t e s) -> p t e s", t=T, e=NE)
        PWT = view(4096, NE * S).rearrange("p (e s) -> p e s", e=NE)
        PWE = view(6144, S)
        XG = view(6400, KD * SLOTS).rearrange("p (k s) -> p k s", k=KD)
        HET = view(7424, (FF // P) * SLOTS).rearrange("p (k s) -> p k s", s=SLOTS)
        SGE = [view(11008 + 512 * i, 512) for i in range(2)]
        HE = [view(12032 + 512 * i, 512) for i in range(2)]
        YE = view(13056, D)
        LOGX = view(14080, T * 16).rearrange("p (t e) -> p t e", t=T)
        LW = view(14112, T * 16).rearrange("p (t e) -> p t e", t=T)
        RPL, TOP = view(14144, 16).rearrange("p (t e) -> p t e", t=T), view(14160, 16).rearrange("p (t e) -> p t e", t=T)
        MASK, EXPL, COMB, SLOT = [view(14176 + 16 * i, 16).rearrange("p (t e) -> p t e", t=T) for i in range(4)]
        ESUM, CNT = view(14240, 2), view(14242, 1)
        MTMP = view(14248, 16).rearrange("p (t e) -> p t e", t=T)
        cnt_i = sb("busiest_expert", 1, I32)
        IOTA = iota_t[:, :]

        def gate_tile(pe, r, e, j0, bank):
            for h in range(2):
                w = expert_half(pe, r, e, j0 + h, (4, 512))
                for k in range(4):
                    last = nc.tensor.matmul(PS[:, bank, :], XG[:, 4 * h + k, :], w[:, k, :],
                                            start=h + k == 0, stop=h == 1 and k == 3)
                last.then_inc(sem(("weights_used", "o_used")[r]), 1)

        def expert_half(eng, r, e, j, shape):
            n = MOE0 + j
            if r == 0:
                eng.wait_ge(sem(f"landed{n % RING}"), e * (16 * PER_EXPERT // RING) + LANDED[n])
            else:
                eng.wait_ge(sem(f"o_landed{n % RING}"), e * (16 * PER_EXPERT // RING) + 16 * (j // RING + 1))
            return half_view(n, shape)

        def expert_used(eng, r, e, j):
            if r == 0:
                eng.wait_ge(sem("weights_used"), e * PER_EXPERT + MOE0 + j)
            else:
                eng.wait_ge(sem("o_used"), e * PER_EXPERT + j)

        PASS = dict(placed=1, placedT=1, PWT=1, PWE=NE + 1, YE=NE + 1, gather=NE, XG=NE, scatter=NE + 1, added=NE + 1,
                    sg=7 * NE, h=7 * NE, T=7 * NE, HT=7 * NE)

        def ms(name):
            return sem("moe_" + name)

        def route_pe(pe):
            for t in range(T):
                for k in range(KD):
                    last = nc.tensor.matmul(PS[:, 4, t * NE:(t + 1) * NE], ht_lhs(k, t), ROUTER[:, k, :],
                                            start=k == 0, stop=k == KD - 1)
            last.then_inc(sem("moe_logits"), 1)
            pe.wait_ge(sem("moe_mask"), 1)
            nc.tensor.matmul(PS[:, 5, 0:NE], SUPPER, MASK[:, 0, :], start=True, stop=True)
            nc.tensor.matmul(PS[:, 5, NE:2 * NE], ONES, MASK[:, 0, :], start=True, stop=False)
            nc.tensor.matmul(PS[:, 5, NE:2 * NE], SUPPER, MASK[:, 1, :], start=False, stop=True)
            nc.tensor.matmul(PS[:, 5, 2 * NE:3 * NE], ONES, MASK[:, 0, :], start=True, stop=False)
            nc.tensor.matmul(PS[:, 5, 2 * NE:3 * NE], ONES, MASK[:, 1, :], start=False, stop=True)\
                .then_inc(sem("moe_places"), 1)

        def route_dve(s):
            s.do(nc.vector.memset(view(14080, 192), NONCAUSAL))
            s.eng.wait_ge(sem("moe_logits"), 1)
            s.do(nc.vector.tensor_copy(LOGX[:, :, 0:NE], PS[:, 4, 0:2 * NE].rearrange("p (t e) -> p t e", t=T)))
            for t in range(T):
                s.do(nc.vector.max(TOP[:, t, :], LOGX[:, t, 0:NE]))
            s.do(nc.vector.tensor_copy(RPL[:, :, 0:2], TOP[:, :, 0:2]))
            for t in range(T):
                s.do(nc.vector.match_replace(out=LW[:, t, 0:14], in_to_replace=RPL[:, t, :],
                                             in_values=LOGX[:, t, 0:14], imm_value=TAKEN))
            s.after(nc.vector.tensor_scalar(MASK, LW[:, :, 0:NE], TAKEN, None, ALU.is_equal).then_inc(sem("moe_mask"), 1), "moe_mask")
            s.after(nc.vector.tensor_tensor(EXPL, LOGX[:, :, 0:NE], bc(TOP[:, :, 0:1], [P, T, NE]), ALU.subtract).then_inc(sem("moe_shifted"), 1), "moe_shifted")
            s.eng.wait_ge(sem("moe_exp"), 1)
            s.do(nc.vector.tensor_tensor(EXPL, EXPL, MASK, ALU.mult))
            s.do(nc.vector.tensor_reduce(ESUM, EXPL, AX.X, ALU.add))
            s.do(nc.vector.reciprocal(ESUM, ESUM))
            s.do(nc.vector.tensor_tensor(COMB, EXPL, bc(ESUM.unsqueeze(2), [P, T, NE]), ALU.mult))
            s.eng.wait_ge(sem("moe_places"), 1)
            s.do(nc.vector.scalar_tensor_tensor(SLOT, PS[:, 5, 0:2 * NE].rearrange("p (t e) -> p t e", t=T), 1.0, MASK,
                                                ALU.add, ALU.mult))
            s.do(nc.vector.tensor_scalar(SLOT, SLOT, -1.0, None, ALU.add))
            s.do(nc.vector.tensor_reduce(CNT, PS[:, 5, 2 * NE:3 * NE], AX.X, ALU.max))
            s.after(nc.vector.tensor_copy(cnt_i[:, :], CNT).then_inc(sem("moe_count"), 1), "moe_count")

        def pass_dve(s, r):
            if r:
                s.do(nc.vector.tensor_scalar(SLOT, SLOT, -float(SLOTS), None, ALU.add))
            for t in range(T):
                s.do(nc.vector.tensor_tensor(PALL[:, t], bc(IOTA.unsqueeze(1), [P, NE, SLOTS]),
                                             bc(SLOT[:, t].unsqueeze(2), [P, NE, SLOTS]), ALU.is_equal))
                ins = nc.vector.tensor_tensor(WSEL[:, t], PALL[:, t], bc(COMB[:, t].unsqueeze(2), [P, NE, SLOTS]),
                                              ALU.mult)
                if t == 0:
                    s.do(ins)
            ins.then_inc(ms("placed"), 1)
            nc.vector.memset(PWE, 0.0).then_inc(ms("PWE"), 1)
            nc.vector.memset(YE, 0.0).then_inc(ms("YE"), 1)
            s.eng.wait_ge(ms("YE"), 1 + r * PASS["YE"])

        def pass_pe(pe, r):
            pe.wait_ge(ms("placed"), 1 + r * PASS["placed"])
            for e in range(NE):
                for t in range(T):
                    c = ((e % 2) * T + t) * SLOTS
                    last = nc.tensor.transpose(PS[:, 4 + e // 2, c:c + SLOTS], WSEL[:, t, e, :], IDENT)
            last.then_inc(ms("placedT"), 1)
            pe.wait_ge(ms("PWT"), 1 + r * PASS["PWT"])

            def scatter(e):
                pe.wait_ge(ms("PWE"), e + 1 + r * PASS["PWE"])
                for t, b in ((0, 6), (1, 2)):
                    for dh in range(2):
                        last = nc.tensor.matmul(PS[:, b + dh, :], PWE[:, t * P:(t + 1) * P],
                                                YE[:, 512 * dh:512 * dh + 512], start=True, stop=True)
                last.then_inc(ms("scatter"), 1)

            with pe.Fori(0, NE) as e:
                pe.wait_ge(ms("YE"), e + 1 + r * PASS["YE"])
                for k in range(KD):
                    for t in range(T):
                        last = nc.tensor.matmul(PS[:, 4 + k // 4, (k % 4) * SLOTS:(k % 4 + 1) * SLOTS],
                                                XN[:, t, k * P:(k + 1) * P],
                                                PALL[:, t, bass.ds(e, 1), :].rearrange("p a s -> p (a s)"),
                                                start=t == 0, stop=t == 1)
                last.then_inc(ms("gather"), 1)
                scatter(e)

                def turn(f):
                    pe.wait_ge(ms("h"), e * 7 + (f + 1) + r * PASS["h"])
                    if f >= 2:
                        pe.wait_ge(ms("HT"), e * 7 + (f - 1) + r * PASS["HT"])
                    for j in range(4):
                        last = nc.tensor.transpose(PS[:, 6 + f % 2, j * SLOTS:(j + 1) * SLOTS],
                                                   HE[f % 2][:, j * P:(j + 1) * P], IDENT)
                    last.then_inc(ms("T"), 1)

                for f in range(7):
                    if f == 0:
                        pe.wait_ge(ms("XG"), e + 1 + r * PASS["XG"])
                    if f >= 2:
                        pe.wait_ge(ms("sg"), e * 7 + (f - 1) + r * PASS["sg"])
                    gate_tile(pe, r, e, 4 * f, f % 2)
                    if f == 0:
                        pe.wait_ge(ms("added"), e + 1 + r * PASS["added"])
                    if f >= 2:
                        pe.wait_ge(ms("h"), e * 7 + (f - 1) + r * PASS["h"])
                    gate_tile(pe, r, e, 4 * f + 2, 2 + f % 2)
                    if f:
                        turn(f - 1)
                turn(6)
                pe.wait_ge(ms("HT"), e * 7 + 7 + r * PASS["HT"])
                for i in range(14):
                    w = expert_half(pe, r, e, 28 + i, (2, D))
                    for k in range(2):
                        for dh in range(2):
                            last = nc.tensor.matmul(PS[:, 4 + dh, :], HET[:, 2 * i + k, :],
                                                    w[:, k, 512 * dh:512 * dh + 512], start=i + k == 0,
                                                    stop=i == 13 and k == 1)
                    last.then_inc(sem(("weights_used", "o_used")[r]), 1)
            pe.wait_ge(ms("YE"), NE + 1 + r * PASS["YE"])
            scatter(NE)

        def pass_act(act, r):
            act.wait_ge(ms("placedT"), 1 + r * PASS["placedT"])
            nc.scalar.activation(PWT, banks(4, 4).rearrange("p (e s) -> p e s", e=NE), ACT.Copy)\
                .then_inc(ms("PWT"), 1)
            act.wait_ge(ms("PWT"), 1 + r * PASS["PWT"])
            with act.Fori(0, NE) as e:
                act.wait_ge(ms("XG"), e + 1 + r * PASS["XG"])
                act.wait_ge(ms("scatter"), e + 1 + r * PASS["scatter"])
                nc.scalar.activation(PWE, PWT[:, bass.ds(e, 1), :].rearrange("p a s -> p (a s)"), ACT.Copy)\
                    .then_inc(ms("PWE"), 1)

                def back(f):
                    act.wait_ge(ms("T"), e * 7 + (f + 1) + r * PASS["T"])
                    nc.scalar.activation(HET[:, 4 * f:4 * f + 4, :],
                                         PS[:, 6 + f % 2, :].rearrange("p (k s) -> p k s", k=4), ACT.Copy)\
                        .then_inc(ms("HT"), 1)

                for f in range(7):
                    expert_used(act, r, e, 4 * f + 2)
                    if f >= 2:
                        act.wait_ge(ms("h"), e * 7 + (f - 1) + r * PASS["h"])
                    nc.scalar.activation(SGE[f % 2], PS[:, f % 2, :], ACT.Silu).then_inc(ms("sg"), 1)
                    if f >= 1:
                        back(f - 1)
                back(6)
                expert_used(act, r, e, PER_EXPERT)
                nc.scalar.activation(YE, banks(4, 2), ACT.Copy).then_inc(ms("YE"), 1)

        def pass_loop_dve(s, r):
            dve = s.eng

            def add(e):
                dve.wait_ge(ms("scatter"), e + 1 + r * PASS["scatter"])
                nc.vector.tensor_tensor(X[:, 0, :], X[:, 0, :], banks(6, 2), ALU.add)
                return nc.vector.tensor_tensor(X[:, 1, :], X[:, 1, :], banks(2, 2), ALU.add)

            with dve.Fori(0, NE) as e:
                dve.wait_ge(ms("gather"), e + 1 + r * PASS["gather"])
                nc.vector.tensor_tensor(XG, banks(4, 2).rearrange("p (k s) -> p k s", k=KD),
                                        bc(GAINC[:, 40:48].unsqueeze(2), [P, KD, SLOTS]), ALU.mult)\
                    .then_inc(ms("XG"), 1)
                add(e).then_inc(ms("added"), 1)
                dve.wait_ge(ms("added"), e + 1 + r * PASS["added"])
                for f in range(7):
                    expert_used(dve, r, e, 4 * f + 4)
                    dve.wait_ge(ms("sg"), e * 7 + (f + 1) + r * PASS["sg"])
                    if f >= 2:
                        dve.wait_ge(ms("T"), e * 7 + (f - 1) + r * PASS["T"])
                    nc.vector.tensor_tensor(HE[f % 2], SGE[f % 2], PS[:, 2 + f % 2, :], ALU.mult)\
                        .then_inc(ms("h"), 1)
            add(NE).then_inc(ms("added"), 1)
            dve.wait_ge(ms("added"), NE + 1 + r * PASS["added"])

        def pass_loads(sp, r):
            def src(name, k0, nk, c0, n):
                return A[name].rearrange("x e (k p) n -> p (x e k) n", p=P), k0, nk, c0, n

            with sp.Fori(0, NE) as e:
                for j in range(PER_EXPERT):
                    if j < 28:
                        f, q = divmod(j, 4)
                        v = A[("moe_w_gate_2", "moe_w_up_2")[q // 2]].rearrange("x e (k p) n -> p (x e k) n", p=P)
                        source = v[:, bass.ds(e * KD + 4 * (q % 2), 4), 512 * f:512 * f + 512]
                        dst = half_view(MOE0 + j, (4, 512))
                    else:
                        v = A["moe_w_down_2"].rearrange("x e (k p) n -> p (x e k) n", p=P)
                        source = v[:, bass.ds(e * (FF // P) + 2 * (j - 28), 2), :]
                        dst = half_view(MOE0 + j, (2, D))
                    if r == 0:
                        sp.wait_ge(sem("weights_used"), e * PER_EXPERT + (MOE0 + j - RING + 1))
                        sp.dma_start(dst, source).then_inc(sem(f"landed{(MOE0 + j) % RING}"), 16)
                    else:
                        if j < RING:
                            sp.wait_ge(ms("scatter"), e + 1 + 1 * PASS["scatter"])
                        else:
                            sp.wait_ge(sem("o_used"), e * PER_EXPERT + (j - RING + 1))
                        sp.dma_start(dst, source).then_inc(sem(f"o_landed{(MOE0 + j) % RING}"), 16)
            if r:
                sp.wait_ge(ms("scatter"), NE + 1 + r * PASS["scatter"])

        def overflow(eng, body):
            eng.wait_ge(sem("moe_count"), 1)
            count = eng.value_load(cnt_i[0:1, 0:1], min_val=0, max_val=S)
            with eng.If(count > OVER):
                body()

        PSTAGE = view(0, 3 * P).rearrange("p (a c) -> p a c", a=3)
        LBT = [view(512 + 16 * i, 4) for i in range(4)]

        def rows_of(a):
            return a.rearrange("a b -> (a b)") if len(a.shape) == 2 else a.rearrange("a b c -> (a b c)")

        PARAMS = [(R_GDN, A["gdn_norm_gain"]), (R_KI, A["idx_k_gain"]), (R_DT, A["dt_bias"]), (R_EA, A["a_log"]),
                  (R_NSA, A["nsa_qk_gain_2"]), (R_DQK, A["diff_qk_gain_2"]), (R_LAM, A["diff_lambda_2"]),
                  (R_DN, A["diff_norm_2"]), (R_GLAN, A["gla_norm_2"]), (R_HGN, A["hgrn_norm_2"])]

        def load_params(eng):
            n = 0
            eng.dma_start(pos_t[:, :], A["positions"].rearrange("b (t p) -> p (b t)", p=P),
                          allow_slow_non_contiguous=True).then_inc(sem("params"), 16)
            n += 1
            for i, name in enumerate(("norm_gain", "norm_attn_2", "norm_ffn_2", "ple_norm_2")):
                eng.dma_start(PSTAGE[16 * i:16 * i + 16, 0, :], A[name].rearrange("l (k p) -> (l k) p", p=P))\
                    .then_inc(sem("params"), 16)
                n += 1
            for L in range(DEPTH):
                eng.dma_start(PSTAGE[0:96, 1 + L, :], A["conv_w"][L].rearrange("k (c p) -> (k c) p", p=P))\
                    .then_inc(sem("params"), 16)
                n += 1
            for dst, src in PARAMS:
                eng.dma_start(dst, rows_of(src).partition_broadcast(P)).then_inc(sem("params"), 16)
                n += 1
            for L in range(DEPTH):
                eng.dma_start(WG2[0:16, L * P:(L + 1) * P], A["gla_w_gate2_2"][L]).then_inc(sem("params"), 16)
                eng.dma_start(GLAB[:, L:L + 1], A["gla_b_gate_2"][L:L + 1, :].rearrange("a p -> p a"),
                              allow_slow_non_contiguous=True).then_inc(sem("params"), 16)
                n += 2
                for j in range(2):
                    eng.dma_start(CMPPOS[64 * j:64 * j + 64, L * CMP_L:(L + 1) * CMP_L],
                                  A["nsa_cmp_pos_2"][L, j].rearrange("l d -> d l"),
                                  allow_slow_non_contiguous=True).then_inc(sem("params"), 16)
                    eng.dma_start(W2[:, L, j], A["nsa_cmp_w2_2"][L, j].rearrange("(k p) n -> p k n", p=P))\
                        .then_inc(sem("params"), 16)
                    n += 2
                eng.dma_start(LBC[:, L:L + 5:4], A["hgrn_lb_logits_2"][L].rearrange("(i p) -> p i", p=P),
                              allow_slow_non_contiguous=True).then_inc(sem("params"), 16)
                n += 1
            eng.dma_start(ROUTER, kview(A["moe_router_2"][0])).then_inc(sem("params"), 16)
            return n + 1

        N_PARAMS = 1 + 4 + 2 + len(PARAMS) + 14 + 1

        def setup_pool(s):
            g = nc.gpsimd

            def triangle(dst, fill_where_not, base, step, cm, op=ALU.is_ge):
                s.do(g.affine_select(out=dst, in_=dst, compare_op=op, fill=fill_where_not, base=base,
                                     pattern=step, channel_multiplier=cm))

            s.do(g.memset(IDENT, 0.0))
            s.after(g.affine_select(out=IDENT, in_=IDENT, compare_op=ALU.not_equal, fill=1.0, base=0,
                                   pattern=[[-1, P]], channel_multiplier=1).then_inc(sem("ident_ready"), 1), "ident_ready")
            s.do(g.memset(ONES, 1.0))
            s.do(g.memset(EPS1, EPS))
            s.do(g.memset(EPSK, EPS * DK))
            for i in range(ROT // 2):
                s.do(g.memset(FREQ[:, i:i + 1], float(np.float32(500000.0) ** np.float32(-2 * i / ROT))))
            for i in range(IDX_ROT // 2):
                s.do(g.memset(FREQ[:, ROT // 2 + i:ROT // 2 + i + 1],
                              float(np.float32(500000.0) ** np.float32(-2 * i / IDX_ROT))))
            for dst, base, step, cm in ((UPPER, 0, 1, -1), (SUPPER, -1, 1, -1), (SLOWER, -1, -1, 1)):
                s.do(g.memset(dst, 1.0))
                triangle(dst, 0.0, base, [[step, P]], cm)
            for l in range(LEVELS):
                n = 1 << l
                nb = P // (2 * n)
                low = MS[:, l, :].rearrange("p (b two n) -> p b two n", two=2, n=n)
                up = MT[:, l, :].rearrange("p (b two n) -> p b two n", two=2, n=n)
                s.do(g.memset(low[:, :, 0, :], 1.0))
                s.do(g.memset(low[:, :, 1, :], 0.0))
                s.do(g.memset(up[:, :, 0, :], 0.0))
                s.do(g.memset(up[:, :, 1, :], 1.0))
                pat, neg = [[-2 * n, nb], [0, 2 * n]], [[2 * n, nb], [0, 2 * n]]
                for dst, lo, hi in ((MS[:, l, :], n, 2 * n - 1), (MT[:, l, :], 0, n - 1)):
                    triangle(dst, 0.0, -lo, pat, 1)
                    triangle(dst, 0.0, hi, neg, -1)
            s.do(g.tensor_copy(MT[:, LEVELS, :], IDENT))
            for t in range(T):
                s.do(g.memset(CB[:, t, :], 0.0))
                triangle(CB[:, t, :], NEG, t * P, [[-1, S]], 1)
                s.do(g.memset(COK[:, t, :], 1.0))
                triangle(COK[:, t, :], 0.0, t * P - CMP_L + 1, [[-CMP_S, 32]], 1)
                s.do(g.memset(CBIAS[:, t, :], 0.0))
                triangle(CBIAS[:, t, :], NEG, t * P - CMP_L + 1, [[-CMP_S, 32]], 1)
            s.after(g.iota(IOTA, pattern=[[1, P]], base=0, channel_multiplier=0,
                          allow_small_or_imprecise_dtypes=True).then_inc(sem("consts_ready"), 1), "consts_ready")

        def setup_pe(pe):
            pe.wait_ge(sem("ident_ready"), 1)
            pe.wait_ge(sem("params"), 16 * N_PARAMS)
            nc.tensor.transpose(PS[:, 0, 0:64], PSTAGE[0:64, 0, :], IDENT[0:64, 0:64])
            for L in range(DEPTH):
                last = nc.tensor.transpose(PS[:, 0, 64 + 96 * L:160 + 96 * L], PSTAGE[0:96, 1 + L, :],
                                           IDENT[0:96, 0:96])
            last.then_inc(sem("param_cols_T"), 1)

        def setup_dve(s):
            s.eng.wait_ge(sem("params"), 16 * N_PARAMS)
            s.eng.wait_ge(sem("param_cols_T"), 1)
            s.after(nc.vector.tensor_copy(cols_t[:, :], PS[:, 0, 0:256]).then_inc(sem("params_ready"), 1), "params_ready")
            s.eng.wait_ge(sem("consts_ready"), 1)
            for L in range(DEPTH):
                lam = R_LAM[:, L * P:(L + 1) * P].rearrange("p (a b d) -> p a b d", a=2, b=2)
                s.do(nc.vector.tensor_tensor(LAMP.rearrange("p (a d) -> p a d", a=2), lam[:, :, 0, :], lam[:, :, 1, :],
                                             ALU.mult))
                s.after(nc.vector.tensor_reduce(LAMS, LAMP.rearrange("p (a d) -> p a d", a=2), AX.X, ALU.add).then_inc(sem("lam_sum"), 1), "lam_sum")
                s.eng.wait_ge(sem("lam_exp"), L + 1)
                s.do(nc.vector.tensor_tensor(LAMC[:, L:L + 1], LAMS[:, 0:1], LAMS[:, 1:2], ALU.subtract))
                s.do(nc.vector.tensor_scalar(LAMC[:, L:L + 1], LAMC[:, L:L + 1], lam_init(L), None, ALU.add))
                row = slice(L * HD, (L + 1) * HD)
                s.do(nc.vector.tensor_scalar(G12[:, L, 0, :], R_DN[:, row], 1.0 - lam_init(L), None, ALU.mult))
                s.do(nc.vector.tensor_copy(G12[:, L, 1, :], R_GLAN[:, row]))
                s.do(nc.vector.tensor_copy(G12[:, L, 2, :], R_HGN[:, row]))
            lb = LBC.rearrange("p (i k) -> p i k", i=2)
            m, e0, e1, ss = [v[:, 0:2] for v in LBT]
            s.do(nc.vector.tensor_tensor(m, lb[:, :, 0], lb[:, :, 1], ALU.max))
            s.do(nc.vector.tensor_tensor(e0, lb[:, :, 0], m, ALU.subtract))
            s.after(nc.vector.tensor_tensor(e1, lb[:, :, 1], m, ALU.subtract).then_inc(sem("lb_shifted"), 1), "lb_shifted")
            s.eng.wait_ge(sem("lb_exp"), 1)
            s.do(nc.vector.tensor_tensor(ss, e0, e1, ALU.add))
            s.do(nc.vector.reciprocal(ss, ss))
            s.do(nc.vector.memset(lb[:, :, 0], 0.0))
            s.do(nc.vector.tensor_tensor(lb[:, :, 1], e1, ss, ALU.mult))
            s.do(nc.vector.tensor_scalar(lb[:, :, 2:4], lb[:, :, 0:2], -1.0, 1.0, ALU.mult, ALU.add))

        def setup_act(s):
            s.eng.wait_ge(sem("params"), 16 * N_PARAMS)
            s.do(nc.scalar.activation(R_EA, R_EA, ACT.Exp))
            for L in range(DEPTH):
                s.eng.wait_ge(sem("lam_sum"), L + 1)
                s.after(nc.scalar.activation(LAMS, LAMS, ACT.Exp).then_inc(sem("lam_exp"), 1), "lam_exp")
            s.eng.wait_ge(sem("lb_shifted"), 1)
            s.do(nc.scalar.activation(LBT[1][:, 0:2], LBT[1][:, 0:2], ACT.Exp))
            s.after(nc.scalar.activation(LBT[2][:, 0:2], LBT[2][:, 0:2], ACT.Exp).then_inc(sem("lb_exp"), 1), "lb_exp")

        RFINAL = view(0, D)
        block = ctx.enter_context(nc.Block())

        @block.sync
        def _(sp):
            sp.dma_start(X, A["x"].rearrange("b (t p) d -> p (b t) d", p=P)).then_inc(sem("x_loaded"), 16)
            for n, load in enumerate(LOADS):
                if load is None:
                    if n == MOE0:
                        pass_loads(sp, 0)
                    if n == MOE0 + NE * PER_EXPERT - 1:
                        overflow(sp, lambda: pass_loads(sp, 1))
                    continue
                shape, parts = load
                if n >= RING:
                    sp.wait_ge(sem("weights_used"), n - RING + 1)
                for j, src in parts:
                    dst = half_view(n, shape)
                    if j is not None:
                        dst = dst[64 * j:64 * j + 64]
                    sp.dma_start(dst, src).then_inc(sem(f"landed{n % RING}"), 16)
            sp.wait_ge(sem("out_ready"), 1)
            sp.dma_start(out.rearrange("b (t p) d -> p (b t) d", p=P), X).then_inc(sem("out_written"), 16)
            sp.wait_ge(sem("out_written"), 16)

        @block.gpsimd
        def _(pool):
            s = Steps(pool, "pool")
            setup_pool(s)
            for L in range(DEPTH):
                s.fence()
                gdn_pool(s, L)
                s.fence()
                dsa_pool(s, L)
                s.fence()
            s.fence()
            pool.dma_start(RFINAL, A["final_gain"].partition_broadcast(P)).then_inc(sem("final_gain"), 16)
            s.fence()
            for L in range(DEPTH):
                for _ in range(4):
                    s.fence()
                pool.dma_start(PP, A["p_2"][L].rearrange("b (t p) c -> p (b t) c", p=P))\
                    .then_inc(sem("ple_loaded"), 16)
                s.fence()
            pool.wait_ge(sem("ple_loaded"), 16 * DEPTH)

        @block.scalar
        def _(act):
            s = Steps(act, "act")
            load_params(act)
            setup_act(s)
            trig_tables(None, s)
            n = at_n = 0
            for L in range(DEPTH):
                norm_act(s, n)
                n += 1
                proj1_act(s, L)
                s.fence()
                gdn_act(s, L)
                s.fence()
                dsa_act(s, L, at_n)
                at_n += T
                s.fence()
                gate_act(s, L)
                mix_act(s, L)
            s.fence()
            norm_act(s, n)
            n += 1
            s.fence()
            for L in range(DEPTH):
                norm_act(s, n)
                n += 1
                u_act(s, L)
                s.fence()
                mixers_act(s, L, at_n)
                at_n += 2 * T
                s.fence()
                gla_act(s, L)
                mix_act(s, DEPTH + L)
                norm_act(s, n)
                n += 1
                s.fence()
                if L % 2 == 0:
                    ffn_act(s, L)
                else:
                    s.eng.wait_ge(sem("moe_shifted"), 1)
                    s.after(nc.scalar.activation(EXPL, EXPL, ACT.Exp).then_inc(sem("moe_exp"), 1), "moe_exp")
                    pass_act(act, 0)
                    overflow(act, lambda: pass_act(act, 1))
                s.fence()
                norm_act(s, n)
                n += 1
                ple_act(s, L)
                s.fence()

        @block.vector
        def _(dve):
            s = Steps(dve, "dve")
            setup_dve(s)
            trig_tables(s, None)
            n = at_n = 0
            for L in range(DEPTH):
                norm_dve(s, n, GAINC[:, 8 * L:8 * L + 8])
                n += 1
                conv_dve(s, L)
                s.fence()
                gdn_dve(s, L)
                s.fence()
                dsa_dve(s, L, at_n)
                at_n += T
                s.fence()
                gate_dve(s, L)
                residual_dve(s, "out", L)
            s.fence()
            norm_dve(s, n, None)
            n += 1
            s.eng.wait_ge(sem("final_gain"), 16)
            s.after(nc.vector.tensor_tensor(X, XN, bc(RFINAL.unsqueeze(1), [P, T, D]), ALU.mult).then_inc(sem("x_updated"), 1), "x_updated")
            s.fence()
            for L in range(DEPTH):
                norm_dve(s, n, GAINC[:, 16 + 8 * L:24 + 8 * L])
                n += 1
                s.fence()
                mixers_dve(s, L, at_n)
                at_n += 2 * T
                s.fence()
                gla_dve(s, L)
                residual_dve(s, "out2", L)
                norm_dve(s, n, GAINC[:, 32 + 8 * L:40 + 8 * L])
                n += 1
                s.fence()
                if L % 2 == 0:
                    ffn_dve(s, L)
                else:
                    route_dve(s)
                    pass_dve(s, 0)
                    pass_loop_dve(s, 0)

                    def second():
                        pass_dve(s, 1)
                        pass_loop_dve(s, 1)

                    own = s.n
                    overflow(dve, second)
                    s.own, s.n = sem("dve_steps_after_experts"), 0
                    s.after(nc.vector.tensor_copy(SS[:, 0:1], SS[:, 0:1]).then_inc(sem("x_updated"), 1), "x_updated")
                s.fence()
                norm_dve(s, n, GAINC[:, 48 + 8 * L:56 + 8 * L])
                n += 1
                ple_dve(s, L)
                s.fence()
            s.after(nc.vector.tensor_copy(SS[:, 0:1], SS[:, 0:1]).then_inc(sem("out_ready"), 1), "out_ready")

        @block.tensor
        def _(pe):
            s = Steps(pe, "pe")
            setup_pe(pe)
            n = at_n = ht = 0
            for L in range(DEPTH):
                if L == 0:
                    pe.wait_ge(sem("params_ready"), 1)
                norm_pe(pe, n)
                n += 1
                proj1_pe(pe, L)
                s.fence()
                gdn_pe(pe, L)
                s.fence()
                dsa_pe(pe, L, at_n)
                at_n += T
                s.fence()
                gate_pe(pe, L)
                mix_pe(pe, "out", L, L)
            s.fence()
            n += 1
            s.fence()
            ht = DEPTH
            for L in range(DEPTH):
                pe.wait_ge(sem("xn_ready"), n + 1)
                norm_pe(pe, n)
                n += 1
                ht += 1
                pe.wait_ge(sem("ht_ready"), ht)
                u_pe(pe, L)
                s.fence()
                mixers_pe(pe, L, at_n)
                at_n += 2 * T
                s.fence()
                gla_pe(pe, L)
                mix_pe(pe, "out2", L, DEPTH + L)
                norm_pe(pe, n)
                n += 1
                ht += 1
                pe.wait_ge(sem("ht_ready"), ht)
                s.fence()
                if L % 2 == 0:
                    ffn_pe(pe, L)
                else:
                    route_pe(pe)
                    pass_pe(pe, 0)
                    overflow(pe, lambda: pass_pe(pe, 1))
                s.fence()
                norm_pe(pe, n)
                n += 1
                ht += 1
                pe.wait_ge(sem("ht_ready"), ht)
                ple_pe(pe, L)
                s.fence()


_INS = {"x": "x", "positions": "positions", "norm_gain": "norm_gain", "w_in": "w_in", "conv_w": "conv_w",
        "a_log": "a_log", "dt_bias": "dt_bias", "gdn_norm_gain": "gdn_norm_gain", "idx_k_gain": "idx_k_gain",
        "w_out": "w_out", "final_gain": "final_gain"}
_INS_2 = ["p_2", "norm_attn_2", "w_in_2", "w_out_2", "nsa_cmp_pos_2", "nsa_cmp_w1_2", "nsa_cmp_w2_2", "nsa_qk_gain_2",
          "diff_qk_gain_2", "diff_lambda_2", "diff_norm_2", "gla_w_gate2_2", "gla_b_gate_2", "gla_norm_2",
          "hgrn_lb_logits_2", "hgrn_norm_2", "norm_ffn_2", "ffn_w_gate_2", "ffn_w_up_2", "ffn_w_down_2",
          "moe_router_2", "moe_w_gate_2", "moe_w_up_2", "moe_w_down_2", "ple_norm_2", "ple_w_gate_2", "ple_w_proj_2"]
OVER = 128


def kernel(**inputs):
    import concourse.bacc as _bacc
    from concourse.bass_utils import run_bass_kernel_spmd as _run

    nc = _bacc.Bacc("TRN2", target_bir_lowering=False, num_devices=1)
    arrays, args = {}, {}
    for name in list(_INS) + _INS_2:
        a = np.ascontiguousarray(inputs[name])
        arrays[f"in_{name}_dram"] = a
        args[name] = nc.dram_tensor(f"in_{name}_dram", a.shape, mybir.dt.from_np(a.dtype), kind="ExternalInput").ap()
    out = nc.dram_tensor("out_0_dram", (1, S, D), F32, kind="ExternalOutput").ap()
    blocks_kernel(nc, args, out)
    r = _run(nc, [arrays], core_ids=[0])
    return r.results[0]["out_0_dram"]
```

```python
import math
from contextlib import ExitStack

import numpy as np

import concourse.bass as bass
from concourse import mybir

P = 128
S = 256
T = S // P
D = 1024
KD = D // P
DEPTH = 2
F32 = mybir.dt.float32
I32 = mybir.dt.int32
ALU = mybir.AluOpType
ACT = mybir.ActivationFunctionType
AX = mybir.AxisListType
EPS = 1e-6
NEG = -1e30
NONCAUSAL = -3.0e38
TAKEN = -3.3e38

HQ, HKV, DH = 8, 2, 128
ROT, IDX_H, IDX_D, IDX_ROT, TOPK = 32, 8, 64, 16, 64
GH, DK, CONV = 8, 128, 4
Q0, K0, V0, Z0, QI0, KI0, WI0, QKV0, ZB0, BETA0, GATE0, COLS1 = (
    0, 1024, 1280, 1536, 2560, 3072, 3136, 3144, 6216, 7240, 7256, 9304)
CT = 3 * GH
W_P1B = GATE0 - ZB0
HD = 64
(NQ0, KC0, KS0, VS0, KW0, VW0, NG0, DQ0, DK0, DV0, GQ0, GK0, GV0, GLR0, GOG0, RQ0, RF0, RI0, ROG0, COLS2) = (
    0, 256, 384, 448, 512, 576, 640, 652, 908, 1164, 1420, 1548, 1676, 1932, 1948, 2204, 2460, 2716, 2972, 3228)
NCMP, CMP_L, CMP_S = 15, 32, 16
FF = 3584
NE = 8
PLE = 256
LEVELS = 7

RING = 7
HALF = 2048
PER_EXPERT = 2 * 7 * 2 + 14


def blocks_kernel(nc, A, out):
    ctx = ExitStack()
    with ctx:
        sems = {}

        def sem(name):
            if name not in sems:
                sems[name] = ctx.enter_context(nc.semaphore(name))
            return sems[name]

        CHAINS = {
            "cmp_by_tensor": ("cmp_hT", "cmp_kv", "cmp_kT", "cmp_scores", "cmp_pT", "cmp_out"),
            "cmp_by_scalar": ("cmp_silu", "cmp_ksq", "cmp_kroot", "cmp_kT_out", "cmp_scaled", "cmp_exp", "cmp_pT_out"),
            "cmp_by_vector": ("cmp_x", "cmp_hid", "cmp_kms", "cmp_k", "cmp_shifted", "cmp_probs", "cmp_done"),
            "gdn_by_scalar": ("gdn_ln", "gdn_eg", "gdn_osq", "gdn_oroot"),
            "gdn_by_vector": ("gdn_xx", "gdn_g", "gdn_gc_out", "gdn_oms"),
            "m_by_scalar": ("m_squares", "m_roots", "gla_ln", "hg_sig", "hg_ln", "m_osq", "m_oroot"),
            "m_by_vector": ("m_means", "m_normed", "gla_zb", "hg_f", "m_oms"),
            "dsa_by_scalar": ("dsa_ksq", "dsa_kroot"),
            "dsa_by_vector": ("dsa_kms", "dsa_roped"),
        }
        CHAINED = {name: (chain, i, len(names)) for chain, names in CHAINS.items() for i, name in enumerate(names)}

        def signal(name):
            return sem(CHAINED[name][0] if name in CHAINED else name)

        def reached(name, times):
            if name in CHAINED:
                _, i, n = CHAINED[name]
                return n * (times - 1) + i + 1
            return times

        def sb(name, cols, dt=F32):
            return ctx.enter_context(nc.sbuf_tensor(name, [P, cols], dt))

        x_t = sb("x", T * D)
        X = x_t[:, :].rearrange("p (t d) -> p t d", t=T)
        ht_t = sb("hT", KD * S)
        HT = ht_t[:, :].rearrange("p (k s) -> p k s", k=KD)
        xn_t = sb("xn", T * D)
        XN = xn_t[:, :].rearrange("p (t d) -> p t d", t=T)
        mix_t = sb("mix", T * D)
        MIX = mix_t[:, :].rearrange("p (t d) -> p t d", t=T)
        ring = sb("ring", RING * HALF)

        ident_t = sb("ident", P)
        IDENT = ident_t[:, :]
        ones_t = sb("ones", P)
        ONES = ones_t[:, :]
        upper_t = sb("upper", P)
        UPPER = upper_t[:, :]
        supper_t = sb("supper", P)
        SUPPER = supper_t[:, :]
        slow_t = sb("slower", P)
        SLOWER = slow_t[:, :]
        iota_t = sb("iota", P)
        ms_t = sb("lvl_lower", LEVELS * P)
        MS = ms_t[:, :].rearrange("p (l c) -> p l c", l=LEVELS)
        mt_t = sb("lvl_upper", (LEVELS + 1) * P)
        MT = mt_t[:, :].rearrange("p (l c) -> p l c", l=LEVELS + 1)
        cb_t = sb("causal_bias", T * S)
        CB = cb_t[:, :].rearrange("p (t s) -> p t s", t=T)
        cok_t = sb("cmp_ok", T * 32)
        COK = cok_t[:, :].rearrange("p (t n) -> p t n", t=T)
        cbias_t = sb("cmp_bias", T * 32)
        CBIAS = cbias_t[:, :].rearrange("p (t n) -> p t n", t=T)
        cols_t = sb("param_cols", 64 + 192)
        GAINC = cols_t[:, 0:64]
        TAPS = cols_t[:, 64:256].rearrange("p (l k c) -> p l k c", l=DEPTH, k=CONV)
        rows_t = sb("param_rows", 2440)
        at = [0]

        def rows(n):
            at[0] += n
            return rows_t[:, at[0] - n:at[0]]

        R_GDN = rows(DEPTH * DK)
        R_KI = rows(DEPTH * IDX_D)
        R_DT = rows(DEPTH * GH)
        R_EA = rows(DEPTH * GH)
        R_NSA = rows(DEPTH * 4 * HD)
        R_DQK = rows(DEPTH * 2 * 32)
        R_LAM = rows(DEPTH * 4 * 32)
        R_DN = rows(DEPTH * HD)
        R_GLAN = rows(DEPTH * HD)
        R_HGN = rows(DEPTH * HD)
        CMPPOS = rows(DEPTH * CMP_L)
        GLAB = rows(DEPTH)
        WG2 = rows(DEPTH * P)
        LBC = rows(2 * 4)
        FREQ = rows(24)
        EPS1, EPSK = rows(1), rows(1)
        sm_t = sb("small", 1100)
        sat = [0]

        def small(n):
            sat[0] += n
            return sm_t[:, sat[0] - n:sat[0]]

        WARM = small(1)
        SS, MSQ, RT, RSTD = small(2), small(2), small(2), small(2)
        SIN, COS = small(T * 24), small(T * 24)
        T_ANG, T_K = small(T * 24), small(T * 24)
        POSF = small(T)
        pos_t = sb("pos", T, I32)
        w2_t = sb("cmp_w2", DEPTH * 2 * 2 * HD)
        W2 = w2_t[:, :].rearrange("p (l j k n) -> p l j k n", l=DEPTH, j=2, k=2)
        router_t = sb("router", KD * NE)
        ROUTER = router_t[:, :].rearrange("p (k e) -> p k e", k=KD)

        AREA = 22720
        area = sb("area", AREA)

        def view(a, n):
            assert a + n <= AREA
            return area[:, a:a + n]

        psum = ctx.enter_context(nc.psum_tensor("psum", [P, 8, 512], F32))
        PS = psum[:, :, :]

        def banks(a, n):
            return PS[:, a:a + n, :].rearrange("p b c -> p (b c)")

        told = {}

        class Steps:

            def __init__(self, eng, name):
                self.eng, self.own, self.n, self.fences = eng, sem(name + "_steps"), 0, 0

            def do(self, ins):
                self.n += 1
                ins.then_inc(self.own, 1)
                self.eng.wait_ge(self.own, self.n)

            def after(self, ins, name):
                told[name] = told.get(name, 0) + 1
                self.eng.wait_ge(signal(name), reached(name, told[name]))

            def fence(self):
                self.fences += 1
                self.eng.drain().then_inc(sem("fence"), 1)
                self.eng.wait_ge(sem("fence"), 4 * self.fences)

        WOVEN = ("p1", "zb", "gate")
        TILES, LOADS = [], []

        def half_view(n, shape):
            k, w = shape
            r = n % RING
            return ring[:, r * HALF:r * HALF + k * w].rearrange("p (k w) -> p k w", k=k)

        def kview(w):
            return w.rearrange("(k p) n -> p k n", p=P)

        def tile(group, w, c0, n, evac, nk=KD):
            per = nk if nk * n <= HALF else nk // 2
            first = len(LOADS)
            for k in range(0, nk, per):
                LOADS.append(((per, n), [(None, kview(w)[:, k:k + per, c0:c0 + n])]))
            bank = 0 if group[0] in WOVEN else 2 * (len(TILES) % 2)
            TILES.append(dict(group=group, n=n, c0=c0, evac=evac, first=first, halves=nk // per, per=per, nk=nk,
                              end=len(LOADS), bank=bank))

        def span(group, w, c0, c1, evac, nk=KD):
            for c in range(c0, c1, 512):
                tile(group, w, c, min(512, c1 - c), evac, nk)

        CMPW = {}
        DOWN = {}
        for L in range(DEPTH):
            w = A["w_in"][L]
            span(("qkv", L), w, QKV0, ZB0, "act")
            span(("ba", L), w, BETA0, GATE0, "act")
            span(("p1", L), w, 0, QKV0, "act")
            span(("zb", L), w, ZB0, BETA0, "act")
            span(("gate", L), w, GATE0, COLS1, "act")
            span(("out", L), A["w_out"][L], 0, D, "dve")
        for L in range(DEPTH):
            span(("u", L), A["w_in_2"][L], 0, COLS2, "act")
            CMPW[L] = len(LOADS)
            for q in range(4):
                src = A["nsa_cmp_w1_2"][L].rearrange("j (l d) n -> j d l n", d=HD)
                LOADS.append(((8, 256), [(j, src[j, :, 8 * q:8 * q + 8, :]) for j in range(2)]))
            span(("out2", L), A["w_out_2"][L], 0, D, "dve")
            if L % 2 == 0:
                for c in range(0, FF, 512):
                    tile(("ffn", L), A["ffn_w_gate_2"][0], c, 512, "act")
                    tile(("ffn", L), A["ffn_w_up_2"][0], c, 512, "dve")
                DOWN[L] = len(LOADS)
                for k in range(0, FF // P, 2):
                    LOADS.append(((2, D), [(None, kview(A["ffn_w_down_2"][0])[:, k:k + 2, :])]))
            else:
                MOE0 = len(LOADS)
                for _ in range(NE * PER_EXPERT):
                    LOADS.append(None)
            span(("pg", L), A["ple_w_gate_2"][L], 0, D, "act")
            span(("pp", L), A["ple_w_proj_2"][L], 0, D, "dve", PLE // P)
        LANDED, counts = [], [0] * RING
        for n, load in enumerate(LOADS):
            counts[n % RING] += 16 * (len(load[1]) if load else 1)
            LANDED.append(counts[n % RING])
        assert PER_EXPERT % RING == 0

        def group(name, L):
            return [g for g, d in enumerate(TILES) if d["group"] == (name, L)]

        def evacuated(g):
            kind = TILES[g]["evac"]
            return "gemm_out_" + kind, sum(1 for d in TILES[:g + 1] if d["evac"] == kind)

        def acc(g):
            return PS[:, TILES[g]["bank"]:TILES[g]["bank"] + 2, :]

        def landed(eng, n):
            eng.wait_ge(sem(f"landed{n % RING}"), LANDED[n])

        def used(n):
            return n + 1

        def gemm_begin(pe, g):
            before = [b for b in range(g) if TILES[b]["bank"] == TILES[g]["bank"]]
            if before:
                name, value = evacuated(before[-1])
                pe.wait_ge(sem(name), value)

        def gemm_steps(pe, gs, lhs, whole=None):
            for g in gs:
                d = TILES[g]
                gemm_begin(pe, g)
                for h in range(d["halves"]):
                    if whole and (g, h) == (gs[0], 1):
                        pe.wait_ge(sem("ht_ready"), whole)
                    n = d["first"] + h
                    landed(pe, n)
                    w = half_view(n, (d["per"], d["n"]))
                    for k in range(d["per"]):
                        kk = h * d["per"] + k
                        for t in range(T):
                            last = nc.tensor.matmul(acc(g)[:, t, 0:d["n"]], lhs(kk, t), w[:, k, :],
                                                    start=kk == 0, stop=kk == d["nk"] - 1)
                        if (k + 1) % max(1, d["per"] // 4) == 0:
                            if k == d["per"] - 1:
                                last.then_inc(sem("weights_used"), 1)
                            yield

        def gemm(pe, g, lhs, whole=None):
            for _ in gemm_steps(pe, [g], lhs, whole):
                pass

        def weave(main, other, n_main, n_other):
            done = 0
            for i in range(n_main):
                next(main)
                while (done + 1) * n_main <= (i + 1) * n_other:
                    next(other)
                    done += 1
            assert next(main, "end") == "end" and next(other, "end") == "end"

        def weave_tensor(main, other, n_main, n_other):
            done = 0
            for i in range(n_main):
                due = 4 * (i + 1) * n_other // n_main
                open_end = 4 * (i * n_other // n_main + 1)
                while next(main) == "gap":
                    for _ in range(min((done + due + 1) // 2, open_end) - done):
                        next(other)
                        done += 1
                while done < due:
                    next(other)
                    done += 1
            assert next(main, "end") == "end" and next(other, "end") == "end"

        def ht_lhs(k, t):
            return HT[:, k, t * P:(t + 1) * P]

        def transposes(blocks, bank0):
            for b, block in enumerate(blocks):
                for t in range(T):
                    src = block(t)
                    m = src.shape[1]
                    last = nc.tensor.transpose(PS[0:m, bank0 + b // 2, (b % 2) * S + t * P:(b % 2) * S + (t + 1) * P],
                                               src, IDENT)
            return last

        def bc(ap, shape):
            return ap.to_broadcast(shape)

        def norm_act(s, n):
            if n == 0:
                s.eng.wait_ge(sem("x_loaded"), 16)
            else:
                s.do(nc.scalar.activation(WARM, ONES[:, 0:1], ACT.Sqrt))
                s.eng.wait_ge(sem("x_updated"), n)
            s.do(nc.scalar.activation(XN[:, 0, :], X[:, 0, :], ACT.Square, accum_out=SS[:, 0:1]))
            s.after(nc.scalar.activation(XN[:, 1, :], X[:, 1, :], ACT.Square, accum_out=SS[:, 1:2]).then_inc(sem("norm_sums"), 1), "norm_sums")
            s.eng.wait_ge(sem("norm_means"), n + 1)
            s.after(nc.scalar.activation(RT, MSQ, ACT.Sqrt).then_inc(sem("norm_roots"), 1), "norm_roots")

        def norm_dve(s, n, gain):
            s.eng.wait_ge(sem("norm_sums"), n + 1)
            s.after(nc.vector.tensor_scalar(MSQ, SS, 1.0 / D, EPS, ALU.mult, ALU.add).then_inc(sem("norm_means"), 1), "norm_means")
            s.eng.wait_ge(sem("norm_roots"), n + 1)
            s.do(nc.vector.reciprocal(RSTD, RT))
            for t in range(T):
                ins = nc.vector.tensor_scalar(XN[:, t, :], X[:, t, :], RSTD[:, t:t + 1], None, ALU.mult)
                if t == 0:
                    s.do(ins)
                else:
                    s.after(ins.then_inc(sem("xn_ready"), 1), "xn_ready")
            if gain is not None:
                for half in range(2):
                    s.eng.wait_ge(sem("norm_transposed"), told.get("ht_ready", 0) + 1)
                    ks = slice(4 * half, 4 * half + 4)
                    s.after(nc.vector.tensor_tensor(HT[:, ks, :], banks(4 + 2 * half, 2).rearrange("p (k s) -> p k s", k=4),
                                                    bc(gain[:, ks].unsqueeze(2), [P, 4, S]), ALU.mult)
                            .then_inc(sem("ht_ready"), 1), "ht_ready")

        def norm_pe(pe, n):
            pe.wait_ge(sem("xn_ready"), n + 1)
            blocks = [(lambda t, k=k: XN[:, t, k * P:(k + 1) * P]) for k in range(KD)]
            transposes(blocks[0:4], 4).then_inc(sem("norm_transposed"), 1)
            transposes(blocks[4:8], 6).then_inc(sem("norm_transposed"), 1)

        U = view(0, T * (QKV0)).rearrange("p (t c) -> p t c", t=T)
        P1B = view(6288, T * W_P1B).rearrange("p (t c) -> p t c", t=T)
        Y = view(8368, CT * S).rearrange("p (c s) -> p c s", c=CT)
        XC = view(14512, CT * (S + 3)).rearrange("p (c s) -> p c s", c=CT)

        def proj1_pe(pe, L):
            pe.wait_ge(sem("ht_ready"), 2 * L + 1)
            if L == 0:
                pe.wait_ge(sem("cols_ready"), 1)
            def sums(hq):
                if L + hq == 0:
                    pe.wait_ge(sem("consts_ready"), 1)
                pe.wait_ge(sem("gdn_squares"), 2 * L + hq + 1)
                if hq:
                    pe.wait_ge(sem("gdn_logs"), 2 * L + 1)
                for b in range(4):
                    last = nc.tensor.matmul(PS[:, 4 + b, :], ONES, (SQ, RN)[hq][:, 512 * b:512 * b + 512],
                                            start=True, stop=True)
                last.then_inc(sem("gdn_sums"), 1)

            for i, g in enumerate(group("qkv", L)):
                d = TILES[g]
                gemm_begin(pe, g)
                for h in range(2):
                    landed(pe, d["first"] + h)
                for j in range(4):
                    for k in range(KD):
                        if g == group("qkv", L)[0] and (j, k) == (0, 4):
                            pe.wait_ge(sem("ht_ready"), 2 * L + 2)
                        n = d["first"] + k // 4
                        last = nc.tensor.matmul(
                            acc(g)[:, j // 2, (j % 2) * S:(j % 2) * S + S],
                            half_view(n, (4, 512))[:, k % 4, j * P:(j + 1) * P], HT[:, k, :],
                            start=k == 0, stop=k == KD - 1)
                        if j == 3 and k % 4 == 3:
                            last.then_inc(sem("weights_used"), 1)
                if i == 3:
                    sums(0)
                if i == 5:
                    sums(1)
            for g in group("ba", L):
                gemm(pe, g, ht_lhs)

        def proj1_act(s, L):
            def conv_silu(j):
                s.eng.wait_ge(sem("conv_done"), 6 * L + j + 1)
                s.do(nc.scalar.activation(Y[:, 4 * j:4 * j + 4, :], Y[:, 4 * j:4 * j + 4, :], ACT.Silu))

            def rsqrt(hq):
                if L + hq == 0:
                    s.eng.wait_ge(sem("consts_ready"), 1)
                s.eng.wait_ge(sem("gdn_sums"), 2 * L + hq + 1)
                scale, eps = (float(DK), EPSK) if hq == 0 else (1.0, EPS1)
                s.after(nc.scalar.activation((SQ, RN)[hq], banks(4, 4), ACT.Ln, bias=eps, scale=scale)
                        .then_inc(sem("gdn_logs"), 1), "gdn_logs")
                s.after(nc.scalar.activation((SQ, RN)[hq], (SQ, RN)[hq], ACT.Exp, scale=-0.5)
                        .then_inc(sem("gdn_rsqrt"), 1), "gdn_rsqrt")

            for j, g in enumerate(group("qkv", L)):
                s.eng.wait_ge(sem("weights_used"), used(TILES[g]["end"] - 1))
                src = acc(g).rearrange("p b (j s) -> p (b j) s", j=2)
                s.after(nc.scalar.activation(XC[:, 4 * j:4 * j + 4, 3:3 + S], src, ACT.Copy).then_inc(sem("gemm_out_act"), 1), "gemm_out_act")
                if L == 0 and j < 4:
                    load_params(s.eng, 8 * j, 8 * j + 8)
                if j:
                    conv_silu(j - 1)
                if j == 2:
                    s.after(nc.scalar.activation(SQ, Y[:, 0:GH, :].rearrange("p c s -> p (c s)"), ACT.Square)
                            .then_inc(sem("gdn_squares"), 1), "gdn_squares")
                if j == 4:
                    s.after(nc.scalar.activation(RN, Y[:, GH:2 * GH, :].rearrange("p c s -> p (c s)"), ACT.Square)
                            .then_inc(sem("gdn_squares"), 1), "gdn_squares")
                    if L == 0:
                        setup_act(s)
                        trig_tables(None, s)
                    rsqrt(0)
            for g in group("ba", L):
                s.eng.wait_ge(sem("weights_used"), used(TILES[g]["end"] - 1))
                s.after(nc.scalar.activation(P1B[:, :, D:W_P1B], acc(g)[:, :, 0:2 * GH], ACT.Copy)
                        .then_inc(sem("gemm_out_act"), 1), "gemm_out_act")
            rsqrt(1)
            conv_silu(5)

        SG = [xn_t[:, 1024 * i:1024 * i + 1024].rearrange("p (t c) -> p t c", t=T) for i in range(2)]

        def woven_act(s, names, L):
            for name in names:
                for i, g in enumerate(group(name, L)):
                    d = TILES[g]
                    for _ in range(d["halves"] - 1):
                        yield
                    s.eng.wait_ge(sem("weights_used"), used(d["end"] - 1))
                    a, b = d["c0"], d["c0"] + d["n"]
                    if name == "p1":
                        parts = [(U[:, :, max(a, lo):min(b, hi)], max(a, lo), min(b, hi), f) for lo, hi, f in
                                 ((0, Z0, ACT.Copy), (Z0, QI0, ACT.Silu), (QI0, QKV0, ACT.Copy))
                                 if max(a, lo) < min(b, hi)]
                    elif name == "zb":
                        parts = [(P1B[:, :, a - ZB0:b - ZB0], a, b, ACT.Silu)]
                    else:
                        if i >= 2:
                            s.eng.wait_ge(sem("gated"), 4 * L + i - 1)
                        parts = [(SG[i % 2], a, b, ACT.Sigmoid)]
                    for dst, lo, hi, f in parts[:-1]:
                        s.do(nc.scalar.activation(dst, acc(g)[:, :, lo - a:hi - a], f))
                    dst, lo, hi, f = parts[-1]
                    s.after(nc.scalar.activation(dst, acc(g)[:, :, lo - a:hi - a], f)
                            .then_inc(sem("gemm_out_act"), 1), "gemm_out_act")
                    yield

        def woven_dve(s, names, L):
            for name in names:
                for i, g in enumerate(group(name, L)):
                    for _ in range(TILES[g]["halves"] - 1):
                        yield
                    if name == "gate":
                        s.eng.wait_ge(sem("gemm_out_act"), evacuated(g)[1])
                        c = 512 * (i % 2)
                        y = U[:, :, Z0 + c:Z0 + c + 512] if i < 2 else P1B[:, :, c:c + 512]
                        s.after(nc.vector.tensor_tensor(y, y, SG[i % 2], ALU.mult).then_inc(sem("gated"), 1), "gated")
                        if i >= 2:
                            mc = MIX[:, :, c:c + 512]
                            s.do(nc.vector.tensor_tensor(mc, mc, y, ALU.mult))
                    yield

        def halves(names, L):
            return sum(TILES[g]["halves"] for name in names for g in group(name, L))

        def conv_dve(s, L):
            def unit_length(hq):
                s.eng.wait_ge(sem("gdn_rsqrt"), 2 * L + hq + 1)
                q = Y[:, GH * hq:GH * hq + GH, :].rearrange("p c s -> p (c s)")
                s.do(nc.vector.tensor_tensor(q, q, (SQ, RN)[hq], ALU.mult))

            s.do(nc.vector.memset(XC[:, :, 0:3], 0.0))
            for j, g in enumerate(group("qkv", L)):
                if L == 0 and j == 4:
                    setup_dve(s)
                    trig_tables(s, None)
                if j == 5:
                    unit_length(0)
                s.eng.wait_ge(sem("gemm_out_act"), evacuated(g)[1])
                for tap in range(CONV):
                    for c in range(4 * j, 4 * j + 4):
                        w = TAPS[:, L, tap, c:c + 1]
                        if tap == 0:
                            ins = nc.vector.tensor_scalar(Y[:, c, :], XC[:, c, 0:S], w, None, ALU.mult)
                        else:
                            ins = nc.vector.scalar_tensor_tensor(Y[:, c, :], XC[:, c, tap:tap + S], w, Y[:, c, :],
                                                                 ALU.mult, ALU.add)
                        if tap == CONV - 1 and c == 4 * j + 3:
                            s.after(ins.then_inc(sem("conv_done"), 1), "conv_done")
                        elif c == 4 * j + 3:
                            s.do(ins)
            unit_length(1)

        HG = 4 * P
        G0 = 14512
        SQ = view(G0, 2048)
        RN = view(G0 + 2048, 2048)

        def unit(k):
            return [view(G0 + k * 1024 + u * 512, 512).rearrange("p (h c) -> p h c", h=4) for u in range(2)]

        LF, LM, XI, XT, VV, AT, BV = [unit(k) for k in range(7)]
        VN = LM
        STATE = view(G0 + 7168, GH * P).rearrange("p (h c) -> p h c", h=GH)
        GG = small(T * GH)
        G3 = GG.rearrange("p (t h) -> p t h", t=T)
        BETA = small(T * GH)
        B3 = BETA.rearrange("p (t h) -> p t h", t=T)
        GC = small(3 * GH)
        EG = small(2 * GH)
        EGL = small(GH)
        GTMP, GTMP2 = small(T * GH), small(T * GH)
        ONM, ONR = small(T * GH), small(T * GH)

        def sm3(ap):
            return ap.rearrange("p (t h) -> p t h", t=T)

        def bank4(b):
            return PS[:, b, :].rearrange("p (h c) -> p h c", h=4)

        def firsts(x, lv):
            return x.rearrange("p h (b two n) -> p h b two n", two=2, n=1 << lv)[:, :, :, 0, :]

        def seconds(x, lv):
            return x.rearrange("p h (b two n) -> p h b two n", two=2, n=1 << lv)[:, :, :, 1, :]

        GDN_STEPS = 2 + 2 * (2 + LEVELS + 3) + 1

        def gdn_pe(pe, L):
            pe.wait_ge(signal("gdn_g"), reached("gdn_g", L + 1))
            for c in range(2):
                nc.tensor.matmul(PS[:, 6, c * GH:c * GH + GH], UPPER, G3[:, c, :], start=True, stop=True)
            nc.tensor.matmul(PS[:, 6, 2 * GH:3 * GH], ONES, G3[:, 0, :], start=True, stop=True)\
                .then_inc(sem("gdn_gc"), 1)
            yield
            pe.wait_ge(signal("gdn_gc_out"), reached("gdn_gc_out", L + 1))
            yield
            for c in range(2):
                tok = slice(c * P, (c + 1) * P)
                for u in range(2):
                    for h in range(4):
                        hh, cs = 4 * u + h, slice(h * P, (h + 1) * P)
                        q, k = Y[:, hh, tok], Y[:, GH + hh, tok]
                        nc.tensor.matmul(PS[:, 6 + u, cs], bc(G3[:, c, hh:hh + 1], [P, P]), UPPER,
                                         start=True, stop=True)
                        nc.tensor.matmul(PS[:, 2 + u, cs], k, k, start=True, stop=True)
                        last = nc.tensor.matmul(PS[:, 4 + u, cs], k, q, start=True, stop=True)
                    last.then_inc(sem("gdn_scores"), 1)
                yield
                yield
                for u in range(2):
                    pe.wait_ge(sem("gdn_init"), 4 * L + 2 * c + u + 1)
                    for h in range(4):
                        last = nc.tensor.transpose(PS[:, 2 + u, h * P:(h + 1) * P], XI[u][:, h, :], IDENT)
                    last.then_inc(sem("gdn_first"), 1)
                yield
                for lv in range(1, LEVELS):
                    base = ((2 * L + c) * (LEVELS - 1) + lv - 1) * 2
                    for u in range(2):
                        if lv == 1:
                            pe.wait_ge(sem("gdn_first_out"), 4 * L + 2 * c + u + 1)
                        else:
                            pe.wait_ge(sem("gdn_X"), base - 2 + u + 1)
                        pe.wait_ge(sem("gdn_Lm"), base + u + 1)
                        for h in range(4):
                            last = nc.tensor.matmul(PS[:, 2 + u, h * P:(h + 1) * P], LM[u][:, h, :], XT[u][:, h, :],
                                                    start=True, stop=True)
                        last.then_inc(sem("gdn_V"), 1)
                    yield "gap"
                    for u in range(2):
                        pe.wait_ge(sem("gdn_V_out"), base + u + 1)
                        for h in range(4):
                            nc.tensor.matmul(PS[:, 4 + u, h * 64:(h + 1) * 64], VV[u][:, h, :],
                                             firsts(XI[u], lv)[:, h], start=True, stop=True)
                        for h in range(4):
                            last = nc.tensor.matmul(PS[:, 6 + u, h * 64:(h + 1) * 64], XI[u][:, h, :],
                                                    seconds(VV[u], lv)[:, h], start=True, stop=True)
                        last.then_inc(sem("gdn_Z"), 1)
                    yield
                for u in range(2):
                    for h in range(4):
                        cs = slice(h * P, (h + 1) * P)
                        last = nc.tensor.transpose(PS[:, 2 + u, cs], Y[:, 2 * GH + 4 * u + h, tok], IDENT)
                    pe.wait_ge(sem("gdn_X"), ((2 * L + c) * (LEVELS - 1) + LEVELS - 2) * 2 + u + 1)
                    for h in range(4):
                        hh, cs = 4 * u + h, slice(h * P, (h + 1) * P)
                        if c == 1:
                            nc.tensor.matmul(PS[:, 4 + u, cs], Y[:, GH + hh, tok], STATE[:, hh, :],
                                             start=True, stop=True)
                            last = nc.tensor.matmul(PS[:, 6 + u, cs], Y[:, hh, tok], STATE[:, hh, :],
                                                    start=True, stop=True)
                        else:
                            last = nc.tensor.transpose(PS[:, 4 + u, cs], Y[:, GH + hh, tok], IDENT)
                    last.then_inc(sem("gdn_vT"), 1)
                yield
                for u in range(2):
                    pe.wait_ge(sem("gdn_B"), 4 * L + 2 * c + u + 1)
                    if c == 0:
                        pe.wait_ge(sem("gdn_k_out"), 2 * L + u + 1)
                    for h in range(4):
                        last = nc.tensor.matmul(PS[:, 4 + u, h * P:(h + 1) * P], XT[u][:, h, :], BV[u][:, h, :],
                                                start=True, stop=True)
                    last.then_inc(sem("gdn_vn"), 1)
                yield
                for u in range(2):
                    pe.wait_ge(sem("gdn_vn_out"), 4 * L + 2 * c + u + 1)
                    for h in range(4):
                        last = nc.tensor.matmul(PS[:, 6 + u, h * P:(h + 1) * P], AT[u][:, h, :], VN[u][:, h, :],
                                                start=True, stop=True)
                    last.then_inc(sem("gdn_o"), 1)
                    if c == 0:
                        pe.wait_ge(sem("gdn_vd"), 2 * L + u + 1)
                        for h in range(4):
                            last = nc.tensor.matmul(PS[:, 2 + u, h * P:(h + 1) * P], LF[u][:, h, :], BV[u][:, h, :],
                                                    start=True, stop=True)
                        last.then_inc(sem("gdn_state"), 1)
                if c == 0:
                    pe.wait_ge(sem("gdn_state_out"), 2 * L + 2)
                    pe.wait_ge(sem("gdn_o_out"), 4 * L + 2)
                yield
            yield

        def gdn_act(s, L):
            s.do(nc.scalar.activation(B3, P1B[:, :, D:D + GH], ACT.Sigmoid))
            s.eng.wait_ge(signal("gdn_xx"), reached("gdn_xx", L + 1))
            s.do(nc.scalar.activation(GTMP2, GTMP, ACT.Abs))
            s.do(nc.scalar.activation(GTMP2, GTMP2, ACT.Exp, scale=-1.0))
            s.after(nc.scalar.activation(GTMP2, GTMP2, ACT.Ln, bias=1.0).then_inc(signal("gdn_ln"), 1), "gdn_ln")
            yield
            s.eng.wait_ge(signal("gdn_gc_out"), reached("gdn_gc_out", L + 1))
            s.do(nc.scalar.activation(EG, GC[:, 0:2 * GH], ACT.Exp))
            s.after(nc.scalar.activation(EGL, GC[:, 2 * GH:3 * GH], ACT.Exp).then_inc(signal("gdn_eg"), 1), "gdn_eg")
            yield
            for c in range(2):
                for u in range(2):
                    s.eng.wait_ge(sem("gdn_gaps"), 4 * L + 2 * c + u + 1)
                    s.do(nc.scalar.activation(XT[u], XT[u], ACT.Exp, scale=-1.0))
                    s.after(nc.scalar.activation(XI[u], XI[u], ACT.Exp).then_inc(sem("gdn_decays"), 1), "gdn_decays")
                yield
                yield
                for u in range(2):
                    s.eng.wait_ge(sem("gdn_first"), 4 * L + 2 * c + u + 1)
                    s.after(nc.scalar.activation(XT[u], bank4(2 + u), ACT.Copy)
                            .then_inc(sem("gdn_first_out"), 1), "gdn_first_out")
                yield
                for lv in range(1, LEVELS):
                    for u in range(2):
                        s.eng.wait_ge(sem("gdn_V"), ((2 * L + c) * (LEVELS - 1) + lv - 1) * 2 + u + 1)
                        s.after(nc.scalar.activation(VV[u], bank4(2 + u), ACT.Copy)
                                .then_inc(sem("gdn_V_out"), 1), "gdn_V_out")
                    yield
                if c == 0:
                    for u in range(2):
                        s.eng.wait_ge(sem("gdn_vT"), 4 * L + u + 1)
                        s.after(nc.scalar.activation(LF[u], bank4(4 + u), ACT.Copy)
                                .then_inc(sem("gdn_k_out"), 1), "gdn_k_out")
                yield
                for u in range(2):
                    s.eng.wait_ge(sem("gdn_vn"), 4 * L + 2 * c + u + 1)
                    s.after(nc.scalar.activation(VN[u], bank4(4 + u), ACT.Copy)
                            .then_inc(sem("gdn_vn_out"), 1), "gdn_vn_out")
                yield
                if c == 0:
                    for u in range(2):
                        s.eng.wait_ge(sem("gdn_state"), 2 * L + u + 1)
                        s.after(nc.scalar.activation(STATE[:, 4 * u:4 * u + 4, :], bank4(2 + u), ACT.Copy)
                                .then_inc(sem("gdn_state_out"), 1), "gdn_state_out")
                yield
            s.eng.wait_ge(sem("gdn_o_out"), 4 * L + 4)
            s.after(nc.scalar.activation(SQ, mix_t[:, :], ACT.Square).then_inc(signal("gdn_osq"), 1), "gdn_osq")
            s.eng.wait_ge(signal("gdn_oms"), reached("gdn_oms", L + 1))
            s.after(nc.scalar.activation(ONR, ONM, ACT.Sqrt).then_inc(signal("gdn_oroot"), 1), "gdn_oroot")
            yield

        def gdn_pool(s, L):
            for c in range(2):
                for lv in range(1, LEVELS):
                    for u in range(2):
                        base = ((2 * L + c) * (LEVELS - 1) + lv - 1) * 2
                        if lv == 1:
                            s.eng.wait_ge(sem("gdn_init"), 4 * L + 2 * c + u + 1)
                            if c == 1:
                                s.eng.wait_ge(sem("gdn_o_out"), 4 * L + u + 1)
                        else:
                            s.eng.wait_ge(sem("gdn_V"), base - 2 + u + 1)
                        s.after(nc.gpsimd.tensor_tensor(LM[u], LF[u], bc(MS[:, lv, :].unsqueeze(1), [P, 4, P]),
                                                        ALU.mult).then_inc(sem("gdn_Lm"), 1), "gdn_Lm")

        def gdn_dve(s, L):
            s.after(nc.vector.tensor_tensor(sm3(GTMP), P1B[:, :, D + GH:D + 2 * GH],
                                            bc(R_DT[:, L * GH:(L + 1) * GH].unsqueeze(1), [P, T, GH]), ALU.add)
                    .then_inc(signal("gdn_xx"), 1), "gdn_xx")
            s.eng.wait_ge(signal("gdn_ln"), reached("gdn_ln", L + 1))
            s.do(nc.vector.scalar_tensor_tensor(GTMP, GTMP, 0.0, GTMP2, ALU.max, ALU.add))
            s.after(nc.vector.scalar_tensor_tensor(G3, sm3(GTMP), -1.0,
                                                   bc(R_EA[:, L * GH:(L + 1) * GH].unsqueeze(1), [P, T, GH]),
                                                   ALU.mult, ALU.mult).then_inc(signal("gdn_g"), 1), "gdn_g")
            yield
            s.eng.wait_ge(sem("gdn_gc"), L + 1)
            s.do(nc.vector.tensor_copy(GC, PS[:, 6, 0:3 * GH]))
            s.after(nc.vector.tensor_tensor(GC[:, 2 * GH:], GC[:, 2 * GH:], GC[:, 0:GH], ALU.subtract)
                    .then_inc(signal("gdn_gc_out"), 1), "gdn_gc_out")
            s.eng.wait_ge(signal("gdn_eg"), reached("gdn_eg", L + 1))
            yield
            for c in range(2):
                for u in range(2):
                    n = 4 * L + 2 * c + u
                    hs = slice(c * GH + 4 * u, c * GH + 4 * u + 4)
                    s.eng.wait_ge(sem("gdn_scores"), n + 1)
                    s.do(nc.vector.tensor_tensor(XI[u], bank4(6 + u), bc(GC[:, hs].unsqueeze(2), [P, 4, P]),
                                                 ALU.subtract))
                    s.do(nc.vector.tensor_scalar(XT[u], XI[u], 0.0, None, ALU.max))
                    s.after(nc.vector.tensor_scalar(XI[u], XI[u], 0.0, None, ALU.min)
                            .then_inc(sem("gdn_gaps"), 1), "gdn_gaps")
                yield
                for u in range(2):
                    n = 4 * L + 2 * c + u
                    hs = slice(c * GH + 4 * u, c * GH + 4 * u + 4)
                    s.eng.wait_ge(sem("gdn_decays"), n + 1)
                    s.do(nc.vector.tensor_tensor(XT[u], XT[u], bc(SLOWER.unsqueeze(1), [P, 4, P]), ALU.mult))
                    s.do(nc.vector.tensor_tensor(XT[u], XT[u], bc(BETA[:, hs].unsqueeze(2), [P, 4, P]), ALU.mult))
                    s.do(nc.vector.tensor_tensor(LF[u], bank4(2 + u), XT[u], ALU.mult))
                    s.do(nc.vector.tensor_tensor(XI[u], XI[u], bc(UPPER.unsqueeze(1), [P, 4, P]), ALU.mult))
                    s.do(nc.vector.tensor_tensor(AT[u], bank4(4 + u), XI[u], ALU.mult))
                    s.do(nc.vector.tensor_tensor(XI[u], LF[u], bc(MS[:, 0, :].unsqueeze(1), [P, 4, P]), ALU.mult))
                    s.after(nc.vector.scalar_tensor_tensor(XI[u], XI[u], -1.0, bc(IDENT.unsqueeze(1), [P, 4, P]),
                                                           ALU.mult, ALU.add).then_inc(sem("gdn_init"), 1), "gdn_init")
                yield
                yield
                for lv in range(1, LEVELS):
                    for u in range(2):
                        s.eng.wait_ge(sem("gdn_Z"), ((2 * L + c) * (LEVELS - 1) + lv - 1) * 2 + u + 1)
                        z = [PS[:, b + u, 0:256].rearrange("p (g n) -> p g n", n=1 << lv) for b in (4, 6)]
                        xi, xt = [v.rearrange("p h (b two n) -> p (h b) two n", two=2, n=1 << lv)[:, :, i, :]
                                  for i, v in enumerate((XI[u], XT[u]))]
                        s.do(nc.vector.tensor_tensor(xi, xi, z[0], ALU.subtract))
                        s.after(nc.vector.tensor_tensor(xt, xt, z[1], ALU.subtract)
                                .then_inc(sem("gdn_X"), 1), "gdn_X")
                    yield
                for u in range(2):
                    n = 4 * L + 2 * c + u
                    hs = slice(c * GH + 4 * u, c * GH + 4 * u + 4)
                    beta, eg = bc(BETA[:, hs].unsqueeze(2), [P, 4, P]), bc(EG[:, hs].unsqueeze(2), [P, 4, P])
                    o = MIX[:, c, 512 * u:512 * u + 512].rearrange("p (h c) -> p h c", h=4)
                    s.eng.wait_ge(sem("gdn_vT"), n + 1)
                    if c == 0:
                        ins = nc.vector.tensor_tensor(BV[u], bank4(2 + u), beta, ALU.mult)
                    else:
                        s.do(nc.vector.tensor_tensor(o, bank4(6 + u), eg, ALU.mult))
                        s.do(nc.vector.tensor_tensor(BV[u], bank4(4 + u), eg, ALU.mult))
                        s.do(nc.vector.tensor_tensor(BV[u], bank4(2 + u), BV[u], ALU.subtract))
                        ins = nc.vector.tensor_tensor(BV[u], BV[u], beta, ALU.mult)
                    s.after(ins.then_inc(sem("gdn_B"), 1), "gdn_B")
                yield
                if c == 0:
                    for u in range(2):
                        s.eng.wait_ge(sem("gdn_vn_out"), 4 * L + u + 1)
                        s.after(nc.vector.tensor_tensor(
                            BV[u], VN[u], bc(EGL[:, 4 * u:4 * u + 4].unsqueeze(2), [P, 4, P]), ALU.mult)
                            .then_inc(sem("gdn_vd"), 1), "gdn_vd")
                yield
                for u in range(2):
                    o = MIX[:, c, 512 * u:512 * u + 512].rearrange("p (h c) -> p h c", h=4)
                    s.eng.wait_ge(sem("gdn_o"), 4 * L + 2 * c + u + 1)
                    if c == 0:
                        ins = nc.vector.tensor_copy(o, bank4(6 + u))
                    else:
                        ins = nc.vector.tensor_tensor(o, o, bank4(6 + u), ALU.add)
                    s.after(ins.then_inc(sem("gdn_o_out"), 1), "gdn_o_out")
                yield
            s.eng.wait_ge(signal("gdn_osq"), reached("gdn_osq", L + 1))
            s.do(nc.vector.tensor_reduce(ONM, SQ.rearrange("p (g c) -> p g c", c=P), AX.X, ALU.add))
            s.after(nc.vector.tensor_scalar(ONM, ONM, 1.0 / DK, EPS, ALU.mult, ALU.add)
                    .then_inc(signal("gdn_oms"), 1), "gdn_oms")
            s.eng.wait_ge(signal("gdn_oroot"), reached("gdn_oroot", L + 1))
            s.do(nc.vector.reciprocal(ONR, ONR))
            o = mix_t[:, :].rearrange("p (g c) -> p g c", c=P)
            s.do(nc.vector.tensor_tensor(o, o, bc(ONR.unsqueeze(2), [P, T * GH, P]), ALU.mult))
            s.do(nc.vector.tensor_tensor(o, o, bc(R_GDN[:, L * DK:(L + 1) * DK].unsqueeze(1), [P, T * GH, P]), ALU.mult))
            yield

        TT = view(8368, 16 * S).rearrange("p (b s) -> p b s", b=16)
        SCORES = view(12464, 8 * S).rearrange("p (h s) -> p h s", h=8)
        PT = view(14512, 8 * T * P).rearrange("p (h j q) -> p h j q", h=8, j=T)
        MAXS, DEN, RDEN = small(8), small(8), small(8)

        ATTN_STEPS = 3

        def attn_pe(pe, n, t, maps, values, outs):
            for h, (q, k) in enumerate(maps):
                last = nc.tensor.matmul(PS[:, 4 + h // 2, (h % 2) * S:(h % 2) * S + (t + 1) * P],
                                        q[:, t * P:(t + 1) * P], k[:, 0:(t + 1) * P], start=True, stop=True)
            last.then_inc(sem("at_scores"), 1)
            yield
            pe.wait_ge(sem("at_probs"), n + 1)
            for h in range(outs):
                for j in range(t + 1):
                    last = nc.tensor.transpose(PS[:, 4 + h // 2, ((h % 2) * T + j) * P:((h % 2) * T + j + 1) * P],
                                               SCORES[:, h, j * P:(j + 1) * P], IDENT)
            last.then_inc(sem("at_transposed"), 1)
            yield
            pe.wait_ge(sem("at_PT"), n + 1)
            w = values(0, 0).shape[1]
            per = 512 // w
            for h in range(outs):
                for j in range(t + 1):
                    last = nc.tensor.matmul(PS[:, 4 + h // per, (h % per) * w:(h % per + 1) * w], PT[:, h, j, :],
                                            values(h, j), start=j == 0, stop=j == t)
            last.then_inc(sem("at_out"), 1)
            yield

        def attn_act(s, n, t, maps, outs, result=None):
            keys = (t + 1) * P
            s.eng.wait_ge(sem("at_max"), n + 1)
            for h in range(maps):
                ins = nc.scalar.activation(SCORES[:, h, 0:keys], SCORES[:, h, 0:keys], ACT.Exp, bias=MAXS[:, h:h + 1],
                                           accum_out=DEN[:, h:h + 1])
            s.after(ins.then_inc(sem("at_exp"), 1), "at_exp")
            yield
            s.eng.wait_ge(sem("at_transposed"), n + 1)
            s.after(nc.scalar.activation(
                PT[:, 0:outs, 0:t + 1, :],
                banks(4, 4).rearrange("p (h j q) -> p h j q", h=8, j=T)[:, 0:outs, 0:t + 1, :], ACT.Copy)
                .then_inc(sem("at_PT"), 1), "at_PT")
            yield
            if result:
                s.eng.wait_ge(sem("at_out"), n + 1)
                result()
            yield

        def attn_dve(s, n, t, maps, scale, bias, result=None, lam=None):
            keys = (t + 1) * P
            sc = SCORES[:, 0:maps, 0:keys]
            s.eng.wait_ge(sem("at_scores"), n + 1)
            s.do(nc.vector.scalar_tensor_tensor(
                sc, banks(4, 4).rearrange("p (h s) -> p h s", h=8)[:, 0:maps, 0:keys], scale,
                bc(bias.unsqueeze(1), [P, maps, keys]), ALU.mult, ALU.add))
            s.do(nc.vector.tensor_reduce(MAXS[:, 0:maps], sc, AX.X, ALU.max))
            s.after(nc.vector.tensor_scalar(MAXS[:, 0:maps], MAXS[:, 0:maps], -1.0, None, ALU.mult)
                    .then_inc(sem("at_max"), 1), "at_max")
            yield
            s.eng.wait_ge(sem("at_exp"), n + 1)
            if lam is None:
                s.after(nc.vector.reciprocal(RDEN[:, 0:maps], DEN[:, 0:maps]).then_inc(sem("at_probs"), 1), "at_probs")
            else:
                s.do(nc.vector.reciprocal(RDEN, DEN))
                s.do(nc.vector.tensor_scalar(RDEN[:, 4:8], RDEN[:, 4:8], lam, None, ALU.mult))
                s.do(nc.vector.tensor_tensor(sc, sc, bc(RDEN.unsqueeze(2), [P, 8, keys]), ALU.mult))
                s.after(nc.vector.tensor_tensor(sc[:, 0:4, :], sc[:, 0:4, :], sc[:, 4:8, :], ALU.subtract)
                        .then_inc(sem("at_probs"), 1), "at_probs")
            yield
            if result:
                s.eng.wait_ge(sem("at_out"), n + 1)
                result()
            yield

        RELU = view(16560, IDX_H * S).rearrange("p (h s) -> p h s", h=IDX_H)
        OA = view(18608, T * D).rearrange("p (t d) -> p t d", t=T)
        KI2 = view(20656, T * P).rearrange("p (t c) -> p t c", t=T)
        ISC, WORK = view(20912, S), view(21168, S)
        SELB = view(21424, T * S).rearrange("p (t s) -> p t s", t=T)
        TOP8, KSS = small(8), small(T)

        def trig_tables(s_dve, s_act):
            a3 = [x.rearrange("p (t f) -> p t f", t=T) for x in (T_ANG, T_K)]
            c1, c2 = 6.28125, 2 * math.pi - 6.28125
            c2 = float(np.float32(int(c2 * 2 ** 21) / 2 ** 21))
            c3 = 2 * math.pi - c1 - c2
            magic = 1.5 * 2 ** 23
            if s_dve:
                s = s_dve
                s.do(nc.vector.tensor_copy(POSF, pos_t[:, :]))
                s.do(nc.vector.tensor_tensor(a3[0], bc(POSF.unsqueeze(2), [P, T, 24]),
                                             bc(FREQ.unsqueeze(1), [P, T, 24]), ALU.mult))
                for quarter, dst in ((0.0, SIN), (0.25, COS)):
                    s.do(nc.vector.tensor_scalar(T_K, T_ANG, 1 / (2 * math.pi), quarter, ALU.mult, ALU.add))
                    s.do(nc.vector.tensor_scalar(T_K, T_K, magic, None, ALU.add))
                    s.do(nc.vector.tensor_scalar(T_K, T_K, magic, None, ALU.subtract))
                    s.do(nc.vector.scalar_tensor_tensor(dst, T_K, -c1, T_ANG, ALU.mult, ALU.add))
                    s.do(nc.vector.scalar_tensor_tensor(dst, T_K, -c2, dst, ALU.mult, ALU.add))
                    s.do(nc.vector.scalar_tensor_tensor(dst, T_K, -c3, dst, ALU.mult, ALU.add))
                    if quarter:
                        s.do(nc.vector.tensor_scalar(dst, dst, math.pi / 2, None, ALU.add))
                    s.do(nc.vector.tensor_scalar(dst, dst, 3.1415925, -3.1415925, ALU.min, ALU.max))
                s.after(nc.vector.tensor_copy(POSF, POSF).then_inc(sem("angles"), 1), "angles")
            else:
                s = s_act
                s.eng.wait_ge(sem("angles"), 1)
                s.do(nc.scalar.activation(SIN, SIN, ACT.Sin))
                s.after(nc.scalar.activation(COS, COS, ACT.Sin).then_inc(sem("tables"), 1), "tables")

        def rope(s, v, half, f0, tmp):
            heads = v.shape[2]
            cos, sin = [bc(x.rearrange("p (t f) -> p t f", t=T)[:, :, f0:f0 + half].unsqueeze(2), [P, T, heads, half])
                        for x in (COS, SIN)]
            a, b = v[:, :, :, 0:half], v[:, :, :, half:2 * half]
            t1, t2 = [x[:, 0:T * heads * half].rearrange("p (t h f) -> p t h f", t=T, h=heads) for x in tmp]
            for t in range(T):
                at, bt, ct, st, u, w = a[:, t], b[:, t], cos[:, t], sin[:, t], t1[:, t], t2[:, t]
                s.do(nc.vector.tensor_tensor(u, at, ct, ALU.mult))
                s.do(nc.vector.tensor_tensor(w, at, st, ALU.mult))
                s.do(nc.vector.tensor_tensor(at, bt, st, ALU.mult))
                s.do(nc.vector.tensor_tensor(bt, bt, ct, ALU.mult))
                s.do(nc.vector.tensor_tensor(at, u, at, ALU.subtract))
                s.do(nc.vector.tensor_tensor(bt, bt, w, ALU.add))

        def dsa_blocks():
            b = [(lambda t, h=h: U[:, t, h * DH:(h + 1) * DH]) for h in range(HQ + HKV)]
            b += [(lambda t, i=i: U[:, t, QI0 + i * P:QI0 + (i + 1) * P]) for i in range(4)]
            return b + [lambda t: KI2[:, t, :]]

        DSA_STEPS = 3 + 2 + 2 * ATTN_STEPS

        def dsa_pe(pe, L, n0):
            yield
            pe.wait_ge(signal("dsa_roped"), reached("dsa_roped", L + 1))
            blocks = dsa_blocks()
            transposes(blocks[0:8], 4).then_inc(sem("dsa_transposed"), 1)
            yield
            pe.wait_ge(sem("dsa_TT"), 2 * L + 1)
            transposes(blocks[8:15], 4).then_inc(sem("dsa_transposed"), 1)
            yield
            for t in range(T):
                if t == 0:
                    pe.wait_ge(sem("dsa_TT"), 2 * L + 2)
                else:
                    pe.wait_ge(sem("dsa_relu"), 2 * L + 1)
                for h in range(IDX_H):
                    r = slice(64 * (h % 2), 64 * (h % 2) + 64)
                    c = (h // 2 % 2) * S
                    last = nc.tensor.matmul(PS[:, 4 + 2 * (h % 2) + h // 4, c:c + (t + 1) * P],
                                            TT[r, 10 + h // 2, t * P:(t + 1) * P], TT[r, 14, 0:(t + 1) * P],
                                            start=True, stop=True)
                last.then_inc(sem("dsa_raw"), 1)
                yield
            for t in range(T):
                if t == 0:
                    pe.wait_ge(sem("dsa_relu"), 2 * L + 2)
                else:
                    pe.wait_ge(sem("dsa_out"), 2 * L + t)
                yield from attn_pe(pe, n0 + t, t, [(TT[:, h, :], TT[:, 8 + h // 4, :]) for h in range(HQ)],
                                   lambda h, j: U[:, j, V0 + (h // 4) * DH:V0 + (h // 4 + 1) * DH], HQ)

        def dsa_act(s, L, n0):
            s.do(nc.scalar.activation(KI2[:, :, 0:IDX_D], U[:, :, KI0:KI0 + IDX_D], ACT.Square))
            s.after(nc.scalar.activation(KI2[:, :, IDX_D:P], U[:, :, KI0:KI0 + IDX_D], ACT.Copy)
                    .then_inc(signal("dsa_ksq"), 1), "dsa_ksq")
            s.eng.wait_ge(signal("dsa_kms"), reached("dsa_kms", L + 1))
            s.after(nc.scalar.activation(KSS, KSS, ACT.Sqrt).then_inc(signal("dsa_kroot"), 1), "dsa_kroot")
            yield
            for i, (a, b) in enumerate(((0, 8), (8, 15))):
                s.eng.wait_ge(sem("dsa_transposed"), 2 * L + i + 1)
                s.after(nc.scalar.activation(TT[:, a:b, :], banks(4, 4).rearrange("p (b s) -> p b s", b=8)[:, 0:b - a, :],
                                             ACT.Copy).then_inc(sem("dsa_TT"), 1), "dsa_TT")
                yield
            for t in range(T):
                s.eng.wait_ge(sem("dsa_raw"), 2 * L + t + 1)
                if t == 1:
                    s.eng.wait_ge(sem("dsa_index"), 2 * L + 1)
                s.after(nc.scalar.activation(
                    RELU[:, :, 0:(t + 1) * P], banks(4, 4).rearrange("p (h s) -> p h s", h=8)[:, :, 0:(t + 1) * P],
                    ACT.Relu).then_inc(sem("dsa_relu"), 1), "dsa_relu")
                yield
            for t in range(T):
                yield from attn_act(s, n0 + t, t, HQ, HQ)

        def dsa_pool(s, L):
            for t in range(T):
                s.eng.wait_ge(sem("dsa_index"), 2 * L + t + 1)
                v = ISC[:, 0:(t + 1) * P]
                s.after(nc.gpsimd.affine_select(out=v, in_=v, compare_op=ALU.is_ge, fill=NONCAUSAL, base=t * P,
                                                pattern=[[-1, (t + 1) * P]], channel_multiplier=1)
                        .then_inc(sem("dsa_edge"), 1), "dsa_edge")

        def dsa_dve(s, L, n0):
            if L == 0:
                s.eng.wait_ge(sem("tables"), 1)
            s.eng.wait_ge(signal("dsa_ksq"), reached("dsa_ksq", L + 1))
            s.do(nc.vector.tensor_reduce(KSS, KI2[:, :, 0:IDX_D], AX.X, ALU.add))
            s.after(nc.vector.tensor_scalar(KSS, KSS, 1.0 / IDX_D, EPS, ALU.mult, ALU.add).then_inc(signal("dsa_kms"), 1), "dsa_kms")
            s.eng.wait_ge(signal("dsa_kroot"), reached("dsa_kroot", L + 1))
            s.do(nc.vector.reciprocal(KSS, KSS))
            ki = U[:, :, KI0:KI0 + IDX_D]
            s.do(nc.vector.tensor_tensor(ki, ki, bc(KSS.unsqueeze(2), [P, T, IDX_D]), ALU.mult))
            s.do(nc.vector.tensor_tensor(ki, ki, bc(R_KI[:, L * IDX_D:(L + 1) * IDX_D].unsqueeze(1), [P, T, IDX_D]),
                                         ALU.mult))
            tmp = [view(14512, 512), view(15024, 512)]
            rope(s, U[:, :, 0:V0].rearrange("p t (h d) -> p t h d", d=DH), ROT // 2, 0, tmp)
            rope(s, U[:, :, QI0:WI0].rearrange("p t (h d) -> p t h d", d=IDX_D), IDX_ROT // 2, ROT // 2, tmp)
            s.do(nc.vector.tensor_copy(KI2[:, :, 0:IDX_D], ki))
            s.do(nc.vector.tensor_copy(KI2[:, :, IDX_D:P], ki))
            wi = U[:, :, WI0:WI0 + IDX_H]
            s.after(nc.vector.tensor_scalar(wi, wi, IDX_H ** -0.5 * IDX_D ** -0.5, None, ALU.mult).then_inc(signal("dsa_roped"), 1), "dsa_roped")
            for _ in range(3):
                yield
            for t in range(T):
                keys = (t + 1) * P
                s.eng.wait_ge(sem("dsa_relu"), 2 * L + t + 1)
                r = RELU[:, :, 0:keys]
                for hp in range(2):
                    rr = RELU[:, 4 * hp:4 * hp + 4, 0:keys]
                    s.do(nc.vector.tensor_tensor(rr, rr, bc(wi[:, t, hp::2].unsqueeze(2), [P, 4, keys]), ALU.mult))
                s.after(nc.vector.tensor_reduce(ISC[:, 0:keys], r.rearrange("p h k -> p k h"), AX.X, ALU.add).then_inc(sem("dsa_index"), 1), "dsa_index")
                s.eng.wait_ge(sem("dsa_edge"), 2 * L + t + 1)
                cur = ISC[:, 0:keys]
                for _ in range(TOPK // 8):
                    s.do(nc.vector.max(TOP8, cur))
                    s.do(nc.vector.match_replace(out=WORK[:, 0:keys], in_to_replace=TOP8, in_values=cur,
                                                 imm_value=TAKEN))
                    cur = WORK[:, 0:keys]
                s.do(nc.vector.tensor_scalar(cur, cur, TAKEN, NEG, ALU.not_equal, ALU.mult))
                s.do(nc.vector.tensor_tensor(SELB[:, t, 0:keys], cur, CB[:, t, 0:keys], ALU.add))
                yield

            def result(t):
                s.after(nc.vector.tensor_tensor(OA[:, t, :].rearrange("p (h d) -> p h d", h=HQ),
                                                banks(4, 2).rearrange("p (h d) -> p h d", h=HQ),
                                                bc(RDEN.unsqueeze(2), [P, HQ, DH]), ALU.mult)
                        .then_inc(sem("dsa_out"), 1), "dsa_out")
                if t == 1:
                    s.do(nc.vector.tensor_tensor(OA, OA, U[:, :, Z0:Z0 + D], ALU.mult))

            for t in range(T):
                yield from attn_dve(s, n0 + t, t, HQ, DH ** -0.5, SELB[:, t, 0:(t + 1) * P], lambda t=t: result(t))

        def mix_pe(pe, name, L, k):
            blocks = [(lambda t, j=j: MIX[:, t, j * P:(j + 1) * P]) for j in range(KD)]
            pe.wait_ge(sem("mix_ready"), 2 * k + 1)
            transposes(blocks[0:4], 4).then_inc(sem("mix_transposed"), 1)
            pe.wait_ge(sem("mix_ready"), 2 * k + 2)
            transposes(blocks[4:8], 6).then_inc(sem("mix_transposed"), 1)
            pe.wait_ge(sem("mixT_ready"), 2 * k + 2)
            for g in group(name, L):
                gemm(pe, g, ht_lhs)

        def mix_act(s, k):
            for half in range(2):
                s.eng.wait_ge(sem("mix_transposed"), 2 * k + half + 1)
                s.after(nc.scalar.activation(HT[:, 4 * half:4 * half + 4, :],
                                             banks(4 + 2 * half, 2).rearrange("p (k s) -> p k s", k=4), ACT.Copy)
                        .then_inc(sem("mixT_ready"), 1), "mixT_ready")

        def residual_dve(s, name, L):
            gs = group(name, L)
            for i, g in enumerate(gs):
                d = TILES[g]
                s.eng.wait_ge(sem("weights_used"), used(d["end"] - 1))
                xs = X[:, :, d["c0"]:d["c0"] + d["n"]]
                s.after(nc.vector.tensor_tensor(xs, xs, acc(g)[:, :, 0:d["n"]], ALU.add).then_inc(sem("gemm_out_dve"), 1), "gemm_out_dve")
            s.after(nc.vector.tensor_copy(SS[:, 0:1], SS[:, 0:1]).then_inc(sem("x_updated"), 1), "x_updated")

        def gate_dve(s):
            for half in range(2):
                c = slice(512 * half, 512 * half + 512)
                s.after(nc.vector.tensor_tensor(MIX[:, :, c], MIX[:, :, c], OA[:, :, c], ALU.add)
                        .then_inc(sem("mix_ready"), 1), "mix_ready")
        U2 = view(0, T * COLS2).rearrange("p (t c) -> p t c", t=T)
        SQ2 = view(16560, T * 1152).rearrange("p (t c) -> p t c", t=T)
        KDUP = view(18864, T * 256).rearrange("p (t w r d) -> p t w r d", t=T, w=2, r=2)
        CX = view(12464, CMP_L * 32).rearrange("p (l m) -> p l m", l=CMP_L)
        HID4 = view(13488, 512).rearrange("p (g r n) -> p g r n", g=4, r=4)
        KCD = view(14000, P).rearrange("p (r d) -> p r d", r=2)
        KCT, VBD = view(14128, P), view(14256, 256)
        CS = view(14512, 256).rearrange("p (t h n) -> p t h n", t=T, h=4)
        PCT = view(14768, 256).rearrange("p (t q) -> p t q", t=T)
        O8 = view(21936, 512).rearrange("p (m d) -> p m d", m=8)
        STATS = small(52)
        ST64 = STATS[:, 0:20].rearrange("p (t g) -> p t g", t=T)
        ST32 = STATS[:, 20:52].rearrange("p (t g) -> p t g", t=T)
        GATES = small(T * 12)
        HSB = view(15024, 256)
        KCS, RG8 = small(1), small(8)
        LAMP, LAMS, LAMC = small(64), small(2), small(DEPTH)
        CMAX, CSUM = small(8), small(8)
        OST = small(T * 12)
        G12 = rows(DEPTH * 192).rearrange("p (l m d) -> p l m d", l=DEPTH, m=3)

        def lam_init(L):
            return 0.8 - 0.6 * math.exp(-0.3 * L)

        def u_pe(pe, L, whole):
            for i, g in enumerate(group("u", L)):
                gemm(pe, g, ht_lhs, whole if i == 0 else None)

        def u_act(s, L):
            for g in group("u", L):
                d = TILES[g]
                s.eng.wait_ge(sem("weights_used"), used(d["end"] - 1))
                s.after(nc.scalar.activation(U2[:, :, d["c0"]:d["c0"] + d["n"]], acc(g)[:, :, 0:d["n"]], ACT.Copy).then_inc(sem("gemm_out_act"), 1), "gemm_out_act")
                if d["c0"] < DV0 <= d["c0"] + d["n"]:
                    s.do(nc.scalar.activation(SQ2[:, :, 0:640], U2[:, :, 0:640], ACT.Square))
                    s.after(nc.scalar.activation(SQ2[:, :, 640:1152], U2[:, :, DQ0:DV0], ACT.Square)
                            .then_inc(signal("m_squares"), 1), "m_squares")
                    s.eng.wait_ge(signal("m_means"), reached("m_means", L + 1))
                    s.after(nc.scalar.activation(STATS, STATS, ACT.Sqrt).then_inc(signal("m_roots"), 1), "m_roots")

        def mixer_blocks():
            b = [(lambda t, i=i: U2[:, t, NQ0 + i * P:NQ0 + (i + 1) * P]) for i in range(2)]
            b += [(lambda t, i=i: KDUP[:, t, i].rearrange("p r d -> p (r d)")) for i in range(2)]
            b += [lambda t: U2[:, t, KC0:KC0 + P]]
            b += [(lambda t, c=c: U2[:, t, c:c + P]) for c in
                  (DQ0, DQ0 + P, DK0, DK0 + P, GQ0, GK0, RQ0, RQ0 + P, RF0, RF0 + P)]
            return b + [lambda t: U2[:, t, GLR0:GLR0 + 16]]

        ORDER = (0, 2, 1, 3)

        def heads2(ap, w):
            return ap.rearrange("p (hh hp d) -> p hp hh d", hh=2, hp=2)

        def nsa_map(h, block, key):
            r = slice(64 * (h % 2), 64 * (h % 2) + 64)
            return TT[r, h // 2, :], TT[r, key, :]

        NSA_MAPS = [(h, kind) for hp in range(2) for kind in range(2) for h in (hp, hp + 2)]

        def diff_map(h, c):
            f = 64 * h + 32 * c
            r = slice(f % P, f % P + 32)
            return TT[r, 5 + f // P, :], TT[r, 7 + f // P, :]

        def prep_pe(pe, L):
            pe.wait_ge(signal("m_normed"), reached("m_normed", L + 1))
            blocks = mixer_blocks()
            transposes(blocks[0:8], 0)
            transposes(blocks[8:16], 4).then_inc(sem("m_transposed"), 1)

        MIXER_STEPS = 11 + 4 * ATTN_STEPS

        def mixers_pe(pe, L, n0):
            yield
            pe.wait_ge(signal("cmp_x"), reached("cmp_x", L + 1))
            for q in range(4):
                n = CMPW[L] + q
                landed(pe, n)
                w = half_view(n, (8, 256))
                for l in range(8):
                    last = nc.tensor.matmul(PS[0:32, 4, 0:256], CX[:, 8 * q + l, :], w[:, l, :], start=q + l == 0,
                                            stop=q == 3 and l == 7)
                last.then_inc(sem("weights_used"), 1)
                if q % 2:
                    yield
            pe.wait_ge(signal("cmp_silu"), reached("cmp_silu", L + 1))
            for half in range(2):
                last = nc.tensor.transpose(PS[:, 5, 32 * half:32 * half + 32], HSB[0:32, half * P:(half + 1) * P],
                                           IDENT[0:32, 0:32])
            last.then_inc(signal("cmp_hT"), 1)
            yield
            pe.wait_ge(signal("cmp_hid"), reached("cmp_hid", L + 1))
            for j in range(2):
                for half in range(2):
                    last = nc.tensor.matmul(PS[:, 4 + j, 0:HD], HID4[:, 2 * j + half].rearrange("p r n -> p (r n)"),
                                            W2[:, L, j, half, :], start=half == 0, stop=half == 1)
            last.then_inc(signal("cmp_kv"), 1)
            yield
            yield
            pe.wait_ge(signal("cmp_k"), reached("cmp_k", L + 1))
            nc.tensor.transpose(PS[:, 6, 0:P], KCD.rearrange("p r d -> p (r d)"), IDENT).then_inc(signal("cmp_kT"), 1)
            yield
            pe.wait_ge(signal("cmp_kT_out"), reached("cmp_kT_out", L + 1))
            for h in range(4):
                r = slice(64 * (h % 2), 64 * (h % 2) + 64)
                for t in range(T):
                    c = (2 * t + h // 2) * 32
                    last = nc.tensor.matmul(PS[:, 6 + h % 2, c:c + 32], TT[r, h // 2, t * P:(t + 1) * P],
                                            KCT[r, 0:32], start=True, stop=True)
            last.then_inc(signal("cmp_scores"), 1)
            yield
            yield
            pe.wait_ge(signal("cmp_probs"), reached("cmp_probs", L + 1))
            for t in range(T):
                last = nc.tensor.transpose(PS[:, 4, t * P:(t + 1) * P], CS[:, t].rearrange("p h n -> p (h n)"), IDENT)
            last.then_inc(signal("cmp_pT"), 1)
            yield
            pe.wait_ge(signal("cmp_pT_out"), reached("cmp_pT_out", L + 1))
            for t in range(T):
                last = nc.tensor.matmul(PS[:, 5, t * 256:(t + 1) * 256], PCT[:, t, :], VBD, start=True, stop=True)
            last.then_inc(signal("cmp_out"), 1)
            yield
            pe.wait_ge(signal("cmp_done"), reached("cmp_done", L + 1))
            for t in range(T):
                n = n0 + t
                if t:
                    pe.wait_ge(sem("nsa_out"), 2 * L + t)
                yield from attn_pe(pe, n, t, [nsa_map(h, 0, 2 + kind) for h, kind in NSA_MAPS],
                                   lambda m, j: U2[:, j, (VS0, VW0)[NSA_MAPS[m][1]]:(VS0, VW0)[NSA_MAPS[m][1]] + HD], 8)
            pe.wait_ge(sem("nsa_out"), 2 * L + 2)
            for t in range(T):
                n = n0 + 2 + t
                if t:
                    pe.wait_ge(sem("diff_out"), 2 * L + t)
                yield from attn_pe(pe, n, t, [diff_map(h, c) for c in range(2) for h in ORDER],
                                   lambda m, j: U2[:, j, DV0 + HD * ORDER[m]:DV0 + HD * (ORDER[m] + 1)], 4)

        def prep_act(s, L):
            s.eng.wait_ge(sem("m_transposed"), L + 1)
            s.after(nc.scalar.activation(TT[:, 8:15, :], banks(4, 4).rearrange("p (b s) -> p b s", b=8)[:, 0:7, :],
                                        ACT.Copy).then_inc(sem("m_TT"), 1), "m_TT")
            s.after(nc.scalar.activation(TT[0:16, 15, :], PS[0:16, 7, S:2 * S], ACT.Copy).then_inc(sem("m_TT"), 1), "m_TT")
            s.after(nc.scalar.activation(TT[:, 0:8, :], banks(0, 4).rearrange("p (b s) -> p b s", b=8), ACT.Copy).then_inc(sem("m_TT"), 1), "m_TT")
            s.do(nc.scalar.activation(GATES.rearrange("p (t g) -> p t g", t=T), U2[:, :, NG0:NG0 + 12], ACT.Sigmoid))
            for c in (GOG0, ROG0):
                ins = nc.scalar.activation(U2[:, :, c:c + 256], U2[:, :, c:c + 256], ACT.Silu)
                if c == GOG0:
                    s.do(ins)
                else:
                    s.after(ins.then_inc(sem("m_gates"), 1), "m_gates")

        def mixers_act(s, L, n0):
            yield
            yield
            s.eng.wait_ge(sem("weights_used"), used(CMPW[L] + 3))
            s.after(nc.scalar.activation(HSB[0:32, :], PS[0:32, 4, 0:256], ACT.Silu).then_inc(signal("cmp_silu"), 1), "cmp_silu")
            yield
            yield
            s.eng.wait_ge(signal("cmp_kv"), reached("cmp_kv", L + 1))
            s.after(nc.scalar.activation(KCD[:, 0, :], PS[:, 4, 0:HD], ACT.Square, accum_out=KCS).then_inc(signal("cmp_ksq"), 1), "cmp_ksq")
            yield
            s.eng.wait_ge(signal("cmp_kms"), reached("cmp_kms", L + 1))
            s.after(nc.scalar.activation(KCS, KCS, ACT.Sqrt).then_inc(signal("cmp_kroot"), 1), "cmp_kroot")
            yield
            s.eng.wait_ge(signal("cmp_kT"), reached("cmp_kT", L + 1))
            s.after(nc.scalar.activation(KCT, PS[:, 6, 0:P], ACT.Copy).then_inc(signal("cmp_kT_out"), 1), "cmp_kT_out")
            yield
            s.eng.wait_ge(signal("cmp_scores"), reached("cmp_scores", L + 1))
            for hp in range(2):
                ins = nc.scalar.activation(CS.rearrange("p t (hh hp) n -> p t hh hp n", hp=2)[:, :, :, hp, :],
                                           PS[:, 6 + hp, 0:P].rearrange("p (t h n) -> p t h n", t=T, h=2),
                                           ACT.Copy, scale=HD ** -0.5)
                if hp == 0:
                    s.do(ins)
                else:
                    s.after(ins.then_inc(signal("cmp_scaled"), 1), "cmp_scaled")
            yield
            s.eng.wait_ge(signal("cmp_shifted"), reached("cmp_shifted", L + 1))
            s.after(nc.scalar.activation(CS, CS, ACT.Exp).then_inc(signal("cmp_exp"), 1), "cmp_exp")
            yield
            s.eng.wait_ge(signal("cmp_pT"), reached("cmp_pT", L + 1))
            s.after(nc.scalar.activation(PCT, PS[:, 4, 0:2 * P].rearrange("p (t q) -> p t q", t=T), ACT.Copy).then_inc(signal("cmp_pT_out"), 1), "cmp_pT_out")
            yield
            yield
            for t in range(T):
                yield from attn_act(s, n0 + t, t, 8, 8)

            def diff_result(t):
                s.after(nc.scalar.activation(
                    heads2(MIX[:, t, 256:512], HD), PS[:, 4, 0:256].rearrange("p (hp hh d) -> p hp hh d", hp=2, hh=2),
                    ACT.Copy).then_inc(sem("diff_out"), 1), "diff_out")

            for t in range(T):
                yield from attn_act(s, n0 + 2 + t, t, 8, 4, lambda t=t: diff_result(t))

        def gain(row, groups):
            w = row.shape[1]
            return bc(row.unsqueeze(1).unsqueeze(1), [P, T, groups, w])

        def nsa_gain(L, i):
            return R_NSA[:, (4 * L + i) * HD:(4 * L + i + 1) * HD]

        def prep_dve(s, L):
            s.eng.wait_ge(signal("m_squares"), reached("m_squares", L + 1))
            s.do(nc.vector.tensor_reduce(ST64, SQ2[:, :, 0:640].rearrange("p t (g d) -> p t g d", d=64), AX.X, ALU.add))
            s.do(nc.vector.tensor_reduce(ST32, SQ2[:, :, 640:1152].rearrange("p t (g d) -> p t g d", d=32), AX.X,
                                         ALU.add))
            s.do(nc.vector.tensor_scalar(ST64, ST64, 1.0 / 64, EPS, ALU.mult, ALU.add))
            s.after(nc.vector.tensor_scalar(ST32, ST32, 1.0 / 32, EPS, ALU.mult, ALU.add).then_inc(signal("m_means"), 1), "m_means")
            s.eng.wait_ge(signal("m_roots"), reached("m_roots", L + 1))
            s.do(nc.vector.reciprocal(STATS, STATS))

            q = U2[:, :, NQ0:KC0].rearrange("p t (g d) -> p t g d", d=HD)
            s.do(nc.vector.tensor_tensor(q, q, bc(ST64[:, :, 0:4].unsqueeze(3), [P, T, 4, HD]), ALU.mult))
            s.do(nc.vector.tensor_tensor(q, q, gain(nsa_gain(L, 0), 4), ALU.mult))
            for i, (c, g) in enumerate(((KS0, 6), (KW0, 8))):
                src = bc(U2[:, :, c:c + HD].unsqueeze(2), [P, T, 2, HD])
                s.do(nc.vector.tensor_tensor(KDUP[:, :, i], src, bc(ST64[:, :, g:g + 1].unsqueeze(3), [P, T, 2, HD]),
                                             ALU.mult))
                s.do(nc.vector.tensor_tensor(KDUP[:, :, i], KDUP[:, :, i], gain(nsa_gain(L, 2 + i), 2), ALU.mult))
            for i, c in enumerate((DQ0, DK0)):
                v = U2[:, :, c:c + 256].rearrange("p t (g d) -> p t g d", d=32)
                s.do(nc.vector.tensor_tensor(v, v, bc(ST32[:, :, 8 * i:8 * i + 8].unsqueeze(3), [P, T, 8, 32]), ALU.mult))
                ins = nc.vector.tensor_tensor(v, v, gain(R_DQK[:, (2 * L + i) * 32:(2 * L + i + 1) * 32], 8), ALU.mult)
                if i == 0:
                    s.do(ins)
                else:
                    s.after(ins.then_inc(signal("m_normed"), 1), "m_normed")

        def mixers_dve(s, L, n0):
            s.eng.wait_ge(sem("m_TT"), 3 * L + 3)
            blocks = TT[:, 4, :].rearrange("p (n b) -> p b n", b=CMP_S)
            s.do(nc.vector.memset(CX, 0.0))
            for a, j in ((0, 0), (0, 1), (1, 0), (1, 1)):
                pr = slice(64 * j, 64 * j + 64)
                ins = nc.vector.tensor_tensor(
                    CX[pr, a * CMP_S:(a + 1) * CMP_S, 16 * j:16 * j + NCMP], blocks[pr, :, a:a + NCMP],
                    bc(CMPPOS[pr, L * CMP_L + a * CMP_S:L * CMP_L + (a + 1) * CMP_S].unsqueeze(2), [64, CMP_S, NCMP]),
                    ALU.add)
                if a * j == 0:
                    s.do(ins)
                else:
                    s.after(ins.then_inc(signal("cmp_x"), 1), "cmp_x")
            s.do(nc.vector.memset(HID4, 0.0))
            s.do(nc.vector.memset(VBD, 0.0))
            yield
            yield
            yield
            s.eng.wait_ge(signal("cmp_hT"), reached("cmp_hT", L + 1))
            hid = PS[:, 5, 0:64].rearrange("p (half j n) -> p j half n", half=2, j=2)
            for j in range(2):
                ins = nc.vector.tensor_copy(HID4[:, 2 * j:2 * j + 2, :, 0:NCMP],
                                            bc(hid[:, j, :, 0:NCMP].unsqueeze(2), [P, 2, 4, NCMP]))
                if j == 0:
                    s.do(ins)
                else:
                    s.after(ins.then_inc(signal("cmp_hid"), 1), "cmp_hid")
            yield
            yield
            s.eng.wait_ge(signal("cmp_ksq"), reached("cmp_ksq", L + 1))
            s.after(nc.vector.tensor_scalar(KCS, KCS, 1.0 / HD, EPS, ALU.mult, ALU.add).then_inc(signal("cmp_kms"), 1), "cmp_kms")
            yield
            s.eng.wait_ge(signal("cmp_kroot"), reached("cmp_kroot", L + 1))
            s.do(nc.vector.reciprocal(KCS, KCS))
            s.do(nc.vector.scalar_tensor_tensor(KCD[:, 0, :], PS[:, 4, 0:HD], KCS, nsa_gain(L, 1), ALU.mult, ALU.mult))
            s.after(nc.vector.tensor_copy(KCD[:, 1, :], KCD[:, 0, :]).then_inc(signal("cmp_k"), 1), "cmp_k")
            for h in range(4):
                r = slice(32 * h, 32 * h + 32)
                s.do(nc.vector.tensor_copy(VBD[r, HD * h:HD * (h + 1)], PS[r, 5, 0:HD]))
            yield
            yield
            s.eng.wait_ge(signal("cmp_scaled"), reached("cmp_scaled", L + 1))
            s.do(nc.vector.tensor_tensor(CS, CS, bc(CBIAS.unsqueeze(2), [P, T, 4, 32]), ALU.add))
            c8 = CS.rearrange("p t h n -> p (t h) n")
            s.do(nc.vector.tensor_reduce(CMAX, c8, AX.X, ALU.max))
            s.after(nc.vector.tensor_tensor(c8, c8, bc(CMAX.unsqueeze(2), [P, 8, 32]), ALU.subtract).then_inc(signal("cmp_shifted"), 1), "cmp_shifted")
            yield
            s.eng.wait_ge(signal("cmp_exp"), reached("cmp_exp", L + 1))
            s.do(nc.vector.tensor_reduce(CSUM, c8, AX.X, ALU.add))
            s.do(nc.vector.reciprocal(CSUM, CSUM))
            s.do(nc.vector.tensor_tensor(c8, c8, bc(CSUM.unsqueeze(2), [P, 8, 32]), ALU.mult))
            s.after(nc.vector.tensor_tensor(CS, CS, bc(COK.unsqueeze(2), [P, T, 4, 32]), ALU.mult).then_inc(signal("cmp_probs"), 1), "cmp_probs")
            yield
            s.eng.wait_ge(sem("m_gates"), L + 1)
            g3 = GATES.rearrange("p (t h k) -> p t h k", t=T, k=3)
            s.eng.wait_ge(signal("cmp_out"), reached("cmp_out", L + 1))
            s.after(nc.vector.tensor_tensor(MIX[:, :, 0:256].rearrange("p t (h d) -> p t h d", h=4),
                                           PS[:, 5, :].rearrange("p (t h d) -> p t h d", t=T, h=4),
                                           bc(g3[:, :, :, 0:1], [P, T, 4, HD]), ALU.mult).then_inc(signal("cmp_done"), 1), "cmp_done")
            yield

            def nsa_result(t):
                s.do(nc.vector.tensor_tensor(
                    RG8.rearrange("p (a k b) -> p a k b", a=2, k=2), RDEN.rearrange("p (a k b) -> p a k b", a=2, k=2),
                    GATES[:, 12 * t:12 * t + 12].rearrange("p (hh hp k) -> p hp k hh", hh=2, hp=2)[:, :, 1:3, :],
                    ALU.mult))
                s.after(nc.vector.tensor_tensor(O8, PS[:, 4, :].rearrange("p (m d) -> p m d", m=8),
                                                bc(RG8.unsqueeze(2), [P, 8, HD]), ALU.mult)
                        .then_inc(sem("nsa_out"), 1), "nsa_out")
                mv = heads2(MIX[:, t, 0:256], HD)
                for kind in range(2):
                    s.do(nc.vector.tensor_tensor(mv, mv, O8.rearrange("p (hp k hh) d -> p hp k hh d", hp=2, k=2)
                                                 [:, :, kind], ALU.add))

            for t in range(T):
                yield from attn_dve(s, n0 + t, t, 8, HD ** -0.5, CB[:, t, 0:(t + 1) * P], lambda t=t: nsa_result(t))
            for t in range(T):
                yield from attn_dve(s, n0 + 2 + t, t, 8, 32 ** -0.5, CB[:, t, 0:(t + 1) * P], lam=LAMC[:, L:L + 1])

        GE = [view(a, 8 * S).rearrange("p (l s) -> p l s", l=8) for a in (16560, 18608)]
        MASKED = view(20656, 8 * P)
        AA = [view(6456 + 128 * i, P) for i in range(2)]
        ACR = [view(6712 + 128 * i, P) for i in range(2)]
        LOGF = view(6968, 3 * S).rearrange("p (f s) -> p f s", f=3)
        GLT, GLT2 = view(7992, S), view(21680, S)
        BSUM = [view(7736, S), GLT, GLT2]
        FAM = ((9, 10, GV0, (0, 1, 2, 3), 32, 512), (11, 13, RI0, (0, 1), 64, 768), (12, 14, RI0, (2, 3), 64, 768))
        UNITS = [(f, h, t) for f in range(3) for h in FAM[f][3] for t in range(T)]
        GLA_ORDER = ([("gaps", 0), ("factors", 0)] + [("unit", u) for u in range(4)] + [("exp", 1)]
                     + [("unit", u) for u in range(4, 10)] + [("exp", 2)]
                     + [("unit", u) for u in range(10, 16)])
        GLA_STEPS = 2 + len(GLA_ORDER) + 1

        def gaps(s, eng, f, name):
            for l in range(8):
                n = 1 << l
                b = BSUM[f].rearrange("p (b two n) -> p b two n", two=2, n=n)
                e = GE[f % 2][:, l, :].rearrange("p (b two n) -> p b two n", two=2, n=n)
                border = bc(b[:, :, 0, n - 1:n], [P, S // (2 * n), n])
                s.do(eng.tensor_tensor(e[:, :, 0, :], border, b[:, :, 0, :], ALU.subtract))
                if l < 7:
                    s.do(eng.tensor_tensor(e[:, :, 1, :], b[:, :, 1, :], border, ALU.subtract))
                else:
                    s.after(eng.tensor_copy(e[:, :, 1, :], b[:, :, 1, :]).then_inc(sem(name), 1), name)

        def factors(s, eng, f, name):
            for l in range(8):
                n = 1 << l
                e = GE[f % 2][:, l, :].rearrange("p (b two n) -> p b two n", two=2, n=n)
                q, k = [TT[:, FAM[f][i], :].rearrange("p (b two n) -> p b two n", two=2, n=n) for i in range(2)]
                s.do(eng.tensor_tensor(e[:, :, 0, :], e[:, :, 0, :], k[:, :, 0, :], ALU.mult))
                ins = eng.tensor_tensor(e[:, :, 1, :], e[:, :, 1, :], q[:, :, 1, :], ALU.mult)
                if l < 7:
                    s.do(ins)
                else:
                    s.after(ins.then_inc(sem(name), 1), name)

        def gla_pool(s, L):
            for f in (1, 2):
                if f == 1:
                    s.eng.wait_ge(sem("hg_sums"), L + 1)
                else:
                    s.eng.wait_ge(sem("gla_prod"), 16 * L + 8)
                gaps(s, nc.gpsimd, f, "hg_gaps")
                s.eng.wait_ge(sem("gla_exp"), 3 * L + f + 1)
                factors(s, nc.gpsimd, f, "hg_GE")

        def gla_pe(pe, L):
            pe.wait_ge(sem("m_TT"), 3 * L + 3)
            nc.tensor.matmul(PS[:, 2, S:2 * S], WG2[0:16, L * P:(L + 1) * P], TT[0:16, 15, :], start=True, stop=True)\
                .then_inc(sem("gla_z"), 1)
            yield
            yield

            def out(u):
                f, h, t = UNITS[u]
                v0 = FAM[f][2] + HD * h
                pe.wait_ge(sem("gla_A"), 16 * L + u + 1)
                if u == 8:
                    pe.wait_ge(sem("gla_first_out"), L + 1)
                dst = PS[:, 3, (4 * t + h) * HD:(4 * t + h + 1) * HD]
                last = nc.tensor.matmul(dst, AA[u % 2], U2[:, t, v0:v0 + HD], start=True, stop=t == 0)
                if t == 1:
                    pe.wait_ge(sem("gla_cross_out"), 8 * L + u // 2 + 1)
                    last = nc.tensor.matmul(dst, ACR[u // 2 % 2], U2[:, 0, v0:v0 + HD], start=False, stop=True)
                last.then_inc(sem("gla_out"), 1)

            for kind, u in GLA_ORDER:
                if kind != "unit":
                    yield
                    continue
                f, h, t = UNITS[u]
                w = FAM[f][4]
                r0 = (w * h) % P
                r, tok = slice(r0, r0 + w), slice(t * P, (t + 1) * P)
                if f == 0:
                    pe.wait_ge(sem("gla_GE"), L + 1)
                else:
                    pe.wait_ge(sem("hg_GE"), 2 * L + f)
                if u:
                    pe.wait_ge(sem("gla_read"), 16 * L + u)
                for l in range(LEVELS):
                    nc.tensor.matmul(PS[:, l // 4, (l % 4) * P:(l % 4 + 1) * P], GE[f % 2][r, l, tok],
                                     GE[f % 2][r, l, tok], start=True, stop=True)
                last = nc.tensor.matmul(PS[:, 1, 3 * P:4 * P], TT[r, FAM[f][1], tok], TT[r, FAM[f][0], tok],
                                        start=True, stop=True)
                if t == 1:
                    last = nc.tensor.matmul(PS[:, 2, (u // 2 % 2) * P:(u // 2 % 2 + 1) * P], GE[f % 2][r, 7, 0:P],
                                            GE[f % 2][r, 7, P:S], start=True, stop=True)
                last.then_inc(sem("gla_prod"), 1)
                if u:
                    out(u - 1)
                yield
            out(15)
            yield

        def gla_act(s, L):
            s.eng.wait_ge(signal("gla_zb"), reached("gla_zb", L + 1))
            s.do(nc.scalar.activation(GLT2, GLT, ACT.Abs))
            s.do(nc.scalar.activation(GLT2, GLT2, ACT.Exp, scale=-1.0))
            s.after(nc.scalar.activation(GLT2, GLT2, ACT.Ln, bias=1.0).then_inc(signal("gla_ln"), 1), "gla_ln")
            rf = TT[:, 13:15, :]
            s.do(nc.scalar.activation(LOGF[:, 1:3, :], rf, ACT.Sigmoid))
            s.after(nc.scalar.activation(rf, rf, ACT.Sigmoid, scale=-1.0).then_inc(signal("hg_sig"), 1), "hg_sig")
            yield
            s.eng.wait_ge(signal("hg_f"), reached("hg_f", L + 1))
            s.after(nc.scalar.activation(LOGF[:, 1:3, :], LOGF[:, 1:3, :], ACT.Ln).then_inc(signal("hg_ln"), 1), "hg_ln")
            yield

            def exponentials(f):
                if f == 0:
                    s.eng.wait_ge(sem("gla_gaps"), L + 1)
                else:
                    s.eng.wait_ge(sem("hg_gaps"), 2 * L + f)
                s.after(nc.scalar.activation(GE[f % 2], GE[f % 2], ACT.Exp).then_inc(sem("gla_exp"), 1), "gla_exp")

            for kind, u in GLA_ORDER:
                if kind in ("gaps", "exp"):
                    exponentials(u)
                elif kind == "unit":
                    if UNITS[u][2] == 1:
                        s.eng.wait_ge(sem("gla_prod"), 16 * L + u + 1)
                        if u >= 4:
                            s.eng.wait_ge(sem("gla_out"), 16 * L + u - 3)
                        s.after(nc.scalar.activation(ACR[u // 2 % 2], PS[:, 2, (u // 2 % 2) * P:(u // 2 % 2 + 1) * P],
                                                     ACT.Copy).then_inc(sem("gla_cross_out"), 1), "gla_cross_out")
                    if u == 8:
                        s.eng.wait_ge(sem("gla_out"), 16 * L + 8)
                        s.after(nc.scalar.activation(MIX[:, :, 512:768], PS[:, 3, :].rearrange("p (t c) -> p t c", t=T),
                                                     ACT.Copy).then_inc(sem("gla_first_out"), 1), "gla_first_out")
                yield
            s.eng.wait_ge(sem("gla_out"), 16 * L + 16)
            s.do(nc.scalar.activation(MIX[:, :, 768:D], PS[:, 3, :].rearrange("p (t c) -> p t c", t=T), ACT.Copy))
            yield

        def post_act(s, L):
            for t in range(T):
                ins = nc.scalar.activation(view(12464, T * 768).rearrange("p (t c) -> p t c", t=T)[:, t, :],
                                           MIX[:, t, 256:D], ACT.Square)
                if t == 0:
                    s.do(ins)
                else:
                    s.after(ins.then_inc(signal("m_osq"), 1), "m_osq")
            s.eng.wait_ge(signal("m_oms"), reached("m_oms", L + 1))
            s.after(nc.scalar.activation(OST, OST, ACT.Sqrt).then_inc(signal("m_oroot"), 1), "m_oroot")

        def gla_dve(s, L):
            s.eng.wait_ge(sem("gla_z"), L + 1)
            s.after(nc.vector.tensor_scalar(GLT, PS[:, 2, S:2 * S], GLAB[:, L:L + 1], None, ALU.add).then_inc(signal("gla_zb"), 1), "gla_zb")
            s.do(nc.vector.tensor_scalar(TT[:, 9, :], TT[:, 9, :], 32 ** -0.5, None, ALU.mult))
            yield
            s.eng.wait_ge(signal("gla_ln"), reached("gla_ln", L + 1))
            s.do(nc.vector.scalar_tensor_tensor(LOGF[:, 0, :], GLT, 0.0, GLT2, ALU.min, ALU.subtract))
            s.do(nc.vector.tensor_scalar(LOGF[:, 0, :], LOGF[:, 0, :], 1.0 / 16, None, ALU.mult))
            s.eng.wait_ge(signal("hg_sig"), reached("hg_sig", L + 1))
            for i in range(2):
                lb, one = LBC[:, 4 * i + L:4 * i + L + 1], LBC[:, 4 * i + 2 + L:4 * i + 3 + L]
                s.do(nc.vector.tensor_scalar(LOGF[:, 1 + i, :], LOGF[:, 1 + i, :], one, lb, ALU.mult, ALU.add))
                s.do(nc.vector.tensor_scalar(TT[:, 13 + i, :], TT[:, 13 + i, :], one, None, ALU.mult))
            s.after(nc.vector.tensor_scalar(LOGF[:, 1:3, :], LOGF[:, 1:3, :], 2.0 ** -63, None, ALU.max).then_inc(signal("hg_f"), 1), "hg_f")
            yield

            def sums(f):
                for t in range(T):
                    ins = nc.vector.tensor_tensor_scan(BSUM[f][:, t * P:(t + 1) * P], ONES,
                                                       LOGF[:, f, t * P:(t + 1) * P], 0.0, ALU.mult, ALU.add)
                    if (f, t) == (2, 1):
                        s.after(ins.then_inc(sem("hg_sums"), 1), "hg_sums")
                    else:
                        s.do(ins)

            for kind, u in GLA_ORDER:
                if kind == "gaps":
                    sums(0)
                    gaps(s, nc.vector, 0, "gla_gaps")
                elif kind == "factors":
                    s.eng.wait_ge(signal("hg_ln"), reached("hg_ln", L + 1))
                    sums(1)
                    sums(2)
                    s.eng.wait_ge(sem("gla_exp"), 3 * L + 1)
                    factors(s, nc.vector, 0, "gla_GE")
                elif kind == "unit":
                    s.eng.wait_ge(sem("gla_prod"), 16 * L + u + 1)
                    if u >= 2:
                        s.eng.wait_ge(sem("gla_out"), 16 * L + u - 1)
                    s.after(nc.vector.tensor_tensor(MASKED, banks(0, 2), mt_t[:, :], ALU.mult)
                            .then_inc(sem("gla_read"), 1), "gla_read")
                    s.after(nc.vector.tensor_reduce(AA[u % 2], MASKED.rearrange("p (l c) -> p c l", l=8), AX.X, ALU.add).then_inc(sem("gla_A"), 1), "gla_A")
                yield
            yield

        def post_dve(s, L):
            s.eng.wait_ge(signal("m_osq"), reached("m_osq", L + 1))
            s.do(nc.vector.tensor_reduce(OST, view(12464, T * 768).rearrange("p (g d) -> p g d", d=HD), AX.X, ALU.add))
            s.after(nc.vector.tensor_scalar(OST, OST, 1.0 / HD, EPS, ALU.mult, ALU.add).then_inc(signal("m_oms"), 1), "m_oms")
            s.eng.wait_ge(signal("m_oroot"), reached("m_oroot", L + 1))
            s.do(nc.vector.reciprocal(OST, OST))
            for t in range(T):
                o = MIX[:, t, 256:D].rearrange("p (g d) -> p g d", d=HD)
                s.do(nc.vector.tensor_tensor(o, o, bc(OST[:, 12 * t:12 * t + 12].unsqueeze(2), [P, 12, HD]), ALU.mult))
                o = MIX[:, t, 256:D].rearrange("p (m h d) -> p m h d", m=3, h=4)
                ins = nc.vector.tensor_tensor(o, o, bc(G12[:, L].unsqueeze(2), [P, 3, 4, HD]), ALU.mult)
                if t == 0:
                    s.do(ins)
                else:
                    s.after(ins.then_inc(sem("mix_ready"), 1), "mix_ready")
            s.do(nc.vector.tensor_tensor(MIX[:, :, 512:768], MIX[:, :, 512:768], U2[:, :, GOG0:GOG0 + 256], ALU.mult))
            s.after(nc.vector.tensor_tensor(MIX[:, :, 768:D], MIX[:, :, 768:D], U2[:, :, ROG0:ROG0 + 256], ALU.mult).then_inc(sem("mix_ready"), 1), "mix_ready")

        HFT = view(0, (FF // P) * S).rearrange("p (k s) -> p k s", s=S)
        SGF = [view(7168 + 1024 * i, 1024).rearrange("p (t c) -> p t c", t=T) for i in range(2)]
        HTOK = [view(9216 + 1024 * i, 1024).rearrange("p (t c) -> p t c", t=T) for i in range(2)]

        def ffn_pe(pe, L):
            gs = group("ffn", L)

            def turn(f):
                pe.wait_ge(sem("gemm_out_dve"), evacuated(gs[2 * f + 1])[1])
                if f >= 2:
                    pe.wait_ge(sem("ffn_HT"), f - 1)
                transposes([(lambda t, j=j: HTOK[f % 2][:, t, j * P:(j + 1) * P]) for j in range(4)], 4 + 2 * (f % 2))\
                    .then_inc(sem("ffn_T"), 1)

            for f in range(7):
                gemm(pe, gs[2 * f], ht_lhs)
                gemm(pe, gs[2 * f + 1], ht_lhs)
                if f:
                    turn(f - 1)
            turn(6)
            pe.wait_ge(sem("ffn_HT"), 7)
            for i in range(14):
                n = DOWN[L] + i
                landed(pe, n)
                w = half_view(n, (2, D))
                for k in range(2):
                    for t in range(T):
                        for dh in range(2):
                            last = nc.tensor.matmul(PS[:, 2 * t + dh, :], HFT[:, 2 * i + k, t * P:(t + 1) * P],
                                                    w[:, k, 512 * dh:512 * dh + 512], start=i + k == 0,
                                                    stop=i == 13 and k == 1)
                last.then_inc(sem("weights_used"), 1)

        def ffn_act(s, L):
            gs = group("ffn", L)

            def back(f):
                s.eng.wait_ge(sem("ffn_T"), f + 1)
                b = 4 + 2 * (f % 2)
                s.after(nc.scalar.activation(HFT[:, 4 * f:4 * f + 4, :], banks(b, 2).rearrange("p (k s) -> p k s", k=4),
                                            ACT.Copy).then_inc(sem("ffn_HT"), 1), "ffn_HT")

            for f in range(7):
                s.eng.wait_ge(sem("weights_used"), used(TILES[gs[2 * f]]["end"] - 1))
                if f >= 2:
                    s.eng.wait_ge(sem("gemm_out_dve"), evacuated(gs[2 * f - 3])[1])
                s.after(nc.scalar.activation(SGF[f % 2], acc(gs[2 * f]), ACT.Silu).then_inc(sem("gemm_out_act"), 1), "gemm_out_act")
                if f >= 2:
                    back(f - 2)
            back(5)
            back(6)

        def ffn_dve(s, L):
            gs = group("ffn", L)
            for f in range(7):
                g = gs[2 * f + 1]
                s.eng.wait_ge(sem("weights_used"), used(TILES[g]["end"] - 1))
                s.eng.wait_ge(sem("gemm_out_act"), evacuated(gs[2 * f])[1])
                if f >= 2:
                    s.eng.wait_ge(sem("ffn_T"), f - 1)
                s.after(nc.vector.tensor_tensor(HTOK[f % 2], SGF[f % 2], acc(g), ALU.mult).then_inc(sem("gemm_out_dve"), 1), "gemm_out_dve")
            s.eng.wait_ge(sem("weights_used"), used(DOWN[L] + 13))
            s.after(nc.vector.tensor_tensor(x_t[:, :], x_t[:, :], banks(0, 4), ALU.add).then_inc(sem("x_updated"), 1), "x_updated")

        PP = view(9216 + 2048, T * PLE).rearrange("p (t c) -> p t c", t=T)
        PPT = view(9216 + 2048 + 512, 2 * S).rearrange("p (k s) -> p k s", k=2)
        SGP = view(12464, T * D).rearrange("p (t c) -> p t c", t=T)
        TMP = view(14512, T * 512).rearrange("p (t c) -> p t c", t=T)

        def ple_pe(pe, L, whole):
            pe.wait_ge(sem("ple_loaded"), 16 * (L + 1))
            transposes([(lambda t, j=j: PP[:, t, j * P:(j + 1) * P]) for j in range(2)], 4).then_inc(sem("ple_T"), 1)
            for i, g in enumerate(group("pg", L)):
                gemm(pe, g, ht_lhs, whole if i == 0 else None)
            pe.wait_ge(sem("ple_pT"), L + 1)
            for g in group("pp", L):
                gemm(pe, g, lambda k, t: PPT[:, k, t * P:(t + 1) * P])

        def ple_act(s, L):
            s.eng.wait_ge(sem("ple_T"), L + 1)
            s.after(nc.scalar.activation(PPT, PS[:, 4, :].rearrange("p (k s) -> p k s", k=2), ACT.Copy).then_inc(sem("ple_pT"), 1), "ple_pT")
            for g in group("pg", L):
                d = TILES[g]
                s.eng.wait_ge(sem("weights_used"), used(d["end"] - 1))
                s.after(nc.scalar.activation(SGP[:, :, d["c0"]:d["c0"] + 512], acc(g), ACT.Sigmoid).then_inc(sem("gemm_out_act"), 1), "gemm_out_act")

        def ple_dve(s, L):
            s.eng.wait_ge(sem("gemm_out_act"), evacuated(group("pg", L)[-1])[1])
            for g in group("pp", L):
                d = TILES[g]
                c = slice(d["c0"], d["c0"] + 512)
                s.eng.wait_ge(sem("weights_used"), used(d["end"] - 1))
                s.after(nc.vector.tensor_tensor(TMP, SGP[:, :, c], acc(g), ALU.mult).then_inc(sem("gemm_out_dve"), 1), "gemm_out_dve")
                s.do(nc.vector.tensor_tensor(X[:, :, c], X[:, :, c], TMP, ALU.add))
            s.after(nc.vector.tensor_copy(SS[:, 0:1], SS[:, 0:1]).then_inc(sem("x_updated"), 1), "x_updated")

        SLOTS = 128
        PALL = view(0, T * NE * SLOTS).rearrange("p (t e s) -> p t e s", t=T, e=NE)
        WSEL = view(2048, T * NE * SLOTS).rearrange("p (t e s) -> p t e s", t=T, e=NE)
        PWT = view(4096, NE * S).rearrange("p (e s) -> p e s", e=NE)
        PWE = view(6144, S)
        XG = view(6400, KD * SLOTS).rearrange("p (k s) -> p k s", k=KD)
        HET = view(7424, (FF // P) * SLOTS).rearrange("p (k s) -> p k s", s=SLOTS)
        SGE = [view(11008 + 512 * i, 512) for i in range(2)]
        HE = [view(12032 + 512 * i, 512) for i in range(2)]
        YE = view(13056, D)
        LOGX = view(14080, T * 16).rearrange("p (t e) -> p t e", t=T)
        LW = view(14112, T * 16).rearrange("p (t e) -> p t e", t=T)
        RPL, TOP = view(14144, 16).rearrange("p (t e) -> p t e", t=T), view(14160, 16).rearrange("p (t e) -> p t e", t=T)
        MASK, EXPL, COMB, SLOT = [view(14176 + 16 * i, 16).rearrange("p (t e) -> p t e", t=T) for i in range(4)]
        ESUM, CNT = view(14240, 2), view(14242, 1)
        MTMP = view(14248, 16).rearrange("p (t e) -> p t e", t=T)
        cnt_i = sb("busiest_expert", 1, I32)
        IOTA = iota_t[:, :]

        def gate_tile(pe, r, e, j0, bank):
            for h in range(2):
                w = expert_half(pe, r, e, j0 + h, (4, 512))
                for k in range(4):
                    last = nc.tensor.matmul(PS[:, bank, :], XG[:, 4 * h + k, :], w[:, k, :],
                                            start=h + k == 0, stop=h == 1 and k == 3)
                last.then_inc(sem(("weights_used", "o_used")[r]), 1)

        def expert_half(eng, r, e, j, shape):
            n = MOE0 + j
            if r == 0:
                eng.wait_ge(sem(f"landed{n % RING}"), e * (16 * PER_EXPERT // RING) + LANDED[n])
            else:
                eng.wait_ge(sem(f"o_landed{n % RING}"), e * (16 * PER_EXPERT // RING) + 16 * (j // RING + 1))
            return half_view(n, shape)

        def expert_used(eng, r, e, j):
            if r == 0:
                eng.wait_ge(sem("weights_used"), e * PER_EXPERT + MOE0 + j)
            else:
                eng.wait_ge(sem("o_used"), e * PER_EXPERT + j)

        PASS = dict(placed=1, placedT=1, PWT=1, PWE=NE + 1, YE=NE + 1, gather=NE, XG=NE, scatter=NE + 1, added=NE + 1,
                    sg=7 * NE, h=7 * NE, T=7 * NE, HT=7 * NE)

        def ms(name):
            return sem("moe_" + name)

        def route_pe(pe):
            for t in range(T):
                for k in range(KD):
                    last = nc.tensor.matmul(PS[:, 4, t * NE:(t + 1) * NE], ht_lhs(k, t), ROUTER[:, k, :],
                                            start=k == 0, stop=k == KD - 1)
            last.then_inc(sem("moe_logits"), 1)
            pe.wait_ge(sem("moe_mask"), 1)
            nc.tensor.matmul(PS[:, 5, 0:NE], SUPPER, MASK[:, 0, :], start=True, stop=True)
            nc.tensor.matmul(PS[:, 5, NE:2 * NE], ONES, MASK[:, 0, :], start=True, stop=False)
            nc.tensor.matmul(PS[:, 5, NE:2 * NE], SUPPER, MASK[:, 1, :], start=False, stop=True)
            nc.tensor.matmul(PS[:, 5, 2 * NE:3 * NE], ONES, MASK[:, 0, :], start=True, stop=False)
            nc.tensor.matmul(PS[:, 5, 2 * NE:3 * NE], ONES, MASK[:, 1, :], start=False, stop=True)\
                .then_inc(sem("moe_places"), 1)

        def route_dve(s):
            s.do(nc.vector.memset(view(14080, 192), NONCAUSAL))
            s.eng.wait_ge(sem("moe_logits"), 1)
            s.do(nc.vector.tensor_copy(LOGX[:, :, 0:NE], PS[:, 4, 0:2 * NE].rearrange("p (t e) -> p t e", t=T)))
            for t in range(T):
                s.do(nc.vector.max(TOP[:, t, :], LOGX[:, t, 0:NE]))
            s.do(nc.vector.tensor_copy(RPL[:, :, 0:2], TOP[:, :, 0:2]))
            for t in range(T):
                s.do(nc.vector.match_replace(out=LW[:, t, 0:14], in_to_replace=RPL[:, t, :],
                                             in_values=LOGX[:, t, 0:14], imm_value=TAKEN))
            s.after(nc.vector.tensor_scalar(MASK, LW[:, :, 0:NE], TAKEN, None, ALU.is_equal).then_inc(sem("moe_mask"), 1), "moe_mask")
            s.after(nc.vector.tensor_tensor(EXPL, LOGX[:, :, 0:NE], bc(TOP[:, :, 0:1], [P, T, NE]), ALU.subtract).then_inc(sem("moe_shifted"), 1), "moe_shifted")
            s.eng.wait_ge(sem("moe_exp"), 1)
            s.do(nc.vector.tensor_tensor(EXPL, EXPL, MASK, ALU.mult))
            s.do(nc.vector.tensor_reduce(ESUM, EXPL, AX.X, ALU.add))
            s.do(nc.vector.reciprocal(ESUM, ESUM))
            s.do(nc.vector.tensor_tensor(COMB, EXPL, bc(ESUM.unsqueeze(2), [P, T, NE]), ALU.mult))
            s.eng.wait_ge(sem("moe_places"), 1)
            s.do(nc.vector.scalar_tensor_tensor(SLOT, PS[:, 5, 0:2 * NE].rearrange("p (t e) -> p t e", t=T), 1.0, MASK,
                                                ALU.add, ALU.mult))
            s.do(nc.vector.tensor_scalar(SLOT, SLOT, -1.0, None, ALU.add))
            s.do(nc.vector.tensor_reduce(CNT, PS[:, 5, 2 * NE:3 * NE], AX.X, ALU.max))
            s.after(nc.vector.tensor_copy(cnt_i[:, :], CNT).then_inc(sem("moe_count"), 1), "moe_count")

        def pass_dve(s, r):
            if r:
                s.do(nc.vector.tensor_scalar(SLOT, SLOT, -float(SLOTS), None, ALU.add))
            for t in range(T):
                s.do(nc.vector.tensor_tensor(PALL[:, t], bc(IOTA.unsqueeze(1), [P, NE, SLOTS]),
                                             bc(SLOT[:, t].unsqueeze(2), [P, NE, SLOTS]), ALU.is_equal))
                ins = nc.vector.tensor_tensor(WSEL[:, t], PALL[:, t], bc(COMB[:, t].unsqueeze(2), [P, NE, SLOTS]),
                                              ALU.mult)
                if t == 0:
                    s.do(ins)
            ins.then_inc(ms("placed"), 1)
            nc.vector.memset(PWE, 0.0).then_inc(ms("PWE"), 1)
            nc.vector.memset(YE, 0.0).then_inc(ms("YE"), 1)
            s.eng.wait_ge(ms("YE"), 1 + r * PASS["YE"])

        def pass_pe(pe, r):
            pe.wait_ge(ms("placed"), 1 + r * PASS["placed"])
            for e in range(NE):
                for t in range(T):
                    c = ((e % 2) * T + t) * SLOTS
                    last = nc.tensor.transpose(PS[:, 4 + e // 2, c:c + SLOTS], WSEL[:, t, e, :], IDENT)
            last.then_inc(ms("placedT"), 1)
            pe.wait_ge(ms("PWT"), 1 + r * PASS["PWT"])

            def scatter(e):
                pe.wait_ge(ms("PWE"), e + 1 + r * PASS["PWE"])
                for t, b in ((0, 6), (1, 2)):
                    for dh in range(2):
                        last = nc.tensor.matmul(PS[:, b + dh, :], PWE[:, t * P:(t + 1) * P],
                                                YE[:, 512 * dh:512 * dh + 512], start=True, stop=True)
                last.then_inc(ms("scatter"), 1)

            with pe.Fori(0, NE) as e:
                pe.wait_ge(ms("YE"), e + 1 + r * PASS["YE"])
                for k in range(KD):
                    for t in range(T):
                        last = nc.tensor.matmul(PS[:, 4 + k // 4, (k % 4) * SLOTS:(k % 4 + 1) * SLOTS],
                                                XN[:, t, k * P:(k + 1) * P],
                                                PALL[:, t, bass.ds(e, 1), :].rearrange("p a s -> p (a s)"),
                                                start=t == 0, stop=t == 1)
                last.then_inc(ms("gather"), 1)
                scatter(e)

                def turn(f):
                    pe.wait_ge(ms("h"), e * 7 + (f + 1) + r * PASS["h"])
                    if f >= 2:
                        pe.wait_ge(ms("HT"), e * 7 + (f - 1) + r * PASS["HT"])
                    for j in range(4):
                        last = nc.tensor.transpose(PS[:, 6 + f % 2, j * SLOTS:(j + 1) * SLOTS],
                                                   HE[f % 2][:, j * P:(j + 1) * P], IDENT)
                    last.then_inc(ms("T"), 1)

                for f in range(7):
                    if f == 0:
                        pe.wait_ge(ms("XG"), e + 1 + r * PASS["XG"])
                    if f >= 2:
                        pe.wait_ge(ms("sg"), e * 7 + (f - 1) + r * PASS["sg"])
                    gate_tile(pe, r, e, 4 * f, f % 2)
                    if f == 0:
                        pe.wait_ge(ms("added"), e + 1 + r * PASS["added"])
                    if f >= 2:
                        pe.wait_ge(ms("h"), e * 7 + (f - 1) + r * PASS["h"])
                    gate_tile(pe, r, e, 4 * f + 2, 2 + f % 2)
                    if f:
                        turn(f - 1)
                turn(6)
                pe.wait_ge(ms("HT"), e * 7 + 7 + r * PASS["HT"])
                for i in range(14):
                    w = expert_half(pe, r, e, 28 + i, (2, D))
                    for k in range(2):
                        for dh in range(2):
                            last = nc.tensor.matmul(PS[:, 4 + dh, :], HET[:, 2 * i + k, :],
                                                    w[:, k, 512 * dh:512 * dh + 512], start=i + k == 0,
                                                    stop=i == 13 and k == 1)
                    last.then_inc(sem(("weights_used", "o_used")[r]), 1)
            pe.wait_ge(ms("YE"), NE + 1 + r * PASS["YE"])
            scatter(NE)

        def pass_act(act, r):
            act.wait_ge(ms("placedT"), 1 + r * PASS["placedT"])
            nc.scalar.activation(PWT, banks(4, 4).rearrange("p (e s) -> p e s", e=NE), ACT.Copy)\
                .then_inc(ms("PWT"), 1)
            act.wait_ge(ms("PWT"), 1 + r * PASS["PWT"])
            with act.Fori(0, NE) as e:
                act.wait_ge(ms("XG"), e + 1 + r * PASS["XG"])
                act.wait_ge(ms("scatter"), e + 1 + r * PASS["scatter"])
                nc.scalar.activation(PWE, PWT[:, bass.ds(e, 1), :].rearrange("p a s -> p (a s)"), ACT.Copy)\
                    .then_inc(ms("PWE"), 1)

                def back(f):
                    act.wait_ge(ms("T"), e * 7 + (f + 1) + r * PASS["T"])
                    nc.scalar.activation(HET[:, 4 * f:4 * f + 4, :],
                                         PS[:, 6 + f % 2, :].rearrange("p (k s) -> p k s", k=4), ACT.Copy)\
                        .then_inc(ms("HT"), 1)

                for f in range(7):
                    expert_used(act, r, e, 4 * f + 2)
                    if f >= 2:
                        act.wait_ge(ms("h"), e * 7 + (f - 1) + r * PASS["h"])
                    nc.scalar.activation(SGE[f % 2], PS[:, f % 2, :], ACT.Silu).then_inc(ms("sg"), 1)
                    if f >= 1:
                        back(f - 1)
                back(6)
                expert_used(act, r, e, PER_EXPERT)
                nc.scalar.activation(YE, banks(4, 2), ACT.Copy).then_inc(ms("YE"), 1)

        def pass_loop_dve(s, r):
            dve = s.eng

            def add(e):
                dve.wait_ge(ms("scatter"), e + 1 + r * PASS["scatter"])
                nc.vector.tensor_tensor(X[:, 0, :], X[:, 0, :], banks(6, 2), ALU.add)
                return nc.vector.tensor_tensor(X[:, 1, :], X[:, 1, :], banks(2, 2), ALU.add)

            with dve.Fori(0, NE) as e:
                dve.wait_ge(ms("gather"), e + 1 + r * PASS["gather"])
                nc.vector.tensor_tensor(XG, banks(4, 2).rearrange("p (k s) -> p k s", k=KD),
                                        bc(GAINC[:, 40:48].unsqueeze(2), [P, KD, SLOTS]), ALU.mult)\
                    .then_inc(ms("XG"), 1)
                add(e).then_inc(ms("added"), 1)
                dve.wait_ge(ms("added"), e + 1 + r * PASS["added"])
                for f in range(7):
                    expert_used(dve, r, e, 4 * f + 4)
                    dve.wait_ge(ms("sg"), e * 7 + (f + 1) + r * PASS["sg"])
                    if f >= 2:
                        dve.wait_ge(ms("T"), e * 7 + (f - 1) + r * PASS["T"])
                    nc.vector.tensor_tensor(HE[f % 2], SGE[f % 2], PS[:, 2 + f % 2, :], ALU.mult)\
                        .then_inc(ms("h"), 1)
            add(NE).then_inc(ms("added"), 1)
            dve.wait_ge(ms("added"), NE + 1 + r * PASS["added"])

        def pass_loads(sp, r):
            def src(name, k0, nk, c0, n):
                return A[name].rearrange("x e (k p) n -> p (x e k) n", p=P), k0, nk, c0, n

            with sp.Fori(0, NE) as e:
                for j in range(PER_EXPERT):
                    if j < 28:
                        f, q = divmod(j, 4)
                        v = A[("moe_w_gate_2", "moe_w_up_2")[q // 2]].rearrange("x e (k p) n -> p (x e k) n", p=P)
                        source = v[:, bass.ds(e * KD + 4 * (q % 2), 4), 512 * f:512 * f + 512]
                        dst = half_view(MOE0 + j, (4, 512))
                    else:
                        v = A["moe_w_down_2"].rearrange("x e (k p) n -> p (x e k) n", p=P)
                        source = v[:, bass.ds(e * (FF // P) + 2 * (j - 28), 2), :]
                        dst = half_view(MOE0 + j, (2, D))
                    if r == 0:
                        sp.wait_ge(sem("weights_used"), e * PER_EXPERT + (MOE0 + j - RING + 1))
                        sp.dma_start(dst, source).then_inc(sem(f"landed{(MOE0 + j) % RING}"), 16)
                    else:
                        if j < RING:
                            sp.wait_ge(ms("scatter"), e + 1 + 1 * PASS["scatter"])
                        else:
                            sp.wait_ge(sem("o_used"), e * PER_EXPERT + (j - RING + 1))
                        sp.dma_start(dst, source).then_inc(sem(f"o_landed{(MOE0 + j) % RING}"), 16)
            if r:
                sp.wait_ge(ms("scatter"), NE + 1 + r * PASS["scatter"])

        def overflow(eng, body):
            eng.wait_ge(sem("moe_count"), 1)
            count = eng.value_load(cnt_i[0:1, 0:1], min_val=0, max_val=S)
            with eng.If(count > OVER):
                body()

        PSTAGE = view(0, 3 * P).rearrange("p (a c) -> p a c", a=3)
        LBT = [view(512 + 16 * i, 4) for i in range(4)]

        def rows_of(a):
            return a.rearrange("a b -> (a b)") if len(a.shape) == 2 else a.rearrange("a b c -> (a b c)")

        PARAMS = [(R_GDN, A["gdn_norm_gain"]), (R_KI, A["idx_k_gain"]), (R_DT, A["dt_bias"]), (R_EA, A["a_log"]),
                  (R_NSA, A["nsa_qk_gain_2"]), (R_DQK, A["diff_qk_gain_2"]), (R_LAM, A["diff_lambda_2"]),
                  (R_DN, A["diff_norm_2"]), (R_GLAN, A["gla_norm_2"]), (R_HGN, A["hgrn_norm_2"])]

        def load_cols(eng):
            for i, name in enumerate(("norm_gain", "norm_attn_2", "norm_ffn_2", "ple_norm_2")):
                eng.dma_start(PSTAGE[16 * i:16 * i + 16, 0, :], A[name].rearrange("l (k p) -> (l k) p", p=P))\
                    .then_inc(sem("col_params"), 16)
            for L in range(DEPTH):
                eng.dma_start(PSTAGE[0:96, 1 + L, :], A["conv_w"][L].rearrange("k (c p) -> (k c) p", p=P))\
                    .then_inc(sem("col_params"), 16)

        OTHERS = [(pos_t[:, :], A["positions"].rearrange("b (t p) -> p (b t)", p=P))]
        OTHERS += [(dst, rows_of(src).partition_broadcast(P)) for dst, src in PARAMS]
        for L in range(DEPTH):
            OTHERS.append((WG2[0:16, L * P:(L + 1) * P], A["gla_w_gate2_2"][L]))
            OTHERS.append((GLAB[:, L:L + 1], A["gla_b_gate_2"][L:L + 1, :].rearrange("a p -> p a")))
            for j in range(2):
                OTHERS.append((CMPPOS[64 * j:64 * j + 64, L * CMP_L:(L + 1) * CMP_L],
                               A["nsa_cmp_pos_2"][L, j].rearrange("l d -> d l")))
                OTHERS.append((W2[:, L, j], A["nsa_cmp_w2_2"][L, j].rearrange("(k p) n -> p k n", p=P)))
            OTHERS.append((LBC[:, L:L + 5:4], A["hgrn_lb_logits_2"][L].rearrange("(i p) -> p i", p=P)))
        OTHERS.append((ROUTER, kview(A["moe_router_2"][0])))

        def load_params(eng, a, b):
            for dst, src in OTHERS[a:b]:
                eng.dma_start(dst, src, allow_slow_non_contiguous=True).then_inc(sem("params"), 16)

        N_COLS, N_PARAMS = 4 + DEPTH, len(OTHERS)
        assert N_PARAMS <= 32

        def setup_pool(s):
            g = nc.gpsimd

            def triangle(dst, fill_where_not, base, step, cm, op=ALU.is_ge):
                s.do(g.affine_select(out=dst, in_=dst, compare_op=op, fill=fill_where_not, base=base,
                                     pattern=step, channel_multiplier=cm))

            s.do(g.memset(IDENT, 0.0))
            s.after(g.affine_select(out=IDENT, in_=IDENT, compare_op=ALU.not_equal, fill=1.0, base=0,
                                   pattern=[[-1, P]], channel_multiplier=1).then_inc(sem("ident_ready"), 1), "ident_ready")
            s.do(g.memset(ONES, 1.0))
            s.do(g.memset(EPS1, EPS))
            s.do(g.memset(EPSK, EPS * DK))
            for i in range(ROT // 2):
                s.do(g.memset(FREQ[:, i:i + 1], float(np.float32(500000.0) ** np.float32(-2 * i / ROT))))
            for i in range(IDX_ROT // 2):
                s.do(g.memset(FREQ[:, ROT // 2 + i:ROT // 2 + i + 1],
                              float(np.float32(500000.0) ** np.float32(-2 * i / IDX_ROT))))
            for dst, base, step, cm in ((UPPER, 0, 1, -1), (SUPPER, -1, 1, -1), (SLOWER, -1, -1, 1)):
                s.do(g.memset(dst, 1.0))
                triangle(dst, 0.0, base, [[step, P]], cm)
            for l in range(LEVELS):
                n = 1 << l
                nb = P // (2 * n)
                low = MS[:, l, :].rearrange("p (b two n) -> p b two n", two=2, n=n)
                up = MT[:, l, :].rearrange("p (b two n) -> p b two n", two=2, n=n)
                s.do(g.memset(low[:, :, 0, :], 1.0))
                s.do(g.memset(low[:, :, 1, :], 0.0))
                s.do(g.memset(up[:, :, 0, :], 0.0))
                s.do(g.memset(up[:, :, 1, :], 1.0))
                pat, neg = [[-2 * n, nb], [0, 2 * n]], [[2 * n, nb], [0, 2 * n]]
                for dst, lo, hi in ((MS[:, l, :], n, 2 * n - 1), (MT[:, l, :], 0, n - 1)):
                    triangle(dst, 0.0, -lo, pat, 1)
                    triangle(dst, 0.0, hi, neg, -1)
            s.do(g.tensor_copy(MT[:, LEVELS, :], IDENT))
            for t in range(T):
                s.do(g.memset(CB[:, t, :], 0.0))
                triangle(CB[:, t, :], NEG, t * P, [[-1, S]], 1)
                s.do(g.memset(COK[:, t, :], 1.0))
                triangle(COK[:, t, :], 0.0, t * P - CMP_L + 1, [[-CMP_S, 32]], 1)
                s.do(g.memset(CBIAS[:, t, :], 0.0))
                triangle(CBIAS[:, t, :], NEG, t * P - CMP_L + 1, [[-CMP_S, 32]], 1)
            s.after(g.iota(IOTA, pattern=[[1, P]], base=0, channel_multiplier=0,
                          allow_small_or_imprecise_dtypes=True).then_inc(sem("consts_ready"), 1), "consts_ready")

        def setup_pe(pe):
            pe.wait_ge(sem("ident_ready"), 1)
            pe.wait_ge(sem("col_params"), 16 * N_COLS)
            nc.tensor.transpose(PS[:, 0, 0:64], PSTAGE[0:64, 0, :], IDENT[0:64, 0:64])
            for L in range(DEPTH):
                last = nc.tensor.transpose(PS[:, 0, 64 + 96 * L:160 + 96 * L], PSTAGE[0:96, 1 + L, :],
                                           IDENT[0:96, 0:96])
            last.then_inc(sem("param_cols_T"), 1)

        def setup_cols(s):
            s.eng.wait_ge(sem("param_cols_T"), 1)
            s.after(nc.vector.tensor_copy(cols_t[:, :], PS[:, 0, 0:256]).then_inc(sem("cols_ready"), 1), "cols_ready")

        def setup_dve(s):
            s.eng.wait_ge(sem("params"), 16 * N_PARAMS)
            s.eng.wait_ge(sem("consts_ready"), 1)
            for L in range(DEPTH):
                lam = R_LAM[:, L * P:(L + 1) * P].rearrange("p (a b d) -> p a b d", a=2, b=2)
                s.do(nc.vector.tensor_tensor(LAMP.rearrange("p (a d) -> p a d", a=2), lam[:, :, 0, :], lam[:, :, 1, :],
                                             ALU.mult))
                s.after(nc.vector.tensor_reduce(LAMS, LAMP.rearrange("p (a d) -> p a d", a=2), AX.X, ALU.add).then_inc(sem("lam_sum"), 1), "lam_sum")
                s.eng.wait_ge(sem("lam_exp"), L + 1)
                s.do(nc.vector.tensor_tensor(LAMC[:, L:L + 1], LAMS[:, 0:1], LAMS[:, 1:2], ALU.subtract))
                s.do(nc.vector.tensor_scalar(LAMC[:, L:L + 1], LAMC[:, L:L + 1], lam_init(L), None, ALU.add))
                row = slice(L * HD, (L + 1) * HD)
                s.do(nc.vector.tensor_scalar(G12[:, L, 0, :], R_DN[:, row], 1.0 - lam_init(L), None, ALU.mult))
                s.do(nc.vector.tensor_copy(G12[:, L, 1, :], R_GLAN[:, row]))
                s.do(nc.vector.tensor_copy(G12[:, L, 2, :], R_HGN[:, row]))
            lb = LBC.rearrange("p (i k) -> p i k", i=2)
            m, e0, e1, ss = [v[:, 0:2] for v in LBT]
            s.do(nc.vector.tensor_tensor(m, lb[:, :, 0], lb[:, :, 1], ALU.max))
            s.do(nc.vector.tensor_tensor(e0, lb[:, :, 0], m, ALU.subtract))
            s.after(nc.vector.tensor_tensor(e1, lb[:, :, 1], m, ALU.subtract).then_inc(sem("lb_shifted"), 1), "lb_shifted")
            s.eng.wait_ge(sem("lb_exp"), 1)
            s.do(nc.vector.tensor_tensor(ss, e0, e1, ALU.add))
            s.do(nc.vector.reciprocal(ss, ss))
            s.do(nc.vector.memset(lb[:, :, 0], 0.0))
            s.do(nc.vector.tensor_tensor(lb[:, :, 1], e1, ss, ALU.mult))
            s.do(nc.vector.tensor_scalar(lb[:, :, 2:4], lb[:, :, 0:2], -1.0, 1.0, ALU.mult, ALU.add))

        def setup_act(s):
            s.eng.wait_ge(sem("params"), 16 * N_PARAMS)
            s.do(nc.scalar.activation(R_EA, R_EA, ACT.Exp))
            for L in range(DEPTH):
                s.eng.wait_ge(sem("lam_sum"), L + 1)
                s.after(nc.scalar.activation(LAMS, LAMS, ACT.Exp).then_inc(sem("lam_exp"), 1), "lam_exp")
            s.eng.wait_ge(sem("lb_shifted"), 1)
            s.do(nc.scalar.activation(LBT[1][:, 0:2], LBT[1][:, 0:2], ACT.Exp))
            s.after(nc.scalar.activation(LBT[2][:, 0:2], LBT[2][:, 0:2], ACT.Exp).then_inc(sem("lb_exp"), 1), "lb_exp")

        RFINAL = view(0, D)
        block = ctx.enter_context(nc.Block())

        @block.sync
        def _(sp):
            sp.dma_start(X, A["x"].rearrange("b (t p) d -> p (b t) d", p=P)).then_inc(sem("x_loaded"), 16)
            load_cols(sp)
            for n, load in enumerate(LOADS):
                if load is None:
                    if n == MOE0:
                        pass_loads(sp, 0)
                    if n == MOE0 + NE * PER_EXPERT - 1:
                        overflow(sp, lambda: pass_loads(sp, 1))
                    continue
                shape, parts = load
                if n >= RING:
                    sp.wait_ge(sem("weights_used"), n - RING + 1)
                for j, src in parts:
                    dst = half_view(n, shape)
                    if j is not None:
                        dst = dst[64 * j:64 * j + 64]
                    sp.dma_start(dst, src).then_inc(sem(f"landed{n % RING}"), 16)
            sp.wait_ge(sem("out_ready"), 1)
            sp.dma_start(out.rearrange("b (t p) d -> p (b t) d", p=P), X).then_inc(sem("out_written"), 16)
            sp.wait_ge(sem("out_written"), 16)

        @block.gpsimd
        def _(pool):
            s = Steps(pool, "pool")
            setup_pool(s)
            for L in range(DEPTH):
                s.fence()
                gdn_pool(s, L)
                s.fence()
                dsa_pool(s, L)
                s.fence()
            s.fence()
            pool.dma_start(RFINAL, A["final_gain"].partition_broadcast(P)).then_inc(sem("final_gain"), 16)
            s.fence()
            for L in range(DEPTH):
                s.fence()
                gla_pool(s, L)
                s.fence()
                s.fence()
                pool.dma_start(PP, A["p_2"][L].rearrange("b (t p) c -> p (b t) c", p=P))\
                    .then_inc(sem("ple_loaded"), 16)
                s.fence()
            pool.wait_ge(sem("ple_loaded"), 16 * DEPTH)

        @block.scalar
        def _(act):
            s = Steps(act, "act")
            n = at_n = 0
            for L in range(DEPTH):
                norm_act(s, n)
                n += 1
                proj1_act(s, L)
                s.fence()
                weave(gdn_act(s, L), woven_act(s, ["p1"], L), GDN_STEPS, halves(["p1"], L))
                s.fence()
                weave(dsa_act(s, L, at_n), woven_act(s, ["zb", "gate"], L), DSA_STEPS, halves(["zb", "gate"], L))
                at_n += T
                s.fence()
                mix_act(s, L)
            s.fence()
            norm_act(s, n)
            n += 1
            s.fence()
            for L in range(DEPTH):
                norm_act(s, n)
                n += 1
                u_act(s, L)
                s.fence()
                prep_act(s, L)
                weave(gla_act(s, L), mixers_act(s, L, at_n), GLA_STEPS, MIXER_STEPS)
                at_n += 2 * T
                post_act(s, L)
                mix_act(s, DEPTH + L)
                norm_act(s, n)
                n += 1
                s.fence()
                if L % 2 == 0:
                    ffn_act(s, L)
                else:
                    s.eng.wait_ge(sem("moe_shifted"), 1)
                    s.after(nc.scalar.activation(EXPL, EXPL, ACT.Exp).then_inc(sem("moe_exp"), 1), "moe_exp")
                    pass_act(act, 0)
                    overflow(act, lambda: pass_act(act, 1))
                s.fence()
                norm_act(s, n)
                n += 1
                ple_act(s, L)
                s.fence()

        @block.vector
        def _(dve):
            s = Steps(dve, "dve")
            setup_cols(s)
            n = at_n = 0
            for L in range(DEPTH):
                norm_dve(s, n, GAINC[:, 8 * L:8 * L + 8])
                n += 1
                conv_dve(s, L)
                s.fence()
                weave(gdn_dve(s, L), woven_dve(s, ["p1"], L), GDN_STEPS, halves(["p1"], L))
                s.fence()
                weave(dsa_dve(s, L, at_n), woven_dve(s, ["zb", "gate"], L), DSA_STEPS, halves(["zb", "gate"], L))
                at_n += T
                s.fence()
                gate_dve(s)
                residual_dve(s, "out", L)
            s.fence()
            norm_dve(s, n, None)
            n += 1
            s.eng.wait_ge(sem("final_gain"), 16)
            s.after(nc.vector.tensor_tensor(X, XN, bc(RFINAL.unsqueeze(1), [P, T, D]), ALU.mult).then_inc(sem("x_updated"), 1), "x_updated")
            s.fence()
            for L in range(DEPTH):
                norm_dve(s, n, GAINC[:, 16 + 8 * L:24 + 8 * L])
                n += 1
                prep_dve(s, L)
                s.fence()
                weave(gla_dve(s, L), mixers_dve(s, L, at_n), GLA_STEPS, MIXER_STEPS)
                at_n += 2 * T
                post_dve(s, L)
                residual_dve(s, "out2", L)
                norm_dve(s, n, GAINC[:, 32 + 8 * L:40 + 8 * L])
                n += 1
                s.fence()
                if L % 2 == 0:
                    ffn_dve(s, L)
                else:
                    route_dve(s)
                    pass_dve(s, 0)
                    pass_loop_dve(s, 0)

                    def second():
                        pass_dve(s, 1)
                        pass_loop_dve(s, 1)

                    own = s.n
                    overflow(dve, second)
                    s.own, s.n = sem("dve_steps_after_experts"), 0
                    s.after(nc.vector.tensor_copy(SS[:, 0:1], SS[:, 0:1]).then_inc(sem("x_updated"), 1), "x_updated")
                s.fence()
                norm_dve(s, n, GAINC[:, 48 + 8 * L:56 + 8 * L])
                n += 1
                ple_dve(s, L)
                s.fence()
            s.after(nc.vector.tensor_copy(SS[:, 0:1], SS[:, 0:1]).then_inc(sem("out_ready"), 1), "out_ready")

        @block.tensor
        def _(pe):
            s = Steps(pe, "pe")
            setup_pe(pe)
            n = at_n = ht = 0
            for L in range(DEPTH):
                norm_pe(pe, n)
                n += 1
                proj1_pe(pe, L)
                s.fence()
                weave_tensor(gdn_pe(pe, L), gemm_steps(pe, group("p1", L), ht_lhs), GDN_STEPS, halves(["p1"], L))
                s.fence()
                weave_tensor(dsa_pe(pe, L, at_n), gemm_steps(pe, group("zb", L) + group("gate", L), ht_lhs), DSA_STEPS,
                             halves(["zb", "gate"], L))
                at_n += T
                s.fence()
                mix_pe(pe, "out", L, L)
            s.fence()
            n += 1
            s.fence()
            ht = DEPTH
            for L in range(DEPTH):
                pe.wait_ge(sem("xn_ready"), n + 1)
                norm_pe(pe, n)
                n += 1
                ht += 1
                pe.wait_ge(sem("ht_ready"), 2 * ht - 1)
                u_pe(pe, L, 2 * ht)
                s.fence()
                prep_pe(pe, L)
                weave(gla_pe(pe, L), mixers_pe(pe, L, at_n), GLA_STEPS, MIXER_STEPS)
                at_n += 2 * T
                mix_pe(pe, "out2", L, DEPTH + L)
                norm_pe(pe, n)
                n += 1
                ht += 1
                pe.wait_ge(sem("ht_ready"), 2 * ht)
                s.fence()
                if L % 2 == 0:
                    ffn_pe(pe, L)
                else:
                    route_pe(pe)
                    pass_pe(pe, 0)
                    overflow(pe, lambda: pass_pe(pe, 1))
                s.fence()
                norm_pe(pe, n)
                n += 1
                ht += 1
                pe.wait_ge(sem("ht_ready"), 2 * ht - 1)
                ple_pe(pe, L, 2 * ht)
                s.fence()


_INS = {"x": "x", "positions": "positions", "norm_gain": "norm_gain", "w_in": "w_in", "conv_w": "conv_w",
        "a_log": "a_log", "dt_bias": "dt_bias", "gdn_norm_gain": "gdn_norm_gain", "idx_k_gain": "idx_k_gain",
        "w_out": "w_out", "final_gain": "final_gain"}
_INS_2 = ["p_2", "norm_attn_2", "w_in_2", "w_out_2", "nsa_cmp_pos_2", "nsa_cmp_w1_2", "nsa_cmp_w2_2", "nsa_qk_gain_2",
          "diff_qk_gain_2", "diff_lambda_2", "diff_norm_2", "gla_w_gate2_2", "gla_b_gate_2", "gla_norm_2",
          "hgrn_lb_logits_2", "hgrn_norm_2", "norm_ffn_2", "ffn_w_gate_2", "ffn_w_up_2", "ffn_w_down_2",
          "moe_router_2", "moe_w_gate_2", "moe_w_up_2", "moe_w_down_2", "ple_norm_2", "ple_w_gate_2", "ple_w_proj_2"]
OVER = 128


def kernel(**inputs):
    import concourse.bacc as _bacc
    from concourse.bass_utils import run_bass_kernel_spmd as _run

    nc = _bacc.Bacc("TRN2", target_bir_lowering=False, num_devices=1)
    arrays, args = {}, {}
    for name in list(_INS) + _INS_2:
        a = np.ascontiguousarray(inputs[name])
        arrays[f"in_{name}_dram"] = a
        args[name] = nc.dram_tensor(f"in_{name}_dram", a.shape, mybir.dt.from_np(a.dtype), kind="ExternalInput").ap()
    out = nc.dram_tensor("out_0_dram", (1, S, D), F32, kind="ExternalOutput").ap()
    blocks_kernel(nc, args, out)
    r = _run(nc, [arrays], core_ids=[0])
    return r.results[0]["out_0_dram"]
```
